# Optimizing a Trainium2 kernel written in Bass

```python
import math
import jax
import jax.numpy as jnp
from jax import lax
import numpy as np

D_MODEL = 1024
BATCH = 1
SEQ = 512
DEPTH = 1

MIX_WIDTH = D_MODEL
N_MIXERS = 4
GROUP_WIDTH = MIX_WIDTH // N_MIXERS
HEADS_PER_GROUP = 4
HEAD_DIM = GROUP_WIDTH // HEADS_PER_GROUP
CONV_WIDTH = 31
MOBA_BLOCK = 256
MOBA_TOPK = 3
Q_CHUNK = 128
N_BUCKETS = 32
T5_MAX_DISTANCE = 128
POOL_WINDOWS = (2, 4, 8, 16)
N_POOL_GROUPS = len(POOL_WINDOWS)
POOL_GROUP_WIDTH = GROUP_WIDTH // N_POOL_GROUPS
SGU_CHUNK = 128
N_EXPERTS = 32
TOP_K = 4
D_FF = D_MODEL
SWIGLU_LIMIT = 7.0
SWIGLU_ALPHA = 1.702
EXPERT_BLOCK = 128
EPS = 1e-6

CONV_IN = 2 * GROUP_WIDTH
ATTN_IN = 3 * GROUP_WIDTH
POOL_IN = GROUP_WIDTH
SGU_IN = 2 * GROUP_WIDTH
CONV_OFF = 0
ATTN_OFF = CONV_OFF + CONV_IN
POOL_OFF = ATTN_OFF + ATTN_IN
SGU_OFF = POOL_OFF + POOL_IN
IN_WIDTH = SGU_OFF + SGU_IN

kernel_name = "hybrid_conv_moba_pool_sgu_moe"

def _rmsnorm(x, g):
    xf = x.astype(jnp.float32)
    y = xf * lax.rsqrt(jnp.mean(xf * xf, axis=-1, keepdims=True) + EPS)
    return (y * g.astype(jnp.float32)).astype(x.dtype)

def _layernorm(x, g, b):
    xf = x.astype(jnp.float32)
    mu = jnp.mean(xf, axis=-1, keepdims=True)
    xc = xf - mu
    y = xc * lax.rsqrt(jnp.mean(xc * xc, axis=-1, keepdims=True) + EPS)
    return (y * g.astype(jnp.float32) + b.astype(jnp.float32)).astype(x.dtype)

def _modulate(h, shift, scale):
    return h * (1 + scale[:, None, :]) + shift[:, None, :]

def conformer_conv(z, conv_w, conv_b, norm_g, norm_b):
    a, gte = jnp.split(z, 2, axis=-1)
    y = a * jax.nn.sigmoid(gte)
    y = lax.conv_general_dilated(
        y, conv_w[:, None, :], window_strides=(1,), padding=[(CONV_WIDTH - 1, 0)],
        dimension_numbers=('NWC', 'WIO', 'NWC'), feature_group_count=GROUP_WIDTH) + conv_b
    B, S, C = y.shape
    y = _layernorm(y.reshape(B, S, HEADS_PER_GROUP, HEAD_DIM),
                   norm_g.reshape(HEADS_PER_GROUP, HEAD_DIM),
                   norm_b.reshape(HEADS_PER_GROUP, HEAD_DIM)).reshape(B, S, C)
    return jax.nn.silu(y)

def _t5_bucket(dist):
    n = jnp.maximum(dist, 0)
    max_exact = N_BUCKETS // 2
    nf = jnp.maximum(n, 1).astype(jnp.float32)
    large = max_exact + (jnp.log(nf / max_exact) / math.log(T5_MAX_DISTANCE / max_exact)
                         * (N_BUCKETS - max_exact)).astype(jnp.int32)
    large = jnp.minimum(large, N_BUCKETS - 1)
    return jnp.where(n < max_exact, n, large)

def moba_attention(q, k, v, rel_bias):
    B, S, H, Dh = q.shape
    q = q.transpose(0, 2, 1, 3)
    k = k.transpose(0, 2, 1, 3)
    v = v.transpose(0, 2, 1, 3)
    n_blocks = -(-S // MOBA_BLOCK)
    s_pad = n_blocks * MOBA_BLOCK
    pad = ((0, 0), (0, 0), (0, s_pad - S), (0, 0))
    k = jnp.pad(k, pad)
    v = jnp.pad(v, pad)
    kb = k.reshape(B, H, n_blocks, MOBA_BLOCK, Dh)
    vb = v.reshape(B, H, n_blocks, MOBA_BLOCK, Dh)
    k_mean = jnp.mean(kb.astype(jnp.float32), axis=3).astype(q.dtype)
    k_sel = min(MOBA_TOPK, n_blocks)
    scale = HEAD_DIM ** -0.5
    bias_table = rel_bias.T.astype(jnp.float32)
    head_idx = jnp.arange(H)
    offs = jnp.arange(MOBA_BLOCK)
    gather_blocks = jax.vmap(jax.vmap(lambda blocks, idx: blocks[idx]))

    def chunk(ci):
        q0 = ci * Q_CHUNK
        qc = lax.dynamic_slice_in_dim(q, q0, Q_CHUNK, axis=2)
        qpos = q0 + jnp.arange(Q_CHUNK)
        own = q0 // MOBA_BLOCK
        gate = jnp.einsum('bhqd,bhnd->bhqn', qc, k_mean).astype(jnp.float32)
        gate = jnp.where(jnp.arange(n_blocks) < own, gate, -jnp.inf)
        _, idx = lax.top_k(gate, k_sel)
        valid = idx < own
        kg = gather_blocks(kb, idx)
        vg = gather_blocks(vb, idx)
        dist_sel = qpos[:, None, None] - (idx[..., None] * MOBA_BLOCK + offs)
        bias_sel = bias_table[head_idx[:, None, None, None], _t5_bucket(dist_sel)]
        s_sel = jnp.einsum('bhqd,bhqnkd->bhqnk', qc, kg).astype(jnp.float32) * scale + bias_sel
        s_sel = jnp.where(valid[..., None], s_sel, -jnp.inf).reshape(B, H, Q_CHUNK, k_sel * MOBA_BLOCK)
        own_start = own * MOBA_BLOCK
        ko = lax.dynamic_slice_in_dim(k, own_start, MOBA_BLOCK, axis=2)
        vo = lax.dynamic_slice_in_dim(v, own_start, MOBA_BLOCK, axis=2)
        dist_own = qpos[:, None] - (own_start + offs)[None, :]
        bias_own = bias_table[:, _t5_bucket(dist_own)]
        s_own = jnp.einsum('bhqd,bhkd->bhqk', qc, ko).astype(jnp.float32) * scale + bias_own
        s_own = jnp.where(dist_own >= 0, s_own, -jnp.inf)
        p = jax.nn.softmax(jnp.concatenate([s_sel, s_own], axis=-1), axis=-1).astype(v.dtype)
        p_sel = p[..., :k_sel * MOBA_BLOCK].reshape(B, H, Q_CHUNK, k_sel, MOBA_BLOCK)
        p_own = p[..., k_sel * MOBA_BLOCK:]
        return (jnp.einsum('bhqnk,bhqnkd->bhqd', p_sel, vg)
                + jnp.einsum('bhqk,bhkd->bhqd', p_own, vo))

    out = lax.map(chunk, jnp.arange(S // Q_CHUNK))
    return out.transpose(1, 0, 3, 2, 4).reshape(B, S, H * Dh)

def multiscale_pool(z, pool_w, pool_scale):
    B, S, C = z.shape
    zg = z.reshape(B, S, N_POOL_GROUPS, POOL_GROUP_WIDTH).astype(jnp.float32)
    csum = jnp.cumsum(zg, axis=1)
    t = jnp.arange(1, S + 1, dtype=jnp.float32)
    pooled = []
    for gi, w in enumerate(POOL_WINDOWS):
        cs = csum[:, :, gi]
        lag = jnp.pad(cs, ((0, 0), (w, 0), (0, 0)))[:, :S]
        pooled.append((cs - lag) / jnp.minimum(t, w)[None, :, None])
    pooled = jnp.stack(pooled, axis=2) - zg
    y = jnp.einsum('bsgc,gcd->bsgd', pooled.astype(z.dtype), pool_w)
    return y.reshape(B, S, C) * pool_scale

def spatial_gating(z, norm_g, norm_b, sgu_w, sgu_b):
    z = jax.nn.gelu(z, approximate=False)
    u, v = jnp.split(z, 2, axis=-1)
    v = _layernorm(v, norm_g, norm_b)
    B, S, C = v.shape
    vc = v.reshape(B, S // SGU_CHUNK, SGU_CHUNK, HEADS_PER_GROUP, HEAD_DIM)
    w = jnp.tril(sgu_w)
    mixed = jnp.einsum('hij,bnjhc->bnihc', w, vc) + sgu_b.T[None, None, :, :, None]
    return u * mixed.reshape(B, S, C)

def _clamped_swiglu(xb, w1, b1, w2, b2):
    hh = xb @ w1 + b1
    x_glu, x_lin = jnp.split(hh, 2, axis=-1)
    x_glu = jnp.minimum(x_glu, SWIGLU_LIMIT)
    x_lin = jnp.clip(x_lin, -SWIGLU_LIMIT, SWIGLU_LIMIT)
    act = x_glu * jax.nn.sigmoid(SWIGLU_ALPHA * x_glu) * (x_lin + 1)
    return act @ w2 + b2

def moe_ffn(h, router_w, router_b, w1, b1, w2, b2):
    B, S, D = h.shape
    N = B * S
    hf = h.reshape(N, D)
    logits = (hf @ router_w + router_b).astype(jnp.float32)
    top_vals, top_idx = lax.top_k(logits, TOP_K)
    gates = jax.nn.softmax(top_vals, axis=-1)
    A = N * TOP_K
    e_flat = top_idx.reshape(A)
    tok_flat = jnp.arange(A) // TOP_K
    order = jnp.argsort(e_flat)
    e_sorted = e_flat[order]
    tok_sorted = tok_flat[order]
    g_sorted = gates.reshape(A)[order]
    sizes = jnp.bincount(e_flat, length=N_EXPERTS)
    padded = ((sizes + EXPERT_BLOCK - 1) // EXPERT_BLOCK) * EXPERT_BLOCK
    pad_end = jnp.cumsum(padded)
    pad_start = pad_end - padded
    grp_start = jnp.cumsum(sizes) - sizes
    dest = pad_start[e_sorted] + jnp.arange(A) - grp_start[e_sorted]
    P = A + N_EXPERTS * EXPERT_BLOCK
    n_blk = P // EXPERT_BLOCK
    row_token = jnp.full((P,), N, dtype=jnp.int32).at[dest].set(tok_sorted.astype(jnp.int32))
    block_expert = jnp.minimum(
        jnp.searchsorted(pad_end, jnp.arange(n_blk) * EXPERT_BLOCK, side='right'), N_EXPERTS - 1)
    x_pad = jnp.concatenate([hf, jnp.zeros((1, D), hf.dtype)], axis=0)
    xs = x_pad[row_token].reshape(n_blk, EXPERT_BLOCK, D)

    def expert_block(args):
        xb, e = args
        return _clamped_swiglu(xb, w1[e], b1[e], w2[e], b2[e])

    ys = lax.map(expert_block, (xs, block_expert)).reshape(P, D)
    y_assign = ys[dest] * g_sorted[:, None].astype(ys.dtype)
    out = jax.ops.segment_sum(y_assign, tok_sorted, num_segments=N)
    return out.reshape(B, S, D).astype(h.dtype)

def setup_inputs(seed: int = 0) -> dict:
    key = jax.random.key(seed)
    ks = jax.random.split(key, 28)
    f32 = jnp.float32

    def nrm(k, shape, scale):
        return jax.random.normal(k, shape, f32) * scale

    L, D, GW, H = DEPTH, D_MODEL, GROUP_WIDTH, HEADS_PER_GROUP
    return {
        'x': nrm(ks[0], (BATCH, SEQ, D), 1.0),
        'c': nrm(ks[1], (BATCH, D), 1.0),
        'w_mod': nrm(ks[2], (L, D, 6 * D), 0.5 * D ** -0.5),
        'b_mod': nrm(ks[3], (L, 6 * D), 0.02),
        'norm1_g': 1.0 + nrm(ks[4], (L, D), 0.05),
        'w_in': nrm(ks[5], (L, D, IN_WIDTH), D ** -0.5),
        'conv_w': nrm(ks[6], (L, CONV_WIDTH, GW), CONV_WIDTH ** -0.5),
        'conv_b': nrm(ks[7], (L, GW), 0.02),
        'conv_norm_g': 1.0 + nrm(ks[8], (L, GW), 0.05),
        'conv_norm_b': nrm(ks[9], (L, GW), 0.02),
        'rel_bias': nrm(ks[10], (N_BUCKETS, H), 0.3),
        'pool_w': nrm(ks[11], (L, N_POOL_GROUPS, POOL_GROUP_WIDTH, POOL_GROUP_WIDTH), POOL_GROUP_WIDTH ** -0.5),
        'pool_scale': 1.0 + nrm(ks[12], (L, GW), 0.05),
        'sgu_norm_g': 1.0 + nrm(ks[13], (L, GW), 0.05),
        'sgu_norm_b': nrm(ks[14], (L, GW), 0.02),
        'sgu_w': nrm(ks[15], (L, H, SGU_CHUNK, SGU_CHUNK), SGU_CHUNK ** -0.5),
        'sgu_b': 1.0 + nrm(ks[16], (L, H, SGU_CHUNK), 0.05),
        'mix_out_g': 1.0 + nrm(ks[17], (L, MIX_WIDTH), 0.05),
        'w_out': nrm(ks[18], (L, MIX_WIDTH, D), MIX_WIDTH ** -0.5),
        'norm2_g': 1.0 + nrm(ks[19], (L, D), 0.05),
        'router_w': nrm(ks[20], (L, D, N_EXPERTS), D ** -0.5),
        'router_b': nrm(ks[21], (L, N_EXPERTS), 0.01),
        'exp_w1': nrm(ks[22], (L, N_EXPERTS, D, 2 * D_FF), D ** -0.5),
        'exp_b1': nrm(ks[23], (L, N_EXPERTS, 2 * D_FF), 0.02),
        'exp_w2': nrm(ks[24], (L, N_EXPERTS, D_FF, D), D_FF ** -0.5),
        'exp_b2': nrm(ks[25], (L, N_EXPERTS, D), 0.02),
        'final_norm_g': 1.0 + nrm(ks[26], (D,), 0.05),
    }

def reference(x, c, w_mod, b_mod, norm1_g, w_in, conv_w, conv_b, conv_norm_g, conv_norm_b,
              rel_bias, pool_w, pool_scale, sgu_norm_g, sgu_norm_b, sgu_w, sgu_b, mix_out_g,
              w_out, norm2_g, router_w, router_b, exp_w1, exp_b1, exp_w2, exp_b2, final_norm_g):
    B, S, D = x.shape
    cond = jax.nn.silu(c)
    for l in range(DEPTH):
        mod = cond @ w_mod[l] + b_mod[l]
        shift1, scale1, gate1, shift2, scale2, gate2 = jnp.split(mod, 6, axis=-1)
        h = _modulate(_rmsnorm(x, norm1_g[l]), shift1, scale1)
        proj = h @ w_in[l]
        y_conv = conformer_conv(proj[..., CONV_OFF:CONV_OFF + CONV_IN],
                                conv_w[l], conv_b[l], conv_norm_g[l], conv_norm_b[l])
        qkv = proj[..., ATTN_OFF:ATTN_OFF + ATTN_IN].reshape(B, S, 3, HEADS_PER_GROUP, HEAD_DIM)
        y_attn = moba_attention(qkv[:, :, 0], qkv[:, :, 1], qkv[:, :, 2], rel_bias)
        y_pool = multiscale_pool(proj[..., POOL_OFF:POOL_OFF + POOL_IN], pool_w[l], pool_scale[l])
        y_sgu = spatial_gating(proj[..., SGU_OFF:SGU_OFF + SGU_IN],
                               sgu_norm_g[l], sgu_norm_b[l], sgu_w[l], sgu_b[l])
        mixed = jnp.concatenate([y_conv, y_attn, y_pool, y_sgu], axis=-1)
        mixed = _rmsnorm(mixed.reshape(B, S, N_MIXERS, GROUP_WIDTH),
                         mix_out_g[l].reshape(N_MIXERS, GROUP_WIDTH)).reshape(B, S, MIX_WIDTH)
        x = x + gate1[:, None, :] * (mixed @ w_out[l])
        h = _modulate(_rmsnorm(x, norm2_g[l]), shift2, scale2)
        x = x + gate2[:, None, :] * moe_ffn(h, router_w[l], router_b[l],
                                            exp_w1[l], exp_b1[l], exp_w2[l], exp_b2[l])
    return _rmsnorm(x, final_norm_g)


_drawn_inputs = setup_inputs


def setup_inputs(seed=0):
    import zlib

    import numpy as np

    out = dict(_drawn_inputs(seed))
    spreads = {}
    factors = {'norm1_g': 2.842,
     'conv_b': 5.931,
     'conv_norm_g': 12.008,
     'conv_norm_b': 27.186,
     'pool_scale': 15.239,
     'sgu_norm_g': 31.628,
     'sgu_norm_b': 64.0,
     'sgu_b': 23.323,
     'mix_out_g': 3.122,
     'router_b': 22.847,
     'exp_b1': 8.0,
     'exp_b2': 23.769,
     'norm2_g': 2.673}
    for name, (base, spread) in spreads.items():
        noise = np.random.default_rng([zlib.crc32(name.encode()), seed]).standard_normal(out[name].shape)
        drawn = base * np.exp(spread * noise) if base else spread * noise
        out[name] = jnp.asarray(drawn.astype(out[name].dtype))
    for name, factor in factors.items():
        out[name] = (out[name] * factor).astype(out[name].dtype)
    return out
```

```python
import math
from contextlib import ExitStack

import numpy as np
import concourse.bass as bass
from concourse import mybir

ALU = mybir.AluOpType
ACT = mybir.ActivationFunctionType
AX = mybir.AxisListType
F32 = mybir.dt.float32
BF16 = mybir.dt.bfloat16
U32 = mybir.dt.uint32

P = 128
D, S = 1024, 512
NT = S // P
KC = D // P
GW, NH, HD = 256, 4, 64
TAPS = 31
PADT = TAPS - 1
NE, TOPK, DFF = 32, 4, 1024
LIM, ALPHA, EPS = 7.0, 1.702, 1e-6
MAXBLK = NE + S * TOPK // P
EMPTY = 4096
NBUCK, MAXDIST = 32, 128
NDIST = S + P
NEG = -1.0e30

C_ID, C_TRI, C_STRICT, C_ONES, C_SLOT = 0, 128, 256, 384, 512
C_PM = 640
C_IOB = 641
C_IOE = C_IOB + MAXBLK
C_TOK = C_IOE + NE
C_ASG = C_TOK + NT
C_RW = C_ASG + NT * TOPK
C_RC = C_RW + 2
C_EPS = C_RC + 32
C_N = C_EPS + 1

R_C, R_N1, R_N2, R_MIX, R_BMOD, R_CB, R_N = 0, 8, 16, 24, 32, 80, 82


def constants():
    c = np.zeros((P, C_N), np.float32)
    p = np.arange(P)
    c[:, C_ID:C_ID + P] = np.eye(P)
    c[:, C_TRI:C_TRI + P] = p[:, None] <= p[None, :]
    c[:, C_STRICT:C_STRICT + P] = p[:, None] < p[None, :]
    c[:, C_ONES:C_ONES + P] = 1.0
    c[:, C_SLOT:C_SLOT + P] = p[None, :] + 1
    c[:, C_PM] = p % NE
    c[:, C_IOB:C_IOB + MAXBLK] = np.arange(MAXBLK)
    c[:, C_IOE:C_IOE + NE] = np.arange(NE)
    tok = p[:, None] + P * np.arange(NT)[None, :]
    c[:, C_TOK:C_TOK + NT] = tok
    c[:, C_ASG:C_ASG + NT * TOPK] = (tok[:, :, None] * TOPK + np.arange(TOPK)).reshape(P, -1)
    for ch in range(2):
        w = 2 ** (1 + 2 * ch + p // 64)
        c[:, C_RW + ch] = 1.0 / w
        c[:, C_RC + 16 * ch:C_RC + 16 * ch + 16] = 1.0 / np.minimum(np.arange(1, 17)[None, :], w[:, None])
    c[:, C_EPS] = EPS
    return c


def distance_buckets():
    dist = (S - 1) - np.arange(NDIST)
    n = np.maximum(dist, 0)
    exact = NBUCK // 2
    large = exact + (np.log(np.maximum(n, 1).astype(np.float32) / np.float32(exact)) / np.float32(math.log(MAXDIST / exact))
                     * (NBUCK - exact)).astype(np.int32)
    b = np.where(n < exact, n, np.minimum(large, NBUCK - 1))
    out = np.zeros((NBUCK + 1, NDIST), np.float32)
    out[:NBUCK] = (b[None, :] == np.arange(NBUCK)[:, None]) & (dist >= 0)[None, :]
    out[NBUCK:] = np.where(dist < 0, NEG, 0.0)
    return out


def build(nc, a, consts_d, buckets_d, out_d):
    with ExitStack() as ctx:
        def sb(name, shape, dt=F32):
            return ctx.enter_context(nc.sbuf_tensor(name, shape, dt))

        def sem(name):
            return ctx.enter_context(nc.semaphore(name))

        w1_slots = sb("w1_slots", [P, KC, 2 * DFF])
        w2_slots = sb("w2_slots", [P, 4, 2048])
        rows = sb("rows", [P, NT, D])
        colsT = sb("colsT", [P, KC, S])
        arena = sb("arena", [P, 16384])
        cst = sb("cst", [P, C_N])
        parms, taps_r, sgub_r = colsT[:, 0, 0:P], colsT[0:2 * TAPS, 1, 0:P], colsT[0:NH, 2, 0:P]
        buckets = colsT[0:NBUCK + 1, 3:5, :].rearrange("p a s -> p (a s)")[:, 0:NDIST]
        sguw_r = colsT[:, 5, :].rearrange("p (h j) -> p h j", h=NH)
        pc = sb("pc", [P, R_N + 2 * TAPS])
        taps = pc[:, R_N:R_N + 2 * TAPS]
        cond = sb("cond", [P, KC])
        mod = sb("mod", [P, 48])
        gs1 = sb("gs1", [P, KC])
        gs2 = sb("gs2", [P, KC])
        st = sb("st", [P, 160])
        lrows = sb("lrows", [P, 5, GW])
        sgub = sb("sgub", [P, NH])
        relb = sb("relb", [NBUCK + 1, NH])
        rw_sb = sb("rw_sb", [P, KC, NE])
        rb_sb = sb("rb_sb", [P, NE])

        def view(kb, n):
            return arena[:, kb * 256:kb * 256 + n]

        x_sb = view(0, NT * D).rearrange("p (t c) -> p t c", t=NT)
        bias_t = view(0, NH * S).rearrange("p (h m) -> p h m", h=NH)
        prob = view(8, 2 * S).rearrange("p (b m) -> p b m", b=2)
        probT = view(12, 2 * S).rearrange("p (b m) -> p b m", b=2)
        pT = view(16, 10 * S).rearrange("p (j s) -> p j s", j=10)
        pR = view(36, NT * 768).rearrange("p (t c) -> p t c", t=NT)
        acc0 = view(48, 2048)
        ypad = view(48, 2 * (PADT + S)).rearrange("p (c s) -> p c s", c=2)
        acc12 = view(56, 2048)
        wmixT = view(53, NH * P).rearrange("p (h i) -> p h i", h=NH)
        poolw = view(55, 2 * P).rearrange("p (c d) -> p c d", c=2)
        gate2 = view(56, D)
        bias_row = view(40, NDIST)[0:NH, :]
        dense = pT[:, 2:4, :].rearrange("p c s -> p (c s)")
        sqv = pT[:, 0:2, :].rearrange("p c s -> p (c s)")
        b_f32 = view(0, 3072)
        b_bf = view(12, 1536).bitcast(BF16)[0:96, :]
        x1 = view(18, NT * D).rearrange("p (t c) -> p t c", t=NT)
        gated = view(38, D)
        sq_dump = view(42, GW)
        g2row = view(46, D)
        gate1 = view(50, D)
        a_g, a_s, a_l = (view(4 * i, DFF) for i in range(3))
        aT = view(34, D).rearrange("p (c s) -> p c s", c=KC)
        xT = view(38, D).rearrange("p (c s) -> p c s", c=KC)
        xg = view(42, D)
        y_sb = view(46, D)
        hot = view(50, NT * P).rearrange("p (t s) -> p t s", t=NT)
        selA = view(52, P // 2).bitcast(BF16)
        selB = arena[:, 52 * 256 + P // 2:52 * 256 + P].bitcast(BF16)
        routing = view(60, 1024)
        fin_g = rows[:, 0, :]

        lg = routing[:, 0:NT * NE].rearrange("p (t e) -> p t e", t=NT)
        memb = routing[:, 128:256].rearrange("p (t e) -> p t e", t=NT)
        pos = routing[:, 256:384].rearrange("p (t e) -> p t e", t=NT)
        eqk = routing[:, 384:512].rearrange("p (t e) -> p t e", t=NT)
        tmpk = routing[:, 512:640].rearrange("p (t e) -> p t e", t=NT)
        v8 = routing[:, 640:672].rearrange("p (t k) -> p t k", t=NT)
        i8 = routing[:, 672:704].bitcast(U32).rearrange("p (t k) -> p t k", t=NT)
        i8f = routing[:, 704:736].rearrange("p (t k) -> p t k", t=NT)
        gk = routing[:, 736:752].rearrange("p (t k) -> p t k", t=NT)
        gsum = routing[:, 752:756]
        cnt = routing[:, 768:800]
        nblk = routing[:, 800:832]
        bend = routing[:, 832:864]
        bstart = routing[:, 864:896]
        slot_no = routing[:, 896:1024]
        vtab = view(53, NT * NE * 4).rearrange("p (t e c) -> p t e c", t=NT, c=4)
        egf = sb("egf", [P, MAXBLK])
        egi = sb("egi", [P, MAXBLK], U32)
        bendi = sb("bendi", [P, NE + 1], U32)
        idx_out = sb("idx_out", [P, MAXBLK], U32)
        idx_tok = sb("idx_tok", [P, MAXBLK], U32)
        gcol = sb("gcol", [P, MAXBLK])
        cur_out = sb("cur_out", [P, 1], U32)
        cur_tok = sb("cur_tok", [P, 1], U32)
        cmp_be = view(0, MAXBLK * NE).rearrange("p (b e) -> p b e", b=MAXBLK)

        ps = ctx.enter_context(nc.psum_tensor("ps", [P, 8, 512], F32))

        bias_d = nc.dram_tensor("bias_scratch", [NH, NDIST], F32).ap()
        skew_d = nc.dram_tensor("skew_scratch", [NH, P, NDIST], F32).ap()
        h2_d = nc.dram_tensor("h2_scratch", [S, D], F32).ap()
        ys_d = nc.dram_tensor("ys_scratch", [S * TOPK, D], F32).ap()

        ident = cst[:, C_ID:C_ID + P]
        ones = cst[:, C_ONES:C_ONES + P]
        eps = cst[:, C_EPS:C_EPS + 1]

        def col(r):
            return pc[:, r:r + 1]

        l_cst, l_par, l_x, l_row, l_sgu = (sem("l_" + n) for n in ("cst", "par", "x", "row", "sgu"))
        l_w1 = [sem(f"l_w1_{k}") for k in range(KC)]
        l_w2 = [sem(f"l_w2_{c}") for c in range(4)]
        l_bt, l_x1, l_be, l_pw = (sem("l_" + n) for n in ("bt", "x1", "be", "pw"))
        l_fin = [sem(f"l_fin_{t}") for t in range(NT)]
        st_bias, st_h2, st_out = (sem("st_" + n) for n in ("bias", "h2", "out"))
        names = """e_act e_glu m_modA t_par c_par c_cond v_ss a_ss v_var a_sd v_xn t_bias c_bias v_mod0 m_mod0 c_mod t_hT a_hT
                   p_proj e_proj w1_free a_scaled g_added g_acc m_mod c_mod12 t_wmix c_wmix g_pw v_conv t_conv
                   v_convE v_poolT m_pool v_sgu m_sgu v_sguE s_att v_att a_att t_att a_attT o_att v_attO
                   v_cx a_silu v_mixed t_mixT a_mixT m_out v_x1 v_h2 t_h2T a_h2T m_lg v_gexp a_gexp v_memb m_rank
                   v_tables g_bf v_chain v_conv_in""".split()
        s = {n: sem(n) for n in names}
        (b_hot, b_tab, b_idx, b_gat, b_xps, b_xT, b_min, b_sig, b_hread, b_act, b_aps, b_aT, b_yev, b_sca,
         b_selA, b_selB, b_chain, b_cur, b_curs, b_lin, b_issued) = (sem("b_" + n) for n in (
             "hot", "tab", "idx", "gat", "xps", "xT", "min", "sig", "hread", "act", "aps", "aT", "yev",
             "sca", "selA", "selB", "chain", "cur", "curs", "lin", "issued"))
        w1_used, w2_used = sem("w1_used"), sem("w2_used")
        f_sum, f_sq, f_sd, f_o = sem("f_sum"), sem("f_sq"), sem("f_sd"), sem("f_o")

        x_rows = a["x"].rearrange("b (t p) d -> p (b t) d", p=P)
        wmod_r = a["w_mod"].rearrange("l (k p) (g n) -> (l k) p g n", p=P, g=6)
        win_r = a["w_in"].rearrange("l (k p) n -> (l k) p n", p=P)
        wout_r = a["w_out"].rearrange("l (c j p) n -> (l c) p j n", p=P, j=2)
        w1_r = a["exp_w1"].rearrange("l e (k p) n -> (l e) k p n", p=P)
        w2_r = a["exp_w2"].rearrange("l e (c p j) n -> (l e) c p (j n)", p=P, j=2)
        ys_r = ys_d.rearrange("(t p k) d -> t p (k d)", p=P, k=TOPK)
        out_r = out_d.rearrange("b (t p) d -> (b t) p d", p=P)
        N_PAR = 12

        def part(t):
            return slice(P * t, P * (t + 1))

        PROJ = [("g", 0, 2), ("a", 0, 0), ("g", 1, 3), ("a", 1, 1), ("f", 4, 4), ("f", 5, 5), ("f", 6, 6), ("f", 7, 7)]
        PROJ += [("v", t, None) for t in range(NT)]
        PROJ += [("f", 8, 10), ("f", 9, 11)]
        PROJ += [("s", t, None) for t in range(NT)]
        NPROJ = len(PROJ)
        ATT = [(h, q) for q in range(NT) for h in range(NH)]
        NA = len(ATT)

        def settle(eng):
            eng.wait_ge(s["v_tables"], 1)

        block = ctx.enter_context(nc.Block())

        @block.sync
        def _(sp):
            sp.dma_start(cst[:], consts_d).then_inc(l_cst, 16)
            for r, name in ((R_C, "c"), (R_N1, "norm1_g"), (R_N2, "norm2_g"), (R_MIX, "mix_out_g"), (R_CB, "conv_b")):
                n = a[name].shape[1] // P
                sp.dma_start(parms[r:r + n, :], a[name].rearrange("l (r q) -> (l r) q", q=P)).then_inc(l_par, 16)
            sp.dma_start(parms[R_BMOD:R_BMOD + 48, :], a["b_mod"].rearrange("l (r q) -> (l r) q", q=P)).then_inc(l_par, 16)
            sp.dma_start(taps_r[:], a["conv_w"].rearrange("l t (h q) -> (l t h) q", q=P)).then_inc(l_par, 16)
            sp.dma_start(sgub_r[:], a["sgu_b"].rearrange("l h q -> (l h) q")).then_inc(l_par, 16)
            sp.dma_start(relb[0:NBUCK, :], a["rel_bias"]).then_inc(l_par, 16)
            sp.dma_start(relb[NBUCK:NBUCK + 1, :], consts_d[0:1, C_ONES:C_ONES + NH]).then_inc(l_par, 16)
            sp.dma_start(buckets, buckets_d).then_inc(l_par, 16)
            sp.dma_start(sguw_r, a["sgu_w"].rearrange("l h i j -> i (l h) j")).then_inc(l_par, 16)
            for k in range(KC):
                sp.dma_start(w1_slots[:, k, :].rearrange("p (g n) -> p g n", g=2), wmod_r[k][:, 0:2, :]).then_inc(l_w1[k], 16)
                if k == 1:
                    sp.dma_start(x_sb, x_rows).then_inc(l_x, 16)
            for k in range(KC):
                sp.wait_ge(s["v_mod0"], k + 1)
                sp.dma_start(w1_slots[:, k, :], win_r[k]).then_inc(l_w1[k], 16)
            for i in range(2 * KC):
                if i >= 4:
                    sp.wait_ge(s["g_added"], i - 3)
                dst = w2_slots[:, i % 4, :].rearrange("p (g n) -> p g n", g=2)
                if i < KC:
                    sp.dma_start(dst, wmod_r[i][:, 3:5, :]).then_inc(l_w2[i % 4], 16)
                else:
                    sp.dma_start(dst[:, 0, :], wmod_r[i - KC][:, 2, :]).then_inc(l_w2[i % 4], 16)
                    sp.dma_start(dst[:, 1, :], wmod_r[i - KC][:, 5, :]).then_inc(l_w2[i % 4], 16)
            for c in range(4):
                sp.wait_ge(s["g_added"], 2 * KC - 3 + c)
                sp.dma_start(w2_slots[:, c, :].rearrange("p (j n) -> p j n", j=2), wout_r[c]).then_inc(l_w2[c], 16)
            for k in range(KC):
                sp.wait_ge(s["p_proj"], NPROJ)
                sp.dma_start(w1_slots[:, k, :], w1_r[0, k]).then_inc(l_w1[k], 16)
            for t in range(NT):
                sp.wait_ge(s["v_h2"], t + 1)
                sp.dma_start(h2_d[part(t), :], rows[:, t, :]).then_inc(st_h2, 16)
            for c in range(4):
                sp.wait_ge(s["m_out"], 2 * NT)
                sp.dma_start(w2_slots[:, c, :], w2_r[0, c]).then_inc(l_w2[c], 16)
            sp.wait_ge(s["v_tables"], 1)

            def load_w1(e, ge):
                for k in range(KC):
                    sp.wait_ge(w1_used, ge * KC + (k + 1))
                    settle(sp)
                    sp.wait_ge(l_w1[k], 16 * (e + 2))
                    settle(sp)
                    sp.dma_start(w1_slots[:, k, :], w1_r[e, k]).then_inc(l_w1[k], 16)

            def load_w2(e, ge):
                for c in range(4):
                    sp.wait_ge(w2_used, ge * 4 + (c + 1))
                    settle(sp)
                    sp.wait_ge(l_w2[c], 16 * (e + 7))
                    settle(sp)
                    sp.dma_start(w2_slots[:, c, :], w2_r[e, c]).then_inc(l_w2[c], 16)

            ge0 = sp.value_load(bendi[0:1, 0:1], min_val=0, max_val=MAXBLK - 1)
            load_w1(1, ge0)
            with sp.Fori(2, NE) as e:
                ge_w1 = sp.value_load(bendi[0:1, bass.ds(e - 1, 1)], min_val=0, max_val=MAXBLK - 1)
                load_w1(e, ge_w1)
                ge_w2 = sp.value_load(bendi[0:1, bass.ds(e - 2, 1)], min_val=0, max_val=MAXBLK - 1)
                load_w2(e - 1, ge_w2)
            ge_l = sp.value_load(bendi[0:1, NE - 2:NE - 1], min_val=0, max_val=MAXBLK - 1)
            load_w2(NE - 1, ge_l)
            last = sp.value_load(bendi[0:1, NE:NE + 1], min_val=0, max_val=MAXBLK - 2)
            sp.wait_ge(b_sca, last * 16 + 16)
            sp.wait_ge(w1_used, last * KC + 2 * KC)
            for k in range(KC):
                sp.wait_ge(l_w1[k], 16 * (NE + 2))
            for t in range(NT):
                sp.dma_start(w1_slots[:, 2 * t:2 * t + 2, :], ys_r[t].rearrange("p (a b) -> p a b", a=2)).then_inc(l_fin[t], 16)
            for t in range(NT):
                sp.wait_ge(f_o, t + 1)
                sp.dma_start(out_r[t], x1[:, t, :]).then_inc(st_out, 16)
            sp.wait_ge(st_out, 16 * NT)

        @block.gpsimd
        def _(pool):
            for i, name in enumerate(("conv_norm_g", "conv_norm_b", "pool_scale", "sgu_norm_g", "sgu_norm_b")):
                pool.dma_start(lrows[:, i, :], a[name].to_broadcast([P, GW])).then_inc(l_row, 16)
            pool.dma_start(rb_sb[:], a["router_b"].to_broadcast([P, NE])).then_inc(l_row, 16)
            pool.dma_start(rw_sb[:], a["router_w"].rearrange("l (k p) e -> p (l k) e", p=P)).then_inc(l_row, 16)
            pool.wait_ge(s["c_bias"], 1)
            pool.dma_start(bias_d, bias_row).then_inc(st_bias, 16)
            pool.wait_ge(s["v_xn"], NT)
            pool.wait_ge(st_bias, 16)
            for h in range(NH):
                pool.dma_start(skew_d[h], bias_d[h:h + 1, :].to_broadcast([P, NDIST])).then_inc(st_bias, 16)
            pool.wait_ge(st_bias, 80)
            pool.dma_start(bias_t, bass.AP(tensor=skew_d.tensor, offset=P - 1,
                                           ap=[[NDIST - 1, P], [P * NDIST, NH], [1, S]])).then_inc(l_bt, 16)
            pool.wait_ge(s["m_mod0"], 1)
            nc.gpsimd.memset(poolw, 0.0).then_inc(s["g_pw"], 1)
            pool.wait_ge(s["g_pw"], 1)
            for g in range(4):
                q = slice(64 * (g % 2), 64 * (g % 2) + 64)
                pool.dma_start(poolw[q, g // 2, q], a["pool_w"][0, g]).then_inc(l_pw, 16)
            for i in range(2 * KC):
                pool.wait_ge(s["a_scaled"], i + 1)
                if i == KC:
                    pool.wait_ge(s["m_modA"], 1)
                if i % KC == 0:
                    nc.gpsimd.tensor_copy(acc12, w2_slots[:, i % 4, :]).then_inc(s["g_added"], 1)
                else:
                    pool.wait_ge(s["g_added"], i)
                    nc.gpsimd.tensor_tensor(acc12, acc12, w2_slots[:, i % 4, :], ALU.add).then_inc(s["g_added"], 1)
            pool.wait_ge(s["v_attO"], NA)
            pool.wait_ge(s["v_sguE"], 8)
            pool.dma_start(x1, x_rows).then_inc(l_x1, 16)
            pool.dma_start(gate1, a["b_mod"][:, 2 * D:3 * D].to_broadcast([P, D])).then_inc(l_x1, 16)
            pool.dma_start(g2row, a["b_mod"][:, 5 * D:6 * D].to_broadcast([P, D])).then_inc(l_x1, 16)
            for j in range(3):
                pool.dma_start(b_f32[32 * j:32 * j + 32, 0:2048], a["exp_b1"][0]).then_inc(l_be, 16)
                pool.dma_start(b_f32[32 * j:32 * j + 32, 2048:3072], a["exp_b2"][0]).then_inc(l_be, 16)
            pool.wait_ge(l_be, 96)
            nc.gpsimd.tensor_copy(b_bf, b_f32[0:96, :]).then_inc(s["g_bf"], 1)
            pool.wait_ge(s["g_bf"], 1)
            nc.gpsimd.tensor_tensor(b_f32[0:96, :], b_f32[0:96, :], b_bf, ALU.subtract).then_inc(s["g_bf"], 1)
            pool.wait_ge(s["g_bf"], 2)
            nc.gpsimd.tensor_copy(b_bf[32:64, :], b_f32[32:64, :]).then_inc(s["g_bf"], 1)
            nc.gpsimd.tensor_copy(b_bf[64:96, :], b_f32[64:96, :]).then_inc(s["g_bf"], 1)
            pool.wait_ge(s["g_bf"], 4)
            nc.gpsimd.tensor_tensor(b_f32[64:96, :], b_f32[64:96, :], b_bf[64:96, :], ALU.subtract).then_inc(s["g_bf"], 1)
            pool.wait_ge(s["g_bf"], 5)
            nc.gpsimd.tensor_copy(b_bf[64:96, :], b_f32[64:96, :]).then_inc(s["g_bf"], 1)

            def gather(g):
                pool.wait_ge(b_idx, g + 1)
                nc.gpsimd.tensor_copy(cur_tok[:], idx_tok[:, bass.ds(g, 1)]).then_inc(b_cur, 1)
                pool.wait_ge(b_cur, g + 1)
                pool.sem_inc(b_issued, 1)
                pool.indirect_dma_start(xg, None, h2_d, bass.IndirectOffsetOnAxis(ap=cur_tok[:], axis=0)).then_inc(b_gat, 16)

            def scatter(g):
                pool.wait_ge(b_yev, g + 2)
                nc.gpsimd.tensor_copy(cur_out[:], idx_out[:, bass.ds(g, 1)]).then_inc(b_curs, 1)
                pool.wait_ge(b_curs, g + 1)
                pool.sem_inc(b_issued, 1)
                pool.indirect_dma_start(ys_d, bass.IndirectOffsetOnAxis(ap=cur_out[:], axis=0), y_sb, None,
                                        bounds_check=S * TOPK - 1, oob_is_err=False).then_inc(b_sca, 16)

            pool.wait_ge(st_h2, 16 * NT)
            pool.wait_ge(s["t_h2T"], KC)
            pool.dma_start(fin_g, a["final_norm_g"].rearrange("(l d) -> l d", l=1).to_broadcast([P, D])).then_inc(l_x1, 16)
            pool.wait_ge(s["v_tables"], 1)
            last_b = pool.value_load(bendi[0:1, NE:NE + 1], min_val=0, max_val=MAXBLK - 2)
            gather(0)
            pool.wait_ge(b_xps, 1)
            gather(1)
            with pool.Fori(1, last_b + 1) as g:
                pool.wait_ge(b_xps, g + 1)
                pool.wait_ge(b_gat, g * 16 + 16)
                gather(g + 1)
                scatter(g - 1)
                pool.wait_ge(b_sca, g * 16)
            scatter(last_b)

        @block.scalar
        def _(act):
            act.wait_ge(l_cst, 16)
            act.wait_ge(s["c_par"], 1)
            nc.scalar.activation(cond[:], pc[:, R_C:R_C + KC], ACT.Silu).then_inc(s["c_cond"], 1)
            act.wait_ge(l_x, 16)
            for t in range(NT):
                nc.scalar.activation(rows[:, t, :], x_sb[:, t, :], ACT.Square, accum_out=st[:, t:t + 1]).then_inc(s["a_ss"], 1)

            sq = [0]

            def root(dst, src, n):
                sq[0] += 1
                act.wait_ge(s["v_var"], sq[0])
                nc.scalar.activation(dst, src, ACT.Sqrt, bias=eps, scale=1.0 / n).then_inc(s["a_sd"], 1)


            def own_root(dst, src, n, sums):
                act.wait_ge(s["a_ss"], sums)
                nc.scalar.activation(dst, src, ACT.Sqrt, bias=eps, scale=1.0 / n).then_inc(s["a_sd"], 1)

            own_root(st[:, 4:8], st[:, 0:4], D, NT)
            act.wait_ge(s["c_mod"], 1)
            for k in range(KC):
                act.wait_ge(s["t_hT"], k + 1)
                nc.scalar.activation(colsT[:, k, :], ps[:, k % 2, :], ACT.Identity, bias=mod[:, k:k + 1],
                                     scale=gs1[:, k:k + 1]).then_inc(s["a_hT"], 1)
            for i, (kind, n, _) in enumerate(PROJ):
                bank = ps[:, 2 + i % 4, :]
                if kind != "a":
                    act.wait_ge(s["p_proj"], i + 1)
                if kind == "g":
                    nc.scalar.activation(pT[:, 2 + n, :], bank, ACT.Sigmoid).then_inc(s["e_act"], 1)
                elif kind == "f":
                    nc.scalar.activation(pT[:, n, :], bank, ACT.Copy).then_inc(s["e_act"], 1)
                elif kind == "v":
                    act.wait_ge(st_bias, 16)
                    nc.scalar.activation(pR[:, n, 0:GW], bank[:, 0:GW], ACT.Copy).then_inc(s["e_act"], 1)
                elif kind == "s":
                    nc.scalar.activation(pR[:, n, GW:3 * GW], bank, ACT.Gelu).then_inc(s["e_act"], 1)
                if i >= 2:
                    c = i - 2
                    act.wait_ge(l_w2[c % 4], 16 * (c // 4 + 1) if c < KC else 32 * (c // 4))
                    nc.scalar.activation(w2_slots[:, c % 4, :], w2_slots[:, c % 4, :], ACT.Copy,
                                         scale=cond[:, c % KC:c % KC + 1]).then_inc(s["a_scaled"], 1)
            root(st[:, 32:48], st[:, 16:32], HD)
            root(st[:, 52:56], st[:, 48:52], GW)
            act.wait_ge(s["v_cx"], 1)
            nc.scalar.activation(rows[:, :, 0:GW], rows[:, :, 0:GW], ACT.Silu).then_inc(s["a_silu"], 1)

            def att_exp(i):
                h, q = ATT[i]
                n = P * (q + 1)
                act.wait_ge(s["v_att"], i + 1)
                nc.scalar.activation(prob[:, i % 2, 0:n], prob[:, i % 2, 0:n], ACT.Exp, bias=st[:, 64 + i:65 + i],
                                     accum_out=st[:, 80 + i:81 + i]).then_inc(s["a_att"], 1)

            def att_evac(i):
                n = P * (ATT[i][1] + 1)
                act.wait_ge(s["t_att"], i + 1)
                if i >= 2:
                    act.wait_ge(s["o_att"], i - 1)
                nc.scalar.activation(probT[:, i % 2, 0:n], ps[:, i % 2, 0:n], ACT.Copy).then_inc(s["a_attT"], 1)

            for i in range(NA + 1):
                if i < NA:
                    att_exp(i)
                if i >= 1:
                    att_evac(i - 1)
            act.wait_ge(s["a_silu"], 1)
            act.wait_ge(s["v_convE"], 1)
            act.wait_ge(s["v_attO"], NA)
            act.wait_ge(s["v_sguE"], 8)
            for t in range(NT):
                for m in range(4):
                    nc.scalar.activation(sq_dump, rows[:, t, GW * m:GW * m + GW], ACT.Square,
                                         accum_out=st[:, 96 + 4 * t + m:97 + 4 * t + m]).then_inc(s["a_ss"], 1)
                    act.wait_ge(s["a_ss"], NT + 4 * t + m + 1)
            own_root(st[:, 112:128], st[:, 96:112], GW, NT + 16)
            for k in range(KC):
                act.wait_ge(s["t_mixT"], k + 1)
                nc.scalar.activation(colsT[:, k, :], ps[:, k % 2, :], ACT.Copy, scale=col(R_MIX + k)).then_inc(s["a_mixT"], 1)
            for t in range(NT):
                act.wait_ge(s["v_x1"], t + 1)
                nc.scalar.activation(rows[:, t, :], x1[:, t, :], ACT.Square, accum_out=st[:, 128 + t:129 + t]).then_inc(s["a_ss"], 1)
            own_root(st[:, 132:136], st[:, 128:132], D, 2 * NT + 16)
            for k in range(KC):
                act.wait_ge(s["t_h2T"], k + 1)
                nc.scalar.activation(colsT[:, k, :], ps[:, k % 2, :], ACT.Identity, bias=mod[:, 24 + k:25 + k],
                                     scale=gs2[:, k:k + 1]).then_inc(s["a_h2T"], 1)
            act.wait_ge(s["v_gexp"], 1)
            nc.scalar.activation(gk[:], gk[:], ACT.Exp).then_inc(s["a_gexp"], 1)

            act.wait_ge(s["v_tables"], 1)
            last_b = act.value_load(bendi[0:1, NE:NE + 1], min_val=0, max_val=MAXBLK - 2)

            def evac_xT(g):
                act.wait_ge(b_xps, g + 1)
                for k in range(KC):
                    last = nc.scalar.activation(xT[:, k, :], ps[:, 6 + k // 4, P * (k % 4):P * (k % 4) + P], ACT.Identity,
                                                bias=mod[:, 24 + k:25 + k], scale=gs2[:, k:k + 1])
                last.then_inc(b_xT, 1)

            def evac_aT(g):
                act.wait_ge(b_aps, g + 1)
                for j in range(2):
                    last = nc.scalar.activation(aT[:, 4 * j:4 * j + 4, :], ps[:, 6 + j, :].rearrange("p (c q) -> p c q", c=4), ACT.Copy)
                last.then_inc(b_aT, 1)

            def sigmoid(g):
                for j in range(2):
                    act.wait_ge(b_min, g * 2 + (j + 1))
                    sl = slice(512 * j, 512 * j + 512)
                    nc.scalar.activation(a_s[:, sl], a_g[:, sl], ACT.Sigmoid, scale=ALPHA).then_inc(b_sig, 1)

            def evac_y(g, wait_scatter):
                act.wait_ge(w2_used, g * 4 + 8)
                if wait_scatter:
                    act.wait_ge(b_sca, g * 16)
                nc.scalar.activation(y_sb.rearrange("p (j n) -> p j n", j=2), ps[:, 4:6, :], ACT.Copy,
                                     scale=gcol[:, bass.ds(g, 1)]).then_inc(b_yev, 1)

            evac_xT(0)
            sigmoid(0)
            evac_xT(1)
            evac_aT(0)
            sigmoid(1)
            evac_xT(2)
            evac_y(0, False)
            with act.Fori(2, last_b + 1) as g:
                evac_aT(g - 1)
                sigmoid(g)
                evac_xT(g + 1)
                evac_y(g - 1, True)
            evac_aT(last_b)
            evac_y(last_b, True)
            for t in range(NT):
                act.wait_ge(f_sum, t + 1)
                nc.scalar.activation(a_g, x1[:, t, :], ACT.Square, accum_out=st[:, t:t + 1]).then_inc(f_sq, 1)
                act.wait_ge(f_sq, t + 1)
                nc.scalar.activation(st[:, 4 + t:5 + t], st[:, t:t + 1], ACT.Sqrt, bias=eps, scale=1.0 / D).then_inc(f_sd, 1)

        @block.vector
        def _(dve):
            V = nc.vector
            chain = [0]

            def link(ins):
                chain[0] += 1
                ins.then_inc(s["v_chain"], 1)
                dve.wait_ge(s["v_chain"], chain[0])


            dve.wait_ge(s["t_par"], 3)
            link(V.tensor_copy(pc[:], ps[:, 0, 0:R_N + 2 * TAPS]))
            V.tensor_copy(sgub[:], ps[:, 0, 256:256 + NH]).then_inc(s["c_par"], 1)
            dve.wait_ge(s["c_cond"], 1)
            dve.wait_ge(s["t_bias"], 1)
            V.tensor_copy(bias_row, ps[0:NH, 6:8, :].rearrange("p b m -> p (b m)")[:, 0:NDIST]).then_inc(s["c_bias"], 1)
            for k in range(KC):
                dve.wait_ge(l_w1[k], 16)
                if k == 0:
                    V.tensor_scalar(acc0, w1_slots[:, 0, :], cond[:, 0:1], None, ALU.mult).then_inc(s["v_mod0"], 1)
                else:
                    dve.wait_ge(s["v_mod0"], k)
                    V.scalar_tensor_tensor(acc0, w1_slots[:, k, :], cond[:, k:k + 1], acc0, ALU.mult, ALU.add).then_inc(s["v_mod0"], 1)
                if k == 3:
                    dve.wait_ge(s["a_sd"], 1)
                    link(V.reciprocal(st[:, 8:12], st[:, 4:8]))
                    for t in range(NT):
                        V.tensor_scalar(rows[:, t, :], x_sb[:, t, :], st[:, 8 + t:9 + t], None, ALU.mult).then_inc(s["v_xn"], 1)
            dve.wait_ge(s["m_mod0"], 1)
            link(V.tensor_tensor(mod[:, 0:16], ps[:, 2, 0:16], pc[:, R_BMOD:R_BMOD + 16], ALU.add))
            V.scalar_tensor_tensor(gs1[:], mod[:, 8:16], 1.0, pc[:, R_N1:R_N1 + KC], ALU.add, ALU.mult).then_inc(s["c_mod"], 1)
            dve.wait_ge(s["t_wmix"], 1)
            V.tensor_tensor(wmixT, ps[:, 1, :].rearrange("p (h i) -> p h i", h=NH),
                            cst[:, None, C_TRI:C_TRI + P].to_broadcast([P, NH, P]), ALU.mult).then_inc(s["c_wmix"], 1)
            dve.wait_ge(s["m_mod0"], 1)
            link(V.memset(ypad[:, :, 0:PADT], 0.0))
            for c in range(2):
                dve.wait_ge(s["p_proj"], 2 * c + 2)
                dve.wait_ge(s["e_act"], c + 1)
                V.tensor_tensor(ypad[:, c, PADT:PADT + S], ps[:, 3 + 2 * c, :], pT[:, 2 + c, :], ALU.mult).then_inc(s["e_glu"], 1)
            dve.wait_ge(s["e_glu"], 2)
            for tap in range(TAPS):
                for c in range(2):
                    w = taps[:, 2 * tap + c:2 * tap + c + 1]
                    src = ypad[:, c, tap:tap + S]
                    if tap:
                        dve.wait_ge(s["v_conv"], 2 * tap + c - 1)
                        V.scalar_tensor_tensor(pT[:, c, :], src, w, pT[:, c, :], ALU.mult, ALU.add).then_inc(s["v_conv"], 1)
                    else:
                        V.tensor_scalar(pT[:, c, :], src, w, col(R_CB + c), ALU.mult, ALU.add).then_inc(s["v_conv"], 1)
            dve.wait_ge(s["e_act"], 12)
            dve.wait_ge(l_row, 16 * 7)
            A, B = pT[:, 2, :], pT[:, 3, :]

            def double(dst, src, lag, half):
                q = slice(64, P) if half else slice(0, P)
                V.tensor_copy(dst[q, 0:lag], src[q, 0:lag]).then_inc(s["v_chain"], 1)
                chain[0] += 1
                link(V.tensor_tensor(dst[q, lag:S], src[q, lag:S], src[q, 0:S - lag], ALU.add))

            def pooled(c, lo, hi):
                for q, src in ((slice(0, 64), lo), (slice(64, P), hi)):
                    z = pT[q, 8 + c, :]
                    link(V.tensor_tensor(src[q, 0:16], src[q, 0:16], cst[q, C_RC + 16 * c:C_RC + 16 * c + 16], ALU.mult))
                    link(V.tensor_tensor(z[:, 0:16], src[q, 0:16], z[:, 0:16], ALU.subtract))
                    link(V.scalar_tensor_tensor(z[:, 16:S], src[q, 16:S], cst[q, C_RW + c:C_RW + c + 1], z[:, 16:S],
                                                ALU.mult, ALU.subtract))

            double(A, pT[:, 8, :], 1, False)
            double(B, A, 2, True)
            pooled(0, A, B)
            double(A, pT[:, 9, :], 1, False)
            double(B, A, 2, False)
            double(A, B, 4, False)
            double(B, A, 8, True)
            pooled(1, A, B)
            V.memset(st[:, 159:160], 0.0).then_inc(s["v_poolT"], 1)

            dve.wait_ge(s["m_modA"], 1)
            link(V.tensor_tensor(mod[:, 24:40], ps[:, 0, 0:16], pc[:, R_BMOD + 24:R_BMOD + 40], ALU.add))
            V.scalar_tensor_tensor(gs2[:], mod[:, 32:40], 1.0, pc[:, R_N2:R_N2 + KC], ALU.add, ALU.mult).then_inc(s["c_mod12"], 1)

            def centre(dst, src, n, base, g):
                m = st[:, base:base + g]
                link(V.tensor_reduce(m, src, AX.X, ALU.add))
                link(V.tensor_scalar(m, m, -1.0 / n, None, ALU.mult))
                link(V.tensor_tensor(dst, src, m[:, :, None].to_broadcast([P, g, n]), ALU.add))

            dve.wait_ge(s["t_conv"], 1)
            cps = ps[:, 6:8, :].rearrange("p b (t c) -> p (b t) c", t=2).rearrange("p t (h d) -> p (t h) d", h=NH)
            cx = rows[:, :, 0:GW]
            dv = dense.rearrange("p (g n) -> p g n", n=HD)
            centre(dv, cps, HD, 16, 16)
            link(V.tensor_tensor(sqv, dense, dense, ALU.mult))
            V.tensor_reduce(st[:, 16:32], sqv.rearrange("p (g n) -> p g n", n=HD), AX.X, ALU.add).then_inc(s["v_var"], 1)
            dve.wait_ge(s["a_sd"], 2)
            link(V.reciprocal(st[:, 16:32], st[:, 32:48]))
            link(V.tensor_tensor(dv, dv, st[:, 16:32, None].to_broadcast([P, 16, HD]), ALU.mult))
            d4 = dense.rearrange("p (t c) -> p t c", t=NT)
            link(V.tensor_tensor(d4, d4, lrows[:, None, 0, :].to_broadcast([P, NT, GW]), ALU.mult))
            V.tensor_tensor(cx, d4, lrows[:, None, 1, :].to_broadcast([P, NT, GW]), ALU.add).then_inc(s["v_cx"], 1)
            dve.wait_ge(s["e_act"], NPROJ - 2)
            sv = pR[:, :, 2 * GW:3 * GW]
            dve.wait_ge(s["v_cx"], 1)
            centre(d4, sv, GW, 48, 4)
            link(V.tensor_tensor(sqv, dense, dense, ALU.mult))
            V.tensor_reduce(st[:, 48:52], sqv.rearrange("p (g n) -> p g n", n=GW), AX.X, ALU.add).then_inc(s["v_var"], 1)
            dve.wait_ge(s["a_sd"], 3)
            link(V.reciprocal(st[:, 48:52], st[:, 52:56]))
            link(V.tensor_tensor(d4, d4, st[:, 48:52, None].to_broadcast([P, NT, GW]), ALU.mult))
            link(V.tensor_tensor(d4, d4, lrows[:, None, 3, :].to_broadcast([P, NT, GW]), ALU.mult))
            V.tensor_tensor(sv, d4, lrows[:, None, 4, :].to_broadcast([P, NT, GW]), ALU.add).then_inc(s["v_sgu"], 1)
            dve.wait_ge(s["m_pool"], 1)
            V.tensor_tensor(rows[:, :, 2 * GW:3 * GW], ps[:, 4:6, :].rearrange("p b (t c) -> p (b t) c", t=2),
                            lrows[:, None, 2, :].to_broadcast([P, NT, GW]), ALU.mult).then_inc(s["v_convE"], 1)

            def att_scores(i):
                h, q = ATT[i]
                n = P * (q + 1)
                dve.wait_ge(s["s_att"], i + 1)
                if i >= 2:
                    dve.wait_ge(s["t_att"], i - 1)
                link(V.scalar_tensor_tensor(prob[:, i % 2, 0:n], ps[:, 6 + h % 2, 0:n], HD ** -0.5,
                                            bias_t[:, h, S - P - P * q:S], ALU.mult, ALU.add))
                V.tensor_reduce(st[:, 64 + i:65 + i], prob[:, i % 2, 0:n], AX.X, ALU.max, negate=True).then_inc(s["v_att"], 1)

            def att_norm(i):
                h, q = ATT[i]
                dve.wait_ge(s["o_att"], i + 1)
                link(V.reciprocal(st[:, 80 + i:81 + i], st[:, 80 + i:81 + i]))
                V.tensor_scalar(rows[:, q, GW + HD * h:GW + HD * h + HD], ps[:, 2 + i % 2, 0:HD], st[:, 80 + i:81 + i],
                                None, ALU.mult).then_inc(s["v_attO"], 1)

            dve.wait_ge(l_bt, 16)
            for i in range(NA + 2):
                if i < NA:
                    att_scores(i)
                if i == 2:
                    dve.wait_ge(s["m_sgu"], 1)
                    for h in range(NH):
                        o = slice(HD * h, HD * h + HD)
                        for b in range(2):
                            t2 = slice(2 * b, 2 * b + 2)
                            V.scalar_tensor_tensor(rows[:, t2, 3 * GW + HD * h:3 * GW + HD * h + HD],
                                                   ps[:, 4 + b, :].rearrange("p (t c) -> p t c", t=2)[:, :, o], sgub[:, h:h + 1],
                                                   pR[:, t2, GW + HD * h:GW + HD * h + HD], ALU.add, ALU.mult).then_inc(s["v_sguE"], 1)
                if i >= 2:
                    att_norm(i - 2)
            dve.wait_ge(s["m_mod"], 1)
            dve.wait_ge(l_x1, 48)
            V.tensor_tensor(gate1, gate1, ps[:, 4:6, :].rearrange("p b n -> p (b n)"), ALU.add).then_inc(s["c_mod12"], 1)
            V.tensor_tensor(gate2, g2row, ps[:, 6:8, :].rearrange("p b n -> p (b n)"), ALU.add).then_inc(s["c_mod12"], 1)
            dve.wait_ge(s["a_sd"], 4)
            link(V.reciprocal(st[:, 112:128], st[:, 112:128]))
            for t in range(NT):
                r = rows[:, t, :].rearrange("p (m c) -> p m c", m=4)
                V.tensor_tensor(r, r, st[:, 112 + 4 * t:116 + 4 * t, None].to_broadcast([P, 4, GW]), ALU.mult).then_inc(s["v_mixed"], 1)
            for t in range(NT):
                dve.wait_ge(s["m_out"], 2 * t + 2)
                po = ps[:, 2 + 2 * (t % 2):4 + 2 * (t % 2), :].rearrange("p b n -> p (b n)")
                if t == 0:
                    dve.wait_ge(s["c_mod12"], 3)
                link(V.tensor_tensor(gated, po, gate1, ALU.mult))
                V.tensor_tensor(x1[:, t, :], x1[:, t, :], gated, ALU.add).then_inc(s["v_x1"], 1)
                dve.wait_ge(s["v_x1"], t + 1)
            dve.wait_ge(s["a_sd"], 5)
            link(V.reciprocal(st[:, 132:136], st[:, 132:136]))
            for t in range(NT):
                V.tensor_scalar(rows[:, t, :], x1[:, t, :], st[:, 132 + t:133 + t], None, ALU.mult).then_inc(s["v_h2"], 1)
            dve.wait_ge(s["m_lg"], 1)
            link(V.tensor_tensor(lg, ps[:, 2, 0:NT * NE].rearrange("p (t e) -> p t e", t=NT),
                                 rb_sb[:, None, :].to_broadcast([P, NT, NE]), ALU.add))
            for t in range(NT):
                link(V.max(v8[:, t, :], lg[:, t, :]))
                link(V.max_index(i8[:, t, :], v8[:, t, :], lg[:, t, :]))
            link(V.tensor_copy(i8f, i8))
            V.tensor_tensor(gk, v8[:, :, 0:TOPK], v8[:, :, 0:1].to_broadcast([P, NT, TOPK]), ALU.subtract).then_inc(s["v_gexp"], 1)
            dve.wait_ge(s["a_gexp"], 1)
            link(V.tensor_reduce(gsum, gk, AX.X, ALU.add))
            link(V.reciprocal(gsum, gsum))
            link(V.tensor_tensor(gk, gk, gsum[:, :, None].to_broadcast([P, NT, TOPK]), ALU.mult))
            iota_e = cst[:, None, C_IOE:C_IOE + NE].to_broadcast([P, NT, NE])
            asg = cst[:, C_ASG:C_ASG + NT * TOPK].rearrange("p (t k) -> p t k", t=NT)
            tab_r, tab_g = vtab[:, :, :, 0], vtab[:, :, :, 2]
            for k in range(TOPK):
                link(V.tensor_tensor(eqk, iota_e, i8f[:, :, k:k + 1].to_broadcast([P, NT, NE]), ALU.is_equal))
                if k == 0:
                    link(V.tensor_copy(memb, eqk))
                    link(V.tensor_tensor(tab_r, eqk, asg[:, :, k:k + 1].to_broadcast([P, NT, NE]), ALU.mult))
                    link(V.tensor_tensor(tab_g, eqk, gk[:, :, k:k + 1].to_broadcast([P, NT, NE]), ALU.mult))
                else:
                    link(V.tensor_tensor(memb, memb, eqk, ALU.add))
                    link(V.tensor_tensor(tmpk, eqk, asg[:, :, k:k + 1].to_broadcast([P, NT, NE]), ALU.mult))
                    link(V.tensor_tensor(tab_r, tab_r, tmpk, ALU.add))
                    link(V.tensor_tensor(tmpk, eqk, gk[:, :, k:k + 1].to_broadcast([P, NT, NE]), ALU.mult))
                    link(V.tensor_tensor(tab_g, tab_g, tmpk, ALU.add))
            V.memset(st[:, 159:160], 0.0).then_inc(s["v_memb"], 1)
            link(V.scalar_tensor_tensor(tab_r, memb, -float(EMPTY), tab_r, ALU.mult, ALU.add))
            link(V.tensor_tensor(vtab[:, :, :, 1], memb, cst[:, C_TOK:C_TOK + NT, None].to_broadcast([P, NT, NE]), ALU.mult))
            link(V.memset(vtab[:, :, :, 3], 0.0))
            dve.wait_ge(s["m_rank"], 1)
            link(V.tensor_copy(cnt, ps[:, 3, 128:160]))
            link(V.tensor_scalar(nblk, cnt, 0.0, None, ALU.is_gt))
            for b in range(1, S // P):
                link(V.scalar_tensor_tensor(nblk, cnt, float(P * b), nblk, ALU.is_gt, ALU.add))
            link(V.tensor_tensor_scan(bend, cst[:, C_ONES:C_ONES + NE], nblk, 0.0, ALU.mult, ALU.add))
            link(V.tensor_copy(bendi[:, 0:NE], bend))
            link(V.tensor_scalar(bendi[:, NE:NE + 1], bend[:, NE - 1:NE], 1.0, None, ALU.subtract))
            link(V.tensor_tensor(bstart, bend, nblk, ALU.subtract))
            link(V.tensor_scalar(bstart, bstart, float(P), 1.0, ALU.mult, ALU.add))
            link(V.tensor_tensor(pos, ps[:, 3, 0:NT * NE].rearrange("p (t e) -> p t e", t=NT),
                                 bstart[:, None, :].to_broadcast([P, NT, NE]), ALU.add))
            link(V.tensor_tensor(pos, pos, memb, ALU.mult))
            dve.wait_ge(s["g_bf"], 6)
            link(V.tensor_tensor(cmp_be, bend[:, None, :].to_broadcast([P, MAXBLK, NE]),
                                 cst[:, C_IOB:C_IOB + MAXBLK, None].to_broadcast([P, MAXBLK, NE]), ALU.is_le))
            link(V.tensor_reduce(egf[:], cmp_be, AX.X, ALU.add))
            link(V.tensor_scalar(egf[:], egf[:], float(NE - 1), None, ALU.min))
            link(V.tensor_copy(egi[:], egf[:]))
            link(V.tensor_copy(slot_no, cst[:, C_SLOT:C_SLOT + P]))
            V.memset(st[:, 158:159], 0.0).then_inc(s["v_tables"], 1)

            last_b = dve.value_load(bendi[0:1, NE:NE + 1], min_val=0, max_val=MAXBLK - 2)

            def one_hot(g):
                e = dve.value_load(egi[0:1, bass.ds(g, 1)], min_val=0, max_val=NE - 1)
                dve.wait_ge(b_tab, g)
                for t in range(NT):
                    last = V.tensor_scalar(hot[:, t, :], slot_no, pos[:, t, bass.ds(e, 1)], None, ALU.is_equal)
                last.then_inc(b_hot, 1)
                dve.wait_ge(b_hot, g + 1)
                V.tensor_scalar(slot_no, slot_no, float(P), None, ALU.add).then_inc(b_chain, 1)
                dve.wait_ge(b_chain, g + 1)

            def table(g):
                dve.wait_ge(b_tab, g + 1)
                V.tensor_scalar(idx_out[:, bass.ds(g, 1)], ps[:, 6, 0:1], float(EMPTY), None, ALU.add)
                V.tensor_copy(idx_tok[:, bass.ds(g, 1)], ps[:, 6, 1:2])
                V.tensor_copy(gcol[:, bass.ds(g, 1)], ps[:, 6, 2:3]).then_inc(b_idx, 1)

            def select(dst, g, signal):
                V.tensor_tensor(dst[0:96, :], cst[0:96, C_PM:C_PM + 1].to_broadcast([96, P]),
                                egf[0:96, bass.ds(g, 1)].to_broadcast([96, P]), ALU.is_equal).then_inc(signal, 1)

            def swiglu(g, first=False):
                dve.wait_ge(w1_used, g * KC + 2 * KC)
                if not first:
                    dve.wait_ge(b_aps, g)
                for j in range(2):
                    sl = slice(512 * j, 512 * j + 512)
                    V.tensor_scalar(a_g[:, sl], ps[:, j, :], LIM, None, ALU.min).then_inc(b_min, 1)
                V.tensor_scalar(a_l.rearrange("p (b n) -> p b n", b=2), ps[:, 2:4, :], LIM, -LIM, ALU.min, ALU.max).then_inc(b_hread, 1)
                dve.wait_ge(b_hread, g + 1)
                dve.wait_ge(b_min, g * 2 + 2)
                dve.wait_ge(b_sig, g * 2 + 1)
                for j in range(2):
                    sl = slice(512 * j, 512 * j + 512)
                    V.scalar_tensor_tensor(a_l[:, sl], a_l[:, sl], 1.0, a_g[:, sl], ALU.add, ALU.mult).then_inc(b_lin, 1)
                for j in range(2):
                    sl = slice(512 * j, 512 * j + 512)
                    dve.wait_ge(b_sig, g * 2 + (j + 1))
                    dve.wait_ge(b_lin, g * 2 + (j + 1))
                    V.tensor_tensor(a_l[:, sl], a_l[:, sl], a_s[:, sl], ALU.mult).then_inc(b_act, 1)

            one_hot(0)
            table(0)
            select(selA, 0, b_selA)
            one_hot(1)
            table(1)
            swiglu(0, first=True)
            dve.wait_ge(w1_used, 2 * KC)
            select(selA, 1, b_selA)
            select(selB, 0, b_selB)
            with dve.Fori(1, last_b + 1) as g:
                one_hot(g + 1)
                table(g + 1)
                swiglu(g)
                dve.wait_ge(w1_used, g * KC + 2 * KC)
                select(selA, g + 1, b_selA)
                dve.wait_ge(w2_used, g * 4 + 4)
                select(selB, g, b_selB)
            for t in range(NT):
                dve.wait_ge(l_fin[t], 16)
                y4 = w1_slots[:, 2 * t:2 * t + 2, :].rearrange("p a (b n) -> p a b n", b=2)
                link(V.tensor_tensor(y4[:, 0, :, :], y4[:, 0, :, :], y4[:, 1, :, :], ALU.add))
                link(V.tensor_tensor(y4[:, 0, 0, :], y4[:, 0, 0, :], y4[:, 0, 1, :], ALU.add))
                link(V.tensor_tensor(y4[:, 0, 0, :], y4[:, 0, 0, :], gate2, ALU.mult))
                V.tensor_tensor(x1[:, t, :], x1[:, t, :], y4[:, 0, 0, :], ALU.add).then_inc(f_sum, 1)
            dve.wait_ge(l_x1, 64)
            for t in range(NT):
                dve.wait_ge(f_sd, t + 1)
                link(V.reciprocal(st[:, 8 + t:9 + t], st[:, 4 + t:5 + t]))
                V.scalar_tensor_tensor(x1[:, t, :], x1[:, t, :], st[:, 8 + t:9 + t], fin_g, ALU.mult, ALU.mult).then_inc(f_o, 1)

        @block.tensor
        def _(pe):
            T = nc.tensor

            def turn(bank, k, src, ev, done):
                for t in range(NT):
                    last = T.transpose(ps[:, bank, part(t)], src[:, t, P * k:P * k + P], ident)
                last.then_inc(done, 1)

            pe.wait_ge(l_cst, 16)
            pe.wait_ge(l_par, 16 * N_PAR)
            T.transpose(ps[:, 0, 0:R_N], parms[0:R_N, :], ident[0:R_N, 0:R_N]).then_inc(s["t_par"], 1)
            T.transpose(ps[:, 0, R_N:R_N + 2 * TAPS], taps_r, ident[0:2 * TAPS, 0:2 * TAPS]).then_inc(s["t_par"], 1)
            T.transpose(ps[:, 0, 256:256 + NH], sgub_r, ident[0:NH, 0:NH]).then_inc(s["t_par"], 1)
            T.matmul(ps[0:NH, 6, :], relb[:], buckets[:, 0:512], start=True, stop=True)
            T.matmul(ps[0:NH, 7, 0:NDIST - 512], relb[:], buckets[:, 512:NDIST], start=True, stop=True).then_inc(s["t_bias"], 1)
            for h in range(NH):
                last = T.transpose(ps[:, 1, part(h)], sguw_r[:, h, :], ident)
            last.then_inc(s["t_wmix"], 1)

            def column_sums(bank, acc, done):
                for j in range(16):
                    last = T.matmul(ps[:, bank, j:j + 1], acc[:, P * j:P * j + P], ones[:, 0:1], start=True, stop=True)
                last.then_inc(done, 1)

            pe.wait_ge(s["v_mod0"], KC)
            column_sums(2, acc0, s["m_mod0"])
            pe.wait_ge(s["v_xn"], NT)
            for k in range(KC):
                if k == 0:
                    pe.wait_ge(s["c_par"], 1)
                if k == 1:
                    pe.wait_ge(s["c_wmix"], 1)
                if k >= 2:
                    pe.wait_ge(s["a_hT"], k - 1)
                turn(k % 2, k, rows, None, s["t_hT"])
            for i, (kind, n, wc) in enumerate(PROJ):
                if i == 0:
                    pe.wait_ge(s["c_mod"], 1)
                j = i - 4
                if j in (1, 3):
                    pe.wait_ge(s["e_glu"], j // 2 + 1)
                elif j in (0, 2):
                    pe.wait_ge(s["e_act"], j // 2 + 1)
                elif j >= 4:
                    pe.wait_ge(s["e_act"], j - 1)
                bank = ps[:, 2 + i % 4, :]
                for k in range(KC):
                    if i == 0:
                        pe.wait_ge(s["a_hT"], k + 1)
                        pe.wait_ge(l_w1[k], 32)
                    if kind == "v":
                        last = T.matmul(bank[:, 0:GW], colsT[:, k, part(n)], w1_slots[:, k, 1024:1280],
                                        start=(k == 0), stop=(k == KC - 1))
                    elif kind == "s":
                        last = T.matmul(bank, colsT[:, k, part(n)], w1_slots[:, k, 1536:2048],
                                        start=(k == 0), stop=(k == KC - 1))
                    else:
                        last = T.matmul(bank, w1_slots[:, k, P * wc:P * wc + P], colsT[:, k, :],
                                        start=(k == 0), stop=(k == KC - 1))
                last.then_inc(s["p_proj"], 1)
                if i == 12:
                    pe.wait_ge(s["g_added"], KC)
                    column_sums(0, acc12, s["m_modA"])
            pe.wait_ge(s["v_conv"], 2 * TAPS)
            pe.wait_ge(s["c_bias"], 1)
            for t in range(NT):
                for c in range(2):
                    last = T.transpose(ps[:, 6 + t // 2, GW * (t % 2) + P * c:GW * (t % 2) + P * c + P],
                                       pT[:, c, part(t)], ident)
            last.then_inc(s["t_conv"], 1)
            pe.wait_ge(s["v_poolT"], 1)
            pe.wait_ge(l_pw, 64)
            pe.wait_ge(s["e_act"], 14)
            for t in range(NT):
                for c in range(2):
                    last = T.matmul(ps[:, 4 + t // 2, GW * (t % 2) + P * c:GW * (t % 2) + P * c + P],
                                    pT[:, 8 + c, part(t)], poolw[:, c, :], start=True, stop=True)
            last.then_inc(s["m_pool"], 1)

            def att_scores(i):
                h, q = ATT[i]
                hp = slice(HD * (h % 2), HD * (h % 2) + HD)
                if i == 0:
                    pe.wait_ge(s["v_sgu"], 1)
                if i >= 2:
                    pe.wait_ge(s["v_att"], i - 1)
                T.matmul(ps[:, 6 + h % 2, 0:P * (q + 1)], pT[hp, 4 + h // 2, part(q)], pT[hp, 6 + h // 2, 0:P * (q + 1)],
                         start=True, stop=True).then_inc(s["s_att"], 1)

            def att_turn(i):
                h, q = ATT[i]
                pe.wait_ge(s["a_att"], i + 1)
                if i == 0:
                    pe.wait_ge(s["c_mod12"], 1)
                if i >= 2:
                    pe.wait_ge(s["a_attT"], i - 1)
                for j in range(q + 1):
                    last = T.transpose(ps[:, i % 2, part(j)], prob[:, i % 2, part(j)], ident)
                last.then_inc(s["t_att"], 1)

            def att_out(i):
                h, q = ATT[i]
                pe.wait_ge(s["a_attT"], i + 1)
                if i >= 2:
                    pe.wait_ge(s["v_attO"], i - 1)
                for j in range(q + 1):
                    last = T.matmul(ps[:, 2 + i % 2, 0:HD], probT[:, i % 2, part(j)], pR[:, j, HD * h:HD * h + HD],
                                    start=(j == 0), stop=(j == q))
                last.then_inc(s["o_att"], 1)

            for i in range(NA + 2):
                if i < NA:
                    att_scores(i)
                if i == 1:
                    pe.wait_ge(s["v_convE"], 1)
                    for t in range(NT):
                        for h in range(NH):
                            last = T.matmul(ps[:, 4 + t // 2, GW * (t % 2) + HD * h:GW * (t % 2) + HD * h + HD], wmixT[:, h, :],
                                            pR[:, t, 2 * GW + HD * h:2 * GW + HD * h + HD], start=True, stop=True)
                    last.then_inc(s["m_sgu"], 1)
                if 1 <= i <= NA:
                    att_turn(i - 1)
                if i >= 2:
                    att_out(i - 2)
            pe.wait_ge(s["g_added"], 2 * KC)
            pe.wait_ge(s["v_sguE"], 8)
            pe.wait_ge(s["v_att"], NA)
            for j in range(4):
                last = T.matmul(ps[:, 4 + j, :], ones, acc12[:, 512 * j:512 * j + 512], start=True, stop=True)
            last.then_inc(s["m_mod"], 1)
            pe.wait_ge(s["v_mixed"], NT)
            for k in range(KC):
                if k >= 2:
                    pe.wait_ge(s["a_mixT"], k - 1)
                turn(k % 2, k, rows, None, s["t_mixT"])
            pe.wait_ge(s["a_mixT"], KC)
            pe.wait_ge(s["c_mod12"], 3)
            pe.wait_ge(s["v_attO"], NA)
            for c in range(4):
                pe.wait_ge(l_w2[c], 112)
            for t in range(NT):
                if t >= 2:
                    pe.wait_ge(s["v_x1"], t - 1)
                for n in range(2):
                    for k in range(KC):
                        last = T.matmul(ps[:, 2 + 2 * (t % 2) + n, :], colsT[:, k, part(t)],
                                        w2_slots[:, k // 2, 1024 * (k % 2) + 512 * n:1024 * (k % 2) + 512 * n + 512],
                                        start=(k == 0), stop=(k == KC - 1))
                    last.then_inc(s["m_out"], 1)
            pe.wait_ge(s["v_h2"], NT)
            for k in range(KC):
                if k >= 2:
                    pe.wait_ge(s["a_h2T"], k - 1)
                turn(k % 2, k, rows, None, s["t_h2T"])
            pe.wait_ge(s["a_h2T"], KC)
            pe.wait_ge(l_row, 16 * 7)
            pe.wait_ge(s["v_x1"], NT)
            for t in range(NT):
                for k in range(KC):
                    last = T.matmul(ps[:, 2, NE * t:NE * t + NE], colsT[:, k, part(t)], rw_sb[:, k, :],
                                    start=(k == 0), stop=(k == KC - 1))
            last.then_inc(s["m_lg"], 1)
            pe.wait_ge(s["v_memb"], 1)
            strict = cst[:, C_STRICT:C_STRICT + P]
            for t in range(NT):
                for j in range(t + 1):
                    T.matmul(ps[:, 3, NE * t:NE * t + NE], strict if j == t else ones, memb[:, j, :],
                             start=(j == 0), stop=(j == t))
            for t in range(NT):
                last = T.matmul(ps[:, 3, 128:128 + NE], ones, memb[:, t, :], start=(t == 0), stop=(t == NT - 1))
            last.then_inc(s["m_rank"], 1)

            pe.nop().then_inc(w1_used, KC)
            pe.nop().then_inc(w2_used, 4)
            pe.nop().then_inc(b_yev, 1)
            pe.wait_ge(s["v_tables"], 1)
            last_b = pe.value_load(bendi[0:1, NE:NE + 1], min_val=0, max_val=MAXBLK - 2)

            def expert(g):
                return pe.value_load(egi[0:1, bass.ds(g, 1)], min_val=0, max_val=NE - 1)

            def table(g):
                e = expert(g)
                pe.wait_ge(b_hot, g + 1)
                pe.wait_ge(b_xT, g)
                for t in range(NT):
                    last = T.matmul(ps[:, 6, 0:4], hot[:, t, :], vtab[:, t, bass.ds(e, 1), :].rearrange("p e c -> p (e c)"),
                                    start=(t == 0), stop=(t == NT - 1))
                last.then_inc(b_tab, 1)

            def turn_rows(g, first=False):
                pe.wait_ge(b_gat, g * 16 + 16)
                pe.wait_ge(b_idx, g + 1)
                if not first:
                    pe.wait_ge(b_aT, g - 1)
                for k in range(KC):
                    last = T.transpose(ps[:, 6 + k // 4, part(k % 4)], xg[:, P * k:P * k + P], ident)
                last.then_inc(b_xps, 1)

            def turn_act(g):
                pe.wait_ge(b_act, g * 2 + 2)
                for i in range(KC):
                    last = T.transpose(ps[:, 6 + i // 4, part(i % 4)],
                                       a_l.rearrange("p (c q j) -> p c j q", c=4, j=2)[:, i // 2, i % 2, :], ident)
                last.then_inc(b_aps, 1)

            def up(g, e, first=False):
                pe.wait_ge(b_selA, g + 1)
                pe.wait_ge(b_xT, g + 1)
                if not first:
                    pe.wait_ge(b_hread, g)
                for n in range(4):
                    T.matmul(ps[:, n, :], selA[0:96, :], b_bf[:, 512 * n:512 * n + 512], start=True, stop=False)
                for k in range(KC):
                    pe.wait_ge(l_w1[k], e * 16 + 48)
                    for n in range(4):
                        last = T.matmul(ps[:, n, :], xT[:, k, :], w1_slots[:, k, 512 * n:512 * n + 512],
                                        start=False, stop=(k == KC - 1))
                    last.then_inc(w1_used, 1)
                    if k == 1:
                        table(g + 1)
                    if k == 4 and not first:
                        pe.wait_ge(b_idx, g + 2)
                        turn_act(g - 1)

            def down(g, e, first=False):
                pe.wait_ge(b_selB, g + 1)
                pe.wait_ge(b_aT, g + 1)
                if not first:
                    pe.wait_ge(b_yev, g + 1)
                for n in range(2):
                    T.matmul(ps[:, 4 + n, :], selB[0:96, :], b_bf[:, 2048 + 512 * n:2560 + 512 * n], start=True, stop=False)
                for c in range(4):
                    pe.wait_ge(l_w2[c], e * 16 + 128)
                    for j in range(2):
                        for n in range(2):
                            last = T.matmul(ps[:, 4 + n, :], aT[:, 2 * c + j, :],
                                            w2_slots[:, c, 1024 * j + 512 * n:1024 * j + 512 * n + 512],
                                            start=False, stop=(c == 3 and j == 1))
                    last.then_inc(w2_used, 1)

            pe.wait_ge(s["g_bf"], 6)
            table(0)
            turn_rows(0, first=True)
            up(0, expert(0), first=True)
            turn_rows(1, first=True)
            with pe.Fori(1, last_b + 1) as g:
                up(g, expert(g))
                turn_rows(g + 1)
                down(g - 1, expert(g - 1))
            pe.wait_ge(b_xT, last_b + 2)
            turn_act(last_b)
            down(last_b, expert(last_b))


_OUTS = [((1, S, D), "float32")]
_INS = ["x", "c", "w_mod", "b_mod", "norm1_g", "w_in", "conv_w", "conv_b", "conv_norm_g", "conv_norm_b", "rel_bias", "pool_w",
        "pool_scale", "sgu_norm_g", "sgu_norm_b", "sgu_w", "sgu_b", "mix_out_g", "w_out", "norm2_g", "router_w", "router_b",
        "exp_w1", "exp_b1", "exp_w2", "exp_b2", "final_norm_g"]


def kernel(**inputs):
    import concourse.bacc as bacc
    from concourse.bass_utils import run_bass_kernel_spmd

    nc = bacc.Bacc("TRN2", target_bir_lowering=False, num_devices=1)
    arrays, args = {}, {}
    for name in _INS:
        v = np.ascontiguousarray(inputs[name])
        arrays[f"in_{name}"] = v
        args[name] = nc.dram_tensor(f"in_{name}", v.shape, mybir.dt.from_np(v.dtype), kind="ExternalInput").ap()
    extra = []
    for name, v in (("consts", constants()), ("buckets", distance_buckets())):
        arrays[f"in_{name}"] = v
        extra.append(nc.dram_tensor(f"in_{name}", v.shape, F32, kind="ExternalInput").ap())
    out = nc.dram_tensor("out_0", _OUTS[0][0], F32, kind="ExternalOutput").ap()
    build(nc, args, extra[0], extra[1], out)
    r = run_bass_kernel_spmd(nc, [arrays], core_ids=[0])
    return r.results[0]["out_0"]
```

```python
import math
from contextlib import ExitStack

import numpy as np
import concourse.bass as bass
from concourse import mybir

ALU = mybir.AluOpType
ACT = mybir.ActivationFunctionType
AX = mybir.AxisListType
F32 = mybir.dt.float32
F32R = mybir.dt.float32r
BF16 = mybir.dt.bfloat16
U32 = mybir.dt.uint32

P = 128
D, S = 1024, 512
NT = S // P
KC = D // P
GW, NH, HD = 256, 4, 64
TAPS = 31
PADT = TAPS - 1
NE, TOPK, DFF = 32, 4, 1024
LIM, ALPHA, EPS = 7.0, 1.702, 1e-6
MAXBLK = NE + S * TOPK // P
EMPTY = 4096
NBUCK, MAXDIST = 32, 128
NDIST = S + P
NEG = -1.0e30

C_ID, C_TRI, C_STRICT, C_ONES, C_SLOT = 0, 128, 256, 384, 512
C_PM = 640
C_IOB = 641
C_IOE = C_IOB + MAXBLK
C_TOK = C_IOE + NE
C_ASG = C_TOK + NT
C_RW = C_ASG + NT * TOPK
C_RC = C_RW + 2
C_EPS = C_RC + 32
C_N = C_EPS + 1

R_C, R_N1, R_N2, R_MIX, R_BMOD, R_CB, R_N = 0, 8, 16, 24, 32, 80, 82


def constants():
    c = np.zeros((P, C_N), np.float32)
    p = np.arange(P)
    c[:, C_ID:C_ID + P] = np.eye(P)
    c[:, C_TRI:C_TRI + P] = p[:, None] <= p[None, :]
    c[:, C_STRICT:C_STRICT + P] = p[:, None] < p[None, :]
    c[:, C_ONES:C_ONES + P] = 1.0
    c[:, C_SLOT:C_SLOT + P] = p[None, :] + 1
    c[:, C_PM] = p % NE
    c[:, C_IOB:C_IOB + MAXBLK] = np.arange(MAXBLK)
    c[:, C_IOE:C_IOE + NE] = np.arange(NE)
    tok = p[:, None] + P * np.arange(NT)[None, :]
    c[:, C_TOK:C_TOK + NT] = tok
    c[:, C_ASG:C_ASG + NT * TOPK] = (tok[:, :, None] * TOPK + np.arange(TOPK)).reshape(P, -1)
    for ch in range(2):
        w = 2 ** (1 + 2 * ch + p // 64)
        c[:, C_RW + ch] = 1.0 / w
        c[:, C_RC + 16 * ch:C_RC + 16 * ch + 16] = 1.0 / np.minimum(np.arange(1, 17)[None, :], w[:, None])
    c[:, C_EPS] = EPS
    return c


def distance_buckets():
    dist = (S - 1) - np.arange(NDIST)
    n = np.maximum(dist, 0)
    exact = NBUCK // 2
    large = exact + (np.log(np.maximum(n, 1).astype(np.float32) / np.float32(exact)) / np.float32(math.log(MAXDIST / exact))
                     * (NBUCK - exact)).astype(np.int32)
    b = np.where(n < exact, n, np.minimum(large, NBUCK - 1))
    out = np.zeros((NBUCK + 1, NDIST), np.float32)
    out[:NBUCK] = (b[None, :] == np.arange(NBUCK)[:, None]) & (dist >= 0)[None, :]
    out[NBUCK:] = np.where(dist < 0, NEG, 0.0)
    return out


def build(nc, a, consts_d, buckets_d, out_d):
    with ExitStack() as ctx:
        def sb(name, shape, dt=F32):
            return ctx.enter_context(nc.sbuf_tensor(name, shape, dt))

        def sem(name):
            return ctx.enter_context(nc.semaphore(name))

        hl_at = (nc.sbuf_base + 31) // 32 * 32
        rows = sb("rows", [P, NT, D])
        colsT = sb("colsT", [P, KC, S])
        arena = sb("arena", [P, 16384])
        arena_at = hl_at + 32 * 1024
        w1_slots = sb("w1_slots", [P, KC, 2 * DFF])
        w2_slots = sb("w2_slots", [P, 4, 2048])
        cst = sb("cst", [P, C_N])
        parms, taps_r, sgub_r = colsT[:, 0, 0:P], colsT[0:2 * TAPS, 1, 0:P], colsT[0:NH, 2, 0:P]
        buckets = colsT[0:NBUCK + 1, 3:5, :].rearrange("p a s -> p (a s)")[:, 0:NDIST]
        sguw_r = colsT[:, 5, :].rearrange("p (h j) -> p h j", h=NH)
        pc = sb("pc", [P, R_N + 2 * TAPS])
        taps = pc[:, R_N:R_N + 2 * TAPS]
        cond = sb("cond", [P, KC])
        mod = sb("mod", [P, 48])
        gs1 = sb("gs1", [P, KC])
        gs2 = sb("gs2", [P, KC])
        st = sb("st", [P, 160])
        lrows = sb("lrows", [P, 5, GW])
        sgub = sb("sgub", [P, NH])
        relb = sb("relb", [NBUCK + 1, NH])
        rw_sb = sb("rw_sb", [P, KC, NE])
        rb_sb = sb("rb_sb", [P, NE])

        def view(kb, n):
            return arena[:, kb * 256:kb * 256 + n]

        x_sb = view(0, NT * D).rearrange("p (t c) -> p t c", t=NT)
        bias_t = view(0, NH * S).rearrange("p (h m) -> p h m", h=NH)
        prob = view(8, 2 * S).rearrange("p (b m) -> p b m", b=2)
        probT = view(12, 2 * S).rearrange("p (b m) -> p b m", b=2)
        pT = view(16, 10 * S).rearrange("p (j s) -> p j s", j=10)
        pR = view(36, NT * 768).rearrange("p (t c) -> p t c", t=NT)
        acc0 = view(48, 2048)
        ypad = view(48, 2 * (PADT + S)).rearrange("p (c s) -> p c s", c=2)
        acc12 = view(56, 2048)
        wmixT = view(53, NH * P).rearrange("p (h i) -> p h i", h=NH)
        poolw = view(55, 2 * P).rearrange("p (c d) -> p c d", c=2)
        gate2 = view(56, D)
        bias_row = view(40, NDIST)[0:NH, :]
        dense = pT[:, 2:4, :].rearrange("p c s -> p (c s)")
        sqv = pT[:, 0:2, :].rearrange("p c s -> p (c s)")
        b_f32 = view(0, 3072)
        gate2 = view(12, D)
        x1 = view(18, NT * D).rearrange("p (t c) -> p t c", t=NT)
        g2row = view(34, D)
        gated = view(46, D)
        gate1 = view(50, D)
        sq_dump = view(54, GW)
        b_bf = view(57, 1536).bitcast(BF16)[0:96, :]
        HI, LO = 0, 1
        NRING = 3
        w_ring = nc.alloc_sbuf_tensor_at("w_ring", [P, NRING, 2, 2048], F32R, offset=hl_at)
        a_g, a_s, a_l = (view(16 + 4 * i, DFF) for i in range(3))
        aT = nc.alloc_sbuf_tensor_at("aT", [P, 2, KC, P], F32R, offset=arena_at + 28 * 1024)
        xT = nc.alloc_sbuf_tensor_at("xT", [P, 2, KC, P], F32R, offset=arena_at + 36 * 1024)
        xg = view(44, D)
        y_sb = view(48, D)
        hot = view(52, NT * P).rearrange("p (t s) -> p t s", t=NT)
        selA = view(54, P // 2).bitcast(BF16)
        selB = arena[:, 54 * 256 + P // 2:54 * 256 + P].bitcast(BF16)
        fin_x1 = w2_slots[:, :, 0:D]
        fin_gate2 = w2_slots[:, 0, D:2 * D]
        fin_g = w2_slots[:, 1, D:2 * D]
        fin_sq = w2_slots[:, 2, D:2 * D]
        routing = view(50, 1024)

        lg = routing[:, 0:NT * NE].rearrange("p (t e) -> p t e", t=NT)
        memb = routing[:, 128:256].rearrange("p (t e) -> p t e", t=NT)
        pos = view(63, 128).rearrange("p (t e) -> p t e", t=NT)
        eqk = routing[:, 384:512].rearrange("p (t e) -> p t e", t=NT)
        tmpk = routing[:, 512:640].rearrange("p (t e) -> p t e", t=NT)
        v8 = routing[:, 640:672].rearrange("p (t k) -> p t k", t=NT)
        i8 = routing[:, 672:704].bitcast(U32).rearrange("p (t k) -> p t k", t=NT)
        i8f = routing[:, 704:736].rearrange("p (t k) -> p t k", t=NT)
        gk = routing[:, 736:752].rearrange("p (t k) -> p t k", t=NT)
        gsum = routing[:, 752:756]
        cnt = routing[:, 768:800]
        nblk = routing[:, 800:832]
        bend = routing[:, 832:864]
        bstart = routing[:, 864:896]
        slot_no = arena[:, 63 * 256 + 128:64 * 256]
        vtab = view(55, NT * NE * 4).rearrange("p (t e c) -> p t e c", t=NT, c=4)
        egf = sb("egf", [P, MAXBLK])
        egi = sb("egi", [P, MAXBLK], U32)
        bendi = sb("bendi", [P, NE + 2], U32)
        idx_out = sb("idx_out", [P, MAXBLK], U32)
        idx_tok = sb("idx_tok", [P, MAXBLK], U32)
        gcol = sb("gcol", [P, MAXBLK])
        cur_out = sb("cur_out", [P, 1], U32)
        cur_tok = sb("cur_tok", [P, 1], U32)
        cmp_be = view(0, MAXBLK * NE).rearrange("p (b e) -> p b e", b=MAXBLK)

        ps = ctx.enter_context(nc.psum_tensor("ps", [P, 8, 512], F32))

        bias_d = nc.dram_tensor("bias_scratch", [NH, NDIST], F32).ap()
        skew_d = nc.dram_tensor("skew_scratch", [NH, P, NDIST], F32).ap()
        h2_d = nc.dram_tensor("h2_scratch", [S, D], F32).ap()
        x1_d = nc.dram_tensor("x1_scratch", [S, D], F32).ap()
        g2_d = nc.dram_tensor("gate2_scratch", [1, D], F32).ap()
        ys_d = nc.dram_tensor("ys_scratch", [S * TOPK, D], F32).ap()

        ident = cst[:, C_ID:C_ID + P]
        ones = cst[:, C_ONES:C_ONES + P]
        eps = cst[:, C_EPS:C_EPS + 1]

        def col(r):
            return pc[:, r:r + 1]

        l_cst, l_par, l_x, l_row, l_sgu = (sem("l_" + n) for n in ("cst", "par", "x", "row", "sgu"))
        l_w1 = [sem(f"l_w1_{k}") for k in range(KC)]
        l_w2 = [sem(f"l_w2_{c}") for c in range(4)]
        l_bt, l_x1, l_be, l_pw = (sem("l_" + n) for n in ("bt", "x1", "be", "pw"))
        l_fin = [sem(f"l_fin_{t}") for t in range(NT)]
        st_bias, st_h2, st_out = (sem("st_" + n) for n in ("bias", "h2", "out"))
        names = """e_act e_glu m_modA t_par c_par c_cond v_ss a_ss v_var a_sd v_xn t_bias c_bias v_mod0 m_mod0 c_mod t_hT a_hT
                   p_proj e_proj w1_free a_scaled g_added g_acc m_mod c_mod12 t_wmix c_wmix g_pw v_conv t_conv
                   v_convE v_poolT m_pool v_sgu m_sgu v_sguE s_att v_att a_att t_att a_attT o_att v_attO
                   v_cx a_silu v_mixed t_mixT a_mixT m_out v_x1 v_h2 t_h2T a_h2T m_lg v_gexp a_gexp v_memb m_rank
                   v_tables g_bf v_chain t_rows2 credit""".split()
        s = {n: sem(n) for n in names}
        h_w1, h_w2, d_w1, d_w2, p_w1, p_w2 = (sem(n) for n in ("h_w1", "h_w2", "d_w1", "d_w2", "p_w1", "p_w2"))
        q_w1, q_w2 = sem("q_w1"), sem("q_w2")
        st_x1, st_g2 = sem("st_x1"), sem("st_g2")
        (b_hot, b_tab, b_idx, b_gat, b_xps, b_xH, b_xL, b_min, b_sig, b_hread, b_act, b_aps, b_aH, b_aL, b_yev, b_sca,
         b_selA, b_selB, b_chain, b_cur, b_curs, b_lin, b_issued) = (sem("b_" + n) for n in (
             "hot", "tab", "idx", "gat", "xps", "xH", "xL", "min", "sig", "hread", "act", "aps", "aH", "aL", "yev",
             "sca", "selA", "selB", "chain", "cur", "curs", "lin", "issued"))
        f_ld, f_sum, f_sq, f_sd, f_o = (sem("f_" + n) for n in ("ld", "sum", "sq", "sd", "o"))

        x_rows = a["x"].rearrange("b (t p) d -> p (b t) d", p=P)
        wmod_r = a["w_mod"].rearrange("l (k p) (g n) -> (l k) p g n", p=P, g=6)
        win_r = a["w_in"].rearrange("l (k p) n -> (l k) p n", p=P)
        wout_r = a["w_out"].rearrange("l (c j p) n -> (l c) p j n", p=P, j=2)
        w1_r = a["exp_w1"].rearrange("l e (k p) n -> (l e) k p n", p=P)
        w2_r = a["exp_w2"].rearrange("l e (c p j) n -> (l e) c p (j n)", p=P, j=2)
        ys_r = ys_d.rearrange("(t p k) d -> t p (k d)", p=P, k=TOPK)
        out_r = out_d.rearrange("b (t p) d -> (b t) p d", p=P)
        N_PAR = 12

        def part(t):
            return slice(P * t, P * (t + 1))

        PROJ = [("g", 0, 2), ("a", 0, 0), ("g", 1, 3), ("a", 1, 1), ("f", 4, 4), ("f", 5, 5), ("f", 6, 6), ("f", 7, 7)]
        PROJ += [("v", t, None) for t in range(NT)]
        PROJ += [("f", 8, 10), ("f", 9, 11)]
        PROJ += [("s", t, None) for t in range(NT)]
        NPROJ = len(PROJ)
        ATT = [(h, q) for q in range(NT) for h in range(NH)]
        NA = len(ATT)

        def settle(eng):
            eng.wait_ge(s["v_tables"], 1)

        block = ctx.enter_context(nc.Block())

        @block.sync
        def _(sp):
            sp.dma_start(cst[:], consts_d).then_inc(l_cst, 16)
            for r, name in ((R_C, "c"), (R_N1, "norm1_g"), (R_N2, "norm2_g"), (R_MIX, "mix_out_g"), (R_CB, "conv_b")):
                n = a[name].shape[1] // P
                sp.dma_start(parms[r:r + n, :], a[name].rearrange("l (r q) -> (l r) q", q=P)).then_inc(l_par, 16)
            sp.dma_start(parms[R_BMOD:R_BMOD + 48, :], a["b_mod"].rearrange("l (r q) -> (l r) q", q=P)).then_inc(l_par, 16)
            sp.dma_start(taps_r[:], a["conv_w"].rearrange("l t (h q) -> (l t h) q", q=P)).then_inc(l_par, 16)
            sp.dma_start(sgub_r[:], a["sgu_b"].rearrange("l h q -> (l h) q")).then_inc(l_par, 16)
            sp.dma_start(relb[0:NBUCK, :], a["rel_bias"]).then_inc(l_par, 16)
            sp.dma_start(relb[NBUCK:NBUCK + 1, :], consts_d[0:1, C_ONES:C_ONES + NH]).then_inc(l_par, 16)
            sp.dma_start(buckets, buckets_d).then_inc(l_par, 16)
            sp.dma_start(sguw_r, a["sgu_w"].rearrange("l h i j -> i (l h) j")).then_inc(l_par, 16)
            for k in range(KC):
                sp.dma_start(w1_slots[:, k, :].rearrange("p (g n) -> p g n", g=2), wmod_r[k][:, 0:2, :]).then_inc(l_w1[k], 16)
                if k == 1:
                    sp.dma_start(x_sb, x_rows).then_inc(l_x, 16)
            for k in range(KC):
                sp.wait_ge(s["v_mod0"], k + 1)
                sp.dma_start(w1_slots[:, k, :], win_r[k]).then_inc(l_w1[k], 16)
            for i in range(2 * KC):
                if i >= 4:
                    sp.wait_ge(s["g_added"], i - 3)
                dst = w2_slots[:, i % 4, :].rearrange("p (g n) -> p g n", g=2)
                if i < KC:
                    sp.dma_start(dst, wmod_r[i][:, 3:5, :]).then_inc(l_w2[i % 4], 16)
                else:
                    sp.dma_start(dst[:, 0, :], wmod_r[i - KC][:, 2, :]).then_inc(l_w2[i % 4], 16)
                    sp.dma_start(dst[:, 1, :], wmod_r[i - KC][:, 5, :]).then_inc(l_w2[i % 4], 16)
            for c in range(4):
                sp.wait_ge(s["g_added"], 2 * KC - 3 + c)
                sp.dma_start(w2_slots[:, c, :].rearrange("p (j n) -> p j n", j=2), wout_r[c]).then_inc(l_w2[c], 16)
            for k in range(KC):
                sp.wait_ge(s["p_proj"], NPROJ)
                sp.dma_start(w1_slots[:, k, :], w1_r[0, k]).then_inc(l_w1[k], 16)
            for t in range(NT):
                sp.wait_ge(s["v_h2"], t + 1)
                sp.dma_start(h2_d[part(t), :], rows[:, t, :]).then_inc(st_h2, 16)
            for t in range(NT):
                sp.dma_start(x1_d[part(t), :], x1[:, t, :]).then_inc(st_x1, 16)
            sp.dma_start(g2_d, gate2[0:1, :]).then_inc(st_g2, 16)
            for c in range(4):
                sp.wait_ge(s["m_out"], 2 * NT)
                sp.dma_start(w2_slots[:, c, :], w2_r[0, c]).then_inc(l_w2[c], 16)
            sp.wait_ge(s["v_tables"], 1)

            def load_w1(e, ge):
                for k in range(KC):
                    sp.wait_ge(d_w1, ge * KC + (k + 1))
                    settle(sp)
                    sp.wait_ge(p_w1, ge * KC + (k + 1))
                    settle(sp)
                    sp.wait_ge(l_w1[k], 16 * (e + 2))
                    settle(sp)
                    sp.dma_start(w1_slots[:, k, :], w1_r[e, k]).then_inc(l_w1[k], 16)

            def load_w2(e, ge):
                for c in range(4):
                    sp.wait_ge(d_w2, ge * 4 + (c + 1))
                    settle(sp)
                    sp.wait_ge(p_w2, ge * 4 + (c + 1))
                    settle(sp)
                    sp.wait_ge(l_w2[c], 16 * (e + 7))
                    settle(sp)
                    sp.dma_start(w2_slots[:, c, :], w2_r[e, c]).then_inc(l_w2[c], 16)

            ge0 = sp.value_load(bendi[0:1, 0:1], min_val=0, max_val=MAXBLK - 1)
            load_w1(1, ge0)
            with sp.Fori(2, NE) as e:
                ge_w1 = sp.value_load(bendi[0:1, bass.ds(e - 1, 1)], min_val=0, max_val=MAXBLK - 1)
                load_w1(e, ge_w1)
                ge_w2 = sp.value_load(bendi[0:1, bass.ds(e - 2, 1)], min_val=0, max_val=MAXBLK - 1)
                load_w2(e - 1, ge_w2)
            ge_l = sp.value_load(bendi[0:1, NE - 2:NE - 1], min_val=0, max_val=MAXBLK - 1)
            load_w2(NE - 1, ge_l)
            last = sp.value_load(bendi[0:1, NE:NE + 1], min_val=0, max_val=MAXBLK - 2)
            sp.wait_ge(d_w2, last * 4 + 8)
            sp.wait_ge(p_w2, last * 4 + 8)
            for c in range(4):
                sp.wait_ge(l_w2[c], 16 * (NE + 7))
            sp.wait_ge(st_x1, 16 * NT)
            sp.wait_ge(st_g2, 16)
            sp.dma_start(fin_x1, x1_d.rearrange("(t p) d -> p t d", p=P)).then_inc(f_ld, 16)
            sp.dma_start(fin_gate2, g2_d.to_broadcast([P, D])).then_inc(f_ld, 16)
            sp.dma_start(fin_g, a["final_norm_g"].rearrange("(l d) -> l d", l=1).to_broadcast([P, D])).then_inc(f_ld, 16)
            sp.wait_ge(b_sca, last * 16 + 16)
            sp.wait_ge(d_w1, last * KC + 2 * KC)
            sp.wait_ge(p_w1, last * KC + 2 * KC)
            for k in range(KC):
                sp.wait_ge(l_w1[k], 16 * (NE + 2))
            for t in range(NT):
                sp.dma_start(w1_slots[:, 2 * t:2 * t + 2, :], ys_r[t].rearrange("p (a b) -> p a b", a=2)).then_inc(l_fin[t], 16)
            for t in range(NT):
                sp.wait_ge(f_o, t + 1)
                sp.dma_start(out_r[t], fin_x1[:, t, :]).then_inc(st_out, 16)
            sp.wait_ge(st_out, 16 * NT)

        @block.gpsimd
        def _(pool):
            for i, name in enumerate(("conv_norm_g", "conv_norm_b", "pool_scale", "sgu_norm_g", "sgu_norm_b")):
                pool.dma_start(lrows[:, i, :], a[name].to_broadcast([P, GW])).then_inc(l_row, 16)
            pool.dma_start(rb_sb[:], a["router_b"].to_broadcast([P, NE])).then_inc(l_row, 16)
            pool.dma_start(rw_sb[:], a["router_w"].rearrange("l (k p) e -> p (l k) e", p=P)).then_inc(l_row, 16)
            pool.wait_ge(s["c_bias"], 1)
            pool.dma_start(bias_d, bias_row).then_inc(st_bias, 16)
            pool.wait_ge(s["v_xn"], NT)
            pool.wait_ge(st_bias, 16)
            for h in range(NH):
                pool.dma_start(skew_d[h], bias_d[h:h + 1, :].to_broadcast([P, NDIST])).then_inc(st_bias, 16)
            pool.wait_ge(st_bias, 80)
            pool.dma_start(bias_t, bass.AP(tensor=skew_d.tensor, offset=P - 1,
                                           ap=[[NDIST - 1, P], [P * NDIST, NH], [1, S]])).then_inc(l_bt, 16)
            pool.wait_ge(s["m_mod0"], 1)
            nc.gpsimd.memset(poolw, 0.0).then_inc(s["g_pw"], 1)
            pool.wait_ge(s["g_pw"], 1)
            for g in range(4):
                q = slice(64 * (g % 2), 64 * (g % 2) + 64)
                pool.dma_start(poolw[q, g // 2, q], a["pool_w"][0, g]).then_inc(l_pw, 16)
            for i in range(2 * KC):
                pool.wait_ge(s["a_scaled"], i + 1)
                if i == KC:
                    pool.wait_ge(s["m_modA"], 1)
                if i % KC == 0:
                    nc.gpsimd.tensor_copy(acc12, w2_slots[:, i % 4, :]).then_inc(s["g_added"], 1)
                else:
                    pool.wait_ge(s["g_added"], i)
                    nc.gpsimd.tensor_tensor(acc12, acc12, w2_slots[:, i % 4, :], ALU.add).then_inc(s["g_added"], 1)
            pool.wait_ge(s["v_attO"], NA)
            pool.wait_ge(s["v_sguE"], 8)
            pool.dma_start(x1, x_rows).then_inc(l_x1, 16)
            pool.dma_start(gate1, a["b_mod"][:, 2 * D:3 * D].to_broadcast([P, D])).then_inc(l_x1, 16)
            pool.dma_start(g2row, a["b_mod"][:, 5 * D:6 * D].to_broadcast([P, D])).then_inc(l_x1, 16)
            pool.wait_ge(s["m_mod"], 1)
            for j in range(3):
                pool.dma_start(b_f32[32 * j:32 * j + 32, 0:2048], a["exp_b1"][0]).then_inc(l_be, 16)
                pool.dma_start(b_f32[32 * j:32 * j + 32, 2048:3072], a["exp_b2"][0]).then_inc(l_be, 16)
            pool.wait_ge(l_be, 96)
            nc.gpsimd.tensor_copy(b_bf, b_f32[0:96, :]).then_inc(s["g_bf"], 1)
            pool.wait_ge(s["g_bf"], 1)
            nc.gpsimd.tensor_tensor(b_f32[0:96, :], b_f32[0:96, :], b_bf, ALU.subtract).then_inc(s["g_bf"], 1)
            pool.wait_ge(s["g_bf"], 2)
            nc.gpsimd.tensor_copy(b_bf[32:64, :], b_f32[32:64, :]).then_inc(s["g_bf"], 1)
            nc.gpsimd.tensor_copy(b_bf[64:96, :], b_f32[64:96, :]).then_inc(s["g_bf"], 1)
            pool.wait_ge(s["g_bf"], 4)
            nc.gpsimd.tensor_tensor(b_f32[64:96, :], b_f32[64:96, :], b_bf[64:96, :], ALU.subtract).then_inc(s["g_bf"], 1)
            pool.wait_ge(s["g_bf"], 5)
            nc.gpsimd.tensor_copy(b_bf[64:96, :], b_f32[64:96, :]).then_inc(s["g_bf"], 1)

            def gather(g):
                pool.wait_ge(b_idx, g + 1)
                nc.gpsimd.tensor_copy(cur_tok[:], idx_tok[:, bass.ds(g, 1)]).then_inc(b_cur, 1)
                pool.wait_ge(b_cur, g + 1)
                pool.sem_inc(b_issued, 1)
                pool.indirect_dma_start(xg, None, h2_d, bass.IndirectOffsetOnAxis(ap=cur_tok[:], axis=0)).then_inc(b_gat, 16)

            def scatter(g):
                pool.wait_ge(b_yev, g + 2)
                nc.gpsimd.tensor_copy(cur_out[:], idx_out[:, bass.ds(g, 1)]).then_inc(b_curs, 1)
                pool.wait_ge(b_curs, g + 1)
                pool.sem_inc(b_issued, 1)
                pool.indirect_dma_start(ys_d, bass.IndirectOffsetOnAxis(ap=cur_out[:], axis=0), y_sb, None,
                                        bounds_check=S * TOPK - 1, oob_is_err=False).then_inc(b_sca, 16)

            pool.wait_ge(st_h2, 16 * NT)
            pool.wait_ge(s["v_tables"], 1)
            last_b = pool.value_load(bendi[0:1, NE:NE + 1], min_val=0, max_val=MAXBLK - 2)
            prev_b = pool.value_load(bendi[0:1, NE + 1:NE + 2], min_val=0, max_val=MAXBLK - 3)
            Q = slice(1536, 2048)

            def low_w1(g, k, off=0):
                pool.wait_ge(h_w1, g * KC + (k + 1))
                r = (k + off) % NRING
                nc.gpsimd.tensor_tensor(w_ring[:, r, LO, Q], w1_slots[:, k, Q], w_ring[:, r, HI, Q].bitcast(F32),
                                        ALU.subtract).then_inc(p_w1, 1)

            def low_w2(g, c):
                pool.wait_ge(h_w2, g * 4 + (c + 1))
                r = (KC + c) % NRING
                nc.gpsimd.tensor_tensor(w_ring[:, r, LO, Q], w2_slots[:, c, Q], w_ring[:, r, HI, Q].bitcast(F32),
                                        ALU.subtract).then_inc(p_w2, 1)

            def step(g, sca=True, w2=True, off=0):
                for k in range(KC):
                    low_w1(g, k, off)
                    if k == 3 and sca:
                        scatter(g - 2)
                    if k == 5:
                        gather(g + 1)
                if w2:
                    for c in range(4):
                        low_w2(g - 1, c)
                if sca:
                    pool.wait_ge(b_sca, g * 16 - 16)
                pool.wait_ge(b_gat, g * 16 + 32)

            gather(0)
            pool.wait_ge(b_gat, 16)
            pool.wait_ge(b_xps, 1)
            step(0, sca=False, w2=False, off=1)
            step(1, sca=False)
            with pool.Fori(2, last_b + 1) as g:
                step(g)
            scatter(prev_b)
            for c in range(4):
                low_w2(last_b, c)
            pool.wait_ge(b_sca, last_b * 16)
            scatter(last_b)

        @block.scalar
        def _(act):
            act.wait_ge(l_cst, 16)
            act.wait_ge(s["c_par"], 1)
            nc.scalar.activation(cond[:], pc[:, R_C:R_C + KC], ACT.Silu).then_inc(s["c_cond"], 1)
            act.wait_ge(l_x, 16)
            for t in range(NT):
                nc.scalar.activation(rows[:, t, :], x_sb[:, t, :], ACT.Square, accum_out=st[:, t:t + 1]).then_inc(s["a_ss"], 1)

            sq = [0]

            def root(dst, src, n):
                sq[0] += 1
                act.wait_ge(s["v_var"], sq[0])
                nc.scalar.activation(dst, src, ACT.Sqrt, bias=eps, scale=1.0 / n).then_inc(s["a_sd"], 1)


            def own_root(dst, src, n, sums):
                act.wait_ge(s["a_ss"], sums)
                nc.scalar.activation(dst, src, ACT.Sqrt, bias=eps, scale=1.0 / n).then_inc(s["a_sd"], 1)

            own_root(st[:, 4:8], st[:, 0:4], D, NT)
            act.wait_ge(s["c_mod"], 1)
            for k in range(KC):
                act.wait_ge(s["t_hT"], k + 1)
                nc.scalar.activation(colsT[:, k, :], ps[:, k % 2, :], ACT.Identity, bias=mod[:, k:k + 1],
                                     scale=gs1[:, k:k + 1]).then_inc(s["a_hT"], 1)
            for i, (kind, n, _) in enumerate(PROJ):
                bank = ps[:, 2 + i % 4, :]
                if kind != "a":
                    act.wait_ge(s["p_proj"], i + 1)
                if kind == "g":
                    nc.scalar.activation(pT[:, 2 + n, :], bank, ACT.Sigmoid).then_inc(s["e_act"], 1)
                elif kind == "f":
                    nc.scalar.activation(pT[:, n, :], bank, ACT.Copy).then_inc(s["e_act"], 1)
                elif kind == "v":
                    act.wait_ge(st_bias, 16)
                    nc.scalar.activation(pR[:, n, 0:GW], bank[:, 0:GW], ACT.Copy).then_inc(s["e_act"], 1)
                elif kind == "s":
                    nc.scalar.activation(pR[:, n, GW:3 * GW], bank, ACT.Gelu).then_inc(s["e_act"], 1)
                if i >= 2:
                    c = i - 2
                    act.wait_ge(l_w2[c % 4], 16 * (c // 4 + 1) if c < KC else 32 * (c // 4))
                    nc.scalar.activation(w2_slots[:, c % 4, :], w2_slots[:, c % 4, :], ACT.Copy,
                                         scale=cond[:, c % KC:c % KC + 1]).then_inc(s["a_scaled"], 1)
            root(st[:, 32:48], st[:, 16:32], HD)
            root(st[:, 52:56], st[:, 48:52], GW)
            act.wait_ge(s["v_cx"], 1)
            nc.scalar.activation(rows[:, :, 0:GW], rows[:, :, 0:GW], ACT.Silu).then_inc(s["a_silu"], 1)

            def att_exp(i):
                h, q = ATT[i]
                n = P * (q + 1)
                act.wait_ge(s["v_att"], i + 1)
                nc.scalar.activation(prob[:, i % 2, 0:n], prob[:, i % 2, 0:n], ACT.Exp, bias=st[:, 64 + i:65 + i],
                                     accum_out=st[:, 80 + i:81 + i]).then_inc(s["a_att"], 1)

            def att_evac(i):
                n = P * (ATT[i][1] + 1)
                act.wait_ge(s["t_att"], i + 1)
                if i >= 2:
                    act.wait_ge(s["o_att"], i - 1)
                nc.scalar.activation(probT[:, i % 2, 0:n], ps[:, i % 2, 0:n], ACT.Copy).then_inc(s["a_attT"], 1)

            for i in range(NA + 1):
                if i < NA:
                    att_exp(i)
                if i >= 1:
                    att_evac(i - 1)
            act.wait_ge(s["a_silu"], 1)
            act.wait_ge(s["v_convE"], 1)
            act.wait_ge(s["v_attO"], NA)
            act.wait_ge(s["v_sguE"], 8)
            for t in range(NT):
                for m in range(4):
                    nc.scalar.activation(sq_dump, rows[:, t, GW * m:GW * m + GW], ACT.Square,
                                         accum_out=st[:, 96 + 4 * t + m:97 + 4 * t + m]).then_inc(s["a_ss"], 1)
                    act.wait_ge(s["a_ss"], NT + 4 * t + m + 1)
            own_root(st[:, 112:128], st[:, 96:112], GW, NT + 16)
            for k in range(KC):
                act.wait_ge(s["t_mixT"], k + 1)
                nc.scalar.activation(colsT[:, k, :], ps[:, k % 2, :], ACT.Copy, scale=col(R_MIX + k)).then_inc(s["a_mixT"], 1)
            for t in range(NT):
                act.wait_ge(s["v_x1"], t + 1)
                nc.scalar.activation(rows[:, t, :], x1[:, t, :], ACT.Square, accum_out=st[:, 128 + t:129 + t]).then_inc(s["a_ss"], 1)
            own_root(st[:, 132:136], st[:, 128:132], D, 2 * NT + 16)
            for k in range(KC):
                act.wait_ge(s["t_h2T"], k + 1)
                nc.scalar.activation(colsT[:, k, :], ps[:, k % 2, :], ACT.Copy).then_inc(s["a_h2T"], 1)
            act.wait_ge(s["v_gexp"], 1)
            nc.scalar.activation(gk[:], gk[:], ACT.Exp).then_inc(s["a_gexp"], 1)

            act.wait_ge(s["v_tables"], 1)
            last_b = act.value_load(bendi[0:1, NE:NE + 1], min_val=0, max_val=MAXBLK - 2)
            prev_b = act.value_load(bendi[0:1, NE + 1:NE + 2], min_val=0, max_val=MAXBLK - 3)

            def high_x(g):
                act.wait_ge(b_xps, g + 1)
                for j in range(2):
                    last = nc.scalar.activation(xT[:, HI, 4 * j:4 * j + 4, :],
                                                ps[:, 6 + j, :].rearrange("p (c q) -> p c q", c=4), ACT.Copy)
                last.then_inc(b_xH, 1)

            def high_a(n):
                act.wait_ge(b_aps, n)
                for j in range(2):
                    last = nc.scalar.activation(aT[:, HI, 4 * j:4 * j + 4, :],
                                                ps[:, 6 + j, :].rearrange("p (c q) -> p c q", c=4), ACT.Copy)
                last.then_inc(b_aH, 1)

            def sigmoid(g):
                for j in range(2):
                    act.wait_ge(b_min, g * 2 + (j + 1))
                    sl = slice(512 * j, 512 * j + 512)
                    nc.scalar.activation(a_s[:, sl], a_g[:, sl], ACT.Sigmoid, scale=ALPHA).then_inc(b_sig, 1)

            def evac_y(n, idx, wait_scatter=True):
                act.wait_ge(q_w2, n * 4)
                if wait_scatter:
                    act.wait_ge(b_sca, idx * 16)
                nc.scalar.activation(y_sb.rearrange("p (j n) -> p j n", j=2), ps[:, 4:6, :], ACT.Copy,
                                     scale=gcol[:, bass.ds(idx, 1)]).then_inc(b_yev, 1)

            def high_w1(g, k, e, off=0):
                act.wait_ge(l_w1[k], e * 16 + 48)
                nc.scalar.activation(w_ring[:, (k + off) % NRING, HI, :], w1_slots[:, k, :], ACT.Copy).then_inc(h_w1, 1)

            def high_w2(g, c, e):
                act.wait_ge(l_w2[c], e * 16 + 128)
                nc.scalar.activation(w_ring[:, (KC + c) % NRING, HI, :], w2_slots[:, c, :], ACT.Copy).then_inc(h_w2, 1)

            def expert(g):
                return act.value_load(egi[0:1, bass.ds(g, 1)], min_val=0, max_val=NE - 1)

            def step(g, last_y=True, tail=True, off=0):
                e = expert(g)
                if tail:
                    e_before = expert(g - 1)
                for k in range(KC):
                    if k >= 3:
                        act.wait_ge(q_w1, g * KC + (k - 2))
                    elif last_y:
                        act.wait_ge(q_w2, g * 4 + (k - 6))
                    elif tail:
                        act.wait_ge(q_w1, 6 + k)
                    high_w1(g, k, e, off)
                    if k == 2 and last_y:
                        evac_y(g - 1, g - 2, wait_scatter=not (isinstance(g, int) and g <= 2))
                    if k == 7 and tail:
                        high_a(g)
                if tail:
                    for c in range(4):
                        if c < 3:
                            act.wait_ge(q_w1, g * KC + (6 + c))
                        else:
                            act.wait_ge(q_w2, g * 4 - 3)
                        high_w2(g - 1, c, e_before)
                high_x(g + 1)
                sigmoid(g)

            act.wait_ge(st_h2, 16 * NT)
            act.wait_ge(st_g2, 16)
            high_x(0)
            step(0, last_y=False, tail=False, off=1)
            step(1, last_y=False)
            with act.Fori(2, last_b + 1) as g:
                step(g)
            evac_y(last_b, prev_b)
            high_a(last_b + 1)
            e_last = expert(last_b)
            for c in range(4):
                if c == 3:
                    act.wait_ge(q_w2, last_b * 4 + 1)
                else:
                    act.wait_ge(q_w1, last_b * KC + (6 + c))
                high_w2(last_b, c, e_last)
            evac_y(last_b + 1, last_b)
            for t in range(NT):
                act.wait_ge(f_sum, t + 1)
                nc.scalar.activation(fin_sq, fin_x1[:, t, :], ACT.Square, accum_out=st[:, t:t + 1]).then_inc(f_sq, 1)
                act.wait_ge(f_sq, t + 1)
                nc.scalar.activation(st[:, 4 + t:5 + t], st[:, t:t + 1], ACT.Sqrt, bias=eps, scale=1.0 / D).then_inc(f_sd, 1)

        @block.vector
        def _(dve):
            V = nc.vector
            chain = [0]

            def link(ins):
                chain[0] += 1
                ins.then_inc(s["v_chain"], 1)
                dve.wait_ge(s["v_chain"], chain[0])


            dve.wait_ge(s["t_par"], 3)
            link(V.tensor_copy(pc[:], ps[:, 0, 0:R_N + 2 * TAPS]))
            V.tensor_copy(sgub[:], ps[:, 0, 256:256 + NH]).then_inc(s["c_par"], 1)
            dve.wait_ge(s["c_cond"], 1)
            dve.wait_ge(s["t_bias"], 1)
            V.tensor_copy(bias_row, ps[0:NH, 6:8, :].rearrange("p b m -> p (b m)")[:, 0:NDIST]).then_inc(s["c_bias"], 1)
            for k in range(KC):
                dve.wait_ge(l_w1[k], 16)
                if k == 0:
                    V.tensor_scalar(acc0, w1_slots[:, 0, :], cond[:, 0:1], None, ALU.mult).then_inc(s["v_mod0"], 1)
                else:
                    dve.wait_ge(s["v_mod0"], k)
                    V.scalar_tensor_tensor(acc0, w1_slots[:, k, :], cond[:, k:k + 1], acc0, ALU.mult, ALU.add).then_inc(s["v_mod0"], 1)
                if k == 3:
                    dve.wait_ge(s["a_sd"], 1)
                    link(V.reciprocal(st[:, 8:12], st[:, 4:8]))
                    for t in range(NT):
                        V.tensor_scalar(rows[:, t, :], x_sb[:, t, :], st[:, 8 + t:9 + t], None, ALU.mult).then_inc(s["v_xn"], 1)
            dve.wait_ge(s["m_mod0"], 1)
            link(V.tensor_tensor(mod[:, 0:16], ps[:, 2, 0:16], pc[:, R_BMOD:R_BMOD + 16], ALU.add))
            V.scalar_tensor_tensor(gs1[:], mod[:, 8:16], 1.0, pc[:, R_N1:R_N1 + KC], ALU.add, ALU.mult).then_inc(s["c_mod"], 1)
            dve.wait_ge(s["t_wmix"], 1)
            V.tensor_tensor(wmixT, ps[:, 1, :].rearrange("p (h i) -> p h i", h=NH),
                            cst[:, None, C_TRI:C_TRI + P].to_broadcast([P, NH, P]), ALU.mult).then_inc(s["c_wmix"], 1)
            dve.wait_ge(s["m_mod0"], 1)
            link(V.memset(ypad[:, :, 0:PADT], 0.0))
            for c in range(2):
                dve.wait_ge(s["p_proj"], 2 * c + 2)
                dve.wait_ge(s["e_act"], c + 1)
                V.tensor_tensor(ypad[:, c, PADT:PADT + S], ps[:, 3 + 2 * c, :], pT[:, 2 + c, :], ALU.mult).then_inc(s["e_glu"], 1)
            dve.wait_ge(s["e_glu"], 2)
            for tap in range(TAPS):
                for c in range(2):
                    w = taps[:, 2 * tap + c:2 * tap + c + 1]
                    src = ypad[:, c, tap:tap + S]
                    if tap:
                        dve.wait_ge(s["v_conv"], 2 * tap + c - 1)
                        V.scalar_tensor_tensor(pT[:, c, :], src, w, pT[:, c, :], ALU.mult, ALU.add).then_inc(s["v_conv"], 1)
                    else:
                        V.tensor_scalar(pT[:, c, :], src, w, col(R_CB + c), ALU.mult, ALU.add).then_inc(s["v_conv"], 1)
            dve.wait_ge(s["e_act"], 12)
            dve.wait_ge(l_row, 16 * 7)
            A, B = pT[:, 2, :], pT[:, 3, :]

            def double(dst, src, lag, half):
                q = slice(64, P) if half else slice(0, P)
                V.tensor_copy(dst[q, 0:lag], src[q, 0:lag]).then_inc(s["v_chain"], 1)
                chain[0] += 1
                link(V.tensor_tensor(dst[q, lag:S], src[q, lag:S], src[q, 0:S - lag], ALU.add))

            def pooled(c, lo, hi):
                for q, src in ((slice(0, 64), lo), (slice(64, P), hi)):
                    z = pT[q, 8 + c, :]
                    link(V.tensor_tensor(src[q, 0:16], src[q, 0:16], cst[q, C_RC + 16 * c:C_RC + 16 * c + 16], ALU.mult))
                    link(V.tensor_tensor(z[:, 0:16], src[q, 0:16], z[:, 0:16], ALU.subtract))
                    link(V.scalar_tensor_tensor(z[:, 16:S], src[q, 16:S], cst[q, C_RW + c:C_RW + c + 1], z[:, 16:S],
                                                ALU.mult, ALU.subtract))

            double(A, pT[:, 8, :], 1, False)
            double(B, A, 2, True)
            pooled(0, A, B)
            double(A, pT[:, 9, :], 1, False)
            double(B, A, 2, False)
            double(A, B, 4, False)
            double(B, A, 8, True)
            pooled(1, A, B)
            V.memset(st[:, 159:160], 0.0).then_inc(s["v_poolT"], 1)

            dve.wait_ge(s["m_modA"], 1)
            link(V.tensor_tensor(mod[:, 24:40], ps[:, 0, 0:16], pc[:, R_BMOD + 24:R_BMOD + 40], ALU.add))
            V.scalar_tensor_tensor(gs2[:], mod[:, 32:40], 1.0, pc[:, R_N2:R_N2 + KC], ALU.add, ALU.mult).then_inc(s["c_mod12"], 1)

            def centre(dst, src, n, base, g):
                m = st[:, base:base + g]
                link(V.tensor_reduce(m, src, AX.X, ALU.add))
                link(V.tensor_scalar(m, m, -1.0 / n, None, ALU.mult))
                link(V.tensor_tensor(dst, src, m[:, :, None].to_broadcast([P, g, n]), ALU.add))

            dve.wait_ge(s["t_conv"], 1)
            cps = ps[:, 6:8, :].rearrange("p b (t c) -> p (b t) c", t=2).rearrange("p t (h d) -> p (t h) d", h=NH)
            cx = rows[:, :, 0:GW]
            dv = dense.rearrange("p (g n) -> p g n", n=HD)
            centre(dv, cps, HD, 16, 16)
            link(V.tensor_tensor(sqv, dense, dense, ALU.mult))
            V.tensor_reduce(st[:, 16:32], sqv.rearrange("p (g n) -> p g n", n=HD), AX.X, ALU.add).then_inc(s["v_var"], 1)
            dve.wait_ge(s["a_sd"], 2)
            link(V.reciprocal(st[:, 16:32], st[:, 32:48]))
            link(V.tensor_tensor(dv, dv, st[:, 16:32, None].to_broadcast([P, 16, HD]), ALU.mult))
            d4 = dense.rearrange("p (t c) -> p t c", t=NT)
            link(V.tensor_tensor(d4, d4, lrows[:, None, 0, :].to_broadcast([P, NT, GW]), ALU.mult))
            V.tensor_tensor(cx, d4, lrows[:, None, 1, :].to_broadcast([P, NT, GW]), ALU.add).then_inc(s["v_cx"], 1)
            dve.wait_ge(s["e_act"], NPROJ - 2)
            sv = pR[:, :, 2 * GW:3 * GW]
            dve.wait_ge(s["v_cx"], 1)
            centre(d4, sv, GW, 48, 4)
            link(V.tensor_tensor(sqv, dense, dense, ALU.mult))
            V.tensor_reduce(st[:, 48:52], sqv.rearrange("p (g n) -> p g n", n=GW), AX.X, ALU.add).then_inc(s["v_var"], 1)
            dve.wait_ge(s["a_sd"], 3)
            link(V.reciprocal(st[:, 48:52], st[:, 52:56]))
            link(V.tensor_tensor(d4, d4, st[:, 48:52, None].to_broadcast([P, NT, GW]), ALU.mult))
            link(V.tensor_tensor(d4, d4, lrows[:, None, 3, :].to_broadcast([P, NT, GW]), ALU.mult))
            V.tensor_tensor(sv, d4, lrows[:, None, 4, :].to_broadcast([P, NT, GW]), ALU.add).then_inc(s["v_sgu"], 1)
            dve.wait_ge(s["m_pool"], 1)
            V.tensor_tensor(rows[:, :, 2 * GW:3 * GW], ps[:, 4:6, :].rearrange("p b (t c) -> p (b t) c", t=2),
                            lrows[:, None, 2, :].to_broadcast([P, NT, GW]), ALU.mult).then_inc(s["v_convE"], 1)

            def att_scores(i):
                h, q = ATT[i]
                n = P * (q + 1)
                dve.wait_ge(s["s_att"], i + 1)
                if i >= 2:
                    dve.wait_ge(s["t_att"], i - 1)
                link(V.scalar_tensor_tensor(prob[:, i % 2, 0:n], ps[:, 6 + h % 2, 0:n], HD ** -0.5,
                                            bias_t[:, h, S - P - P * q:S], ALU.mult, ALU.add))
                V.tensor_reduce(st[:, 64 + i:65 + i], prob[:, i % 2, 0:n], AX.X, ALU.max, negate=True).then_inc(s["v_att"], 1)

            def att_norm(i):
                h, q = ATT[i]
                dve.wait_ge(s["o_att"], i + 1)
                link(V.reciprocal(st[:, 80 + i:81 + i], st[:, 80 + i:81 + i]))
                V.tensor_scalar(rows[:, q, GW + HD * h:GW + HD * h + HD], ps[:, 2 + i % 2, 0:HD], st[:, 80 + i:81 + i],
                                None, ALU.mult).then_inc(s["v_attO"], 1)

            dve.wait_ge(l_bt, 16)
            for i in range(NA + 2):
                if i < NA:
                    att_scores(i)
                if i == 2:
                    dve.wait_ge(s["m_sgu"], 1)
                    for h in range(NH):
                        o = slice(HD * h, HD * h + HD)
                        for b in range(2):
                            t2 = slice(2 * b, 2 * b + 2)
                            V.scalar_tensor_tensor(rows[:, t2, 3 * GW + HD * h:3 * GW + HD * h + HD],
                                                   ps[:, 4 + b, :].rearrange("p (t c) -> p t c", t=2)[:, :, o], sgub[:, h:h + 1],
                                                   pR[:, t2, GW + HD * h:GW + HD * h + HD], ALU.add, ALU.mult).then_inc(s["v_sguE"], 1)
                if i >= 2:
                    att_norm(i - 2)
            dve.wait_ge(s["m_mod"], 1)
            dve.wait_ge(l_x1, 48)
            V.tensor_tensor(gate1, gate1, ps[:, 4:6, :].rearrange("p b n -> p (b n)"), ALU.add).then_inc(s["c_mod12"], 1)
            V.tensor_tensor(gate2, g2row, ps[:, 6:8, :].rearrange("p b n -> p (b n)"), ALU.add).then_inc(s["c_mod12"], 1)
            dve.wait_ge(s["a_sd"], 4)
            link(V.reciprocal(st[:, 112:128], st[:, 112:128]))
            for t in range(NT):
                r = rows[:, t, :].rearrange("p (m c) -> p m c", m=4)
                V.tensor_tensor(r, r, st[:, 112 + 4 * t:116 + 4 * t, None].to_broadcast([P, 4, GW]), ALU.mult).then_inc(s["v_mixed"], 1)
            for t in range(NT):
                dve.wait_ge(s["m_out"], 2 * t + 2)
                po = ps[:, 2 + 2 * (t % 2):4 + 2 * (t % 2), :].rearrange("p b n -> p (b n)")
                if t == 0:
                    dve.wait_ge(s["c_mod12"], 3)
                link(V.tensor_tensor(gated, po, gate1, ALU.mult))
                V.tensor_tensor(x1[:, t, :], x1[:, t, :], gated, ALU.add).then_inc(s["v_x1"], 1)
                dve.wait_ge(s["v_x1"], t + 1)
            dve.wait_ge(s["a_sd"], 5)
            link(V.reciprocal(st[:, 132:136], st[:, 132:136]))
            dve.wait_ge(s["t_rows2"], 1)
            for t in range(NT):
                h2 = rows[:, t, :].rearrange("p (b n) -> p b n", b=2)
                link(V.scalar_tensor_tensor(h2, x1[:, t, :].rearrange("p (b n) -> p b n", b=2), st[:, 132 + t:133 + t],
                                            ps[:, 6:8, :], ALU.mult, ALU.mult))
                V.tensor_tensor(h2, h2, ps[:, 0:2, :], ALU.add).then_inc(s["v_h2"], 1)
            dve.wait_ge(s["m_lg"], 1)
            link(V.tensor_tensor(lg, ps[:, 2, 0:NT * NE].rearrange("p (t e) -> p t e", t=NT),
                                 rb_sb[:, None, :].to_broadcast([P, NT, NE]), ALU.add))
            for t in range(NT):
                link(V.max(v8[:, t, :], lg[:, t, :]))
                link(V.max_index(i8[:, t, :], v8[:, t, :], lg[:, t, :]))
            link(V.tensor_copy(i8f, i8))
            V.tensor_tensor(gk, v8[:, :, 0:TOPK], v8[:, :, 0:1].to_broadcast([P, NT, TOPK]), ALU.subtract).then_inc(s["v_gexp"], 1)
            dve.wait_ge(s["a_gexp"], 1)
            link(V.tensor_reduce(gsum, gk, AX.X, ALU.add))
            link(V.reciprocal(gsum, gsum))
            link(V.tensor_tensor(gk, gk, gsum[:, :, None].to_broadcast([P, NT, TOPK]), ALU.mult))
            iota_e = cst[:, None, C_IOE:C_IOE + NE].to_broadcast([P, NT, NE])
            asg = cst[:, C_ASG:C_ASG + NT * TOPK].rearrange("p (t k) -> p t k", t=NT)
            tab_r, tab_g = vtab[:, :, :, 0], vtab[:, :, :, 2]
            for k in range(TOPK):
                link(V.tensor_tensor(eqk, iota_e, i8f[:, :, k:k + 1].to_broadcast([P, NT, NE]), ALU.is_equal))
                if k == 0:
                    link(V.tensor_copy(memb, eqk))
                    link(V.tensor_tensor(tab_r, eqk, asg[:, :, k:k + 1].to_broadcast([P, NT, NE]), ALU.mult))
                    link(V.tensor_tensor(tab_g, eqk, gk[:, :, k:k + 1].to_broadcast([P, NT, NE]), ALU.mult))
                else:
                    link(V.tensor_tensor(memb, memb, eqk, ALU.add))
                    link(V.tensor_tensor(tmpk, eqk, asg[:, :, k:k + 1].to_broadcast([P, NT, NE]), ALU.mult))
                    link(V.tensor_tensor(tab_r, tab_r, tmpk, ALU.add))
                    link(V.tensor_tensor(tmpk, eqk, gk[:, :, k:k + 1].to_broadcast([P, NT, NE]), ALU.mult))
                    link(V.tensor_tensor(tab_g, tab_g, tmpk, ALU.add))
            V.memset(st[:, 159:160], 0.0).then_inc(s["v_memb"], 1)
            link(V.scalar_tensor_tensor(tab_r, memb, -float(EMPTY), tab_r, ALU.mult, ALU.add))
            link(V.tensor_tensor(vtab[:, :, :, 1], memb, cst[:, C_TOK:C_TOK + NT, None].to_broadcast([P, NT, NE]), ALU.mult))
            link(V.memset(vtab[:, :, :, 3], 0.0))
            dve.wait_ge(s["m_rank"], 1)
            link(V.tensor_copy(cnt, ps[:, 3, 128:160]))
            link(V.tensor_scalar(nblk, cnt, 0.0, None, ALU.is_gt))
            for b in range(1, S // P):
                link(V.scalar_tensor_tensor(nblk, cnt, float(P * b), nblk, ALU.is_gt, ALU.add))
            link(V.tensor_tensor_scan(bend, cst[:, C_ONES:C_ONES + NE], nblk, 0.0, ALU.mult, ALU.add))
            link(V.tensor_copy(bendi[:, 0:NE], bend))
            link(V.tensor_scalar(bendi[:, NE:NE + 1], bend[:, NE - 1:NE], 1.0, None, ALU.subtract))
            link(V.tensor_scalar(bendi[:, NE + 1:NE + 2], bend[:, NE - 1:NE], 2.0, None, ALU.subtract))
            link(V.tensor_tensor(bstart, bend, nblk, ALU.subtract))
            link(V.tensor_scalar(bstart, bstart, float(P), 1.0, ALU.mult, ALU.add))
            link(V.tensor_tensor(pos, ps[:, 3, 0:NT * NE].rearrange("p (t e) -> p t e", t=NT),
                                 bstart[:, None, :].to_broadcast([P, NT, NE]), ALU.add))
            link(V.tensor_tensor(pos, pos, memb, ALU.mult))
            dve.wait_ge(s["g_bf"], 6)
            link(V.tensor_tensor(cmp_be, bend[:, None, :].to_broadcast([P, MAXBLK, NE]),
                                 cst[:, C_IOB:C_IOB + MAXBLK, None].to_broadcast([P, MAXBLK, NE]), ALU.is_le))
            link(V.tensor_reduce(egf[:], cmp_be, AX.X, ALU.add))
            link(V.tensor_scalar(egf[:], egf[:], float(NE - 1), None, ALU.min))
            link(V.tensor_copy(egi[:], egf[:]))
            link(V.tensor_copy(slot_no, cst[:, C_SLOT:C_SLOT + P]))
            V.memset(st[:, 158:159], 0.0).then_inc(s["v_tables"], 1)

            last_b = dve.value_load(bendi[0:1, NE:NE + 1], min_val=0, max_val=MAXBLK - 2)

            def one_hot(g):
                e = dve.value_load(egi[0:1, bass.ds(g, 1)], min_val=0, max_val=NE - 1)
                dve.wait_ge(b_tab, g)
                for t in range(NT):
                    last = V.tensor_scalar(hot[:, t, :], slot_no, pos[:, t, bass.ds(e, 1)], None, ALU.is_equal)
                last.then_inc(b_hot, 1)
                dve.wait_ge(b_hot, g + 1)
                V.tensor_scalar(slot_no, slot_no, float(P), None, ALU.add).then_inc(b_chain, 1)
                dve.wait_ge(b_chain, g + 1)

            def table(g):
                dve.wait_ge(b_tab, g + 1)
                V.tensor_scalar(idx_out[:, bass.ds(g, 1)], ps[:, 6, 0:1], float(EMPTY), None, ALU.add)
                V.tensor_copy(idx_tok[:, bass.ds(g, 1)], ps[:, 6, 1:2])
                V.tensor_copy(gcol[:, bass.ds(g, 1)], ps[:, 6, 2:3]).then_inc(b_idx, 1)

            def select(dst, g, signal):
                V.tensor_tensor(dst[0:96, :], cst[0:96, C_PM:C_PM + 1].to_broadcast([96, P]),
                                egf[0:96, bass.ds(g, 1)].to_broadcast([96, P]), ALU.is_equal).then_inc(signal, 1)

            def low_w1(g, k, off=0):
                dve.wait_ge(h_w1, g * KC + (k + 1))
                r = (k + off) % NRING
                V.tensor_tensor(w_ring[:, r, LO, 0:1536], w1_slots[:, k, 0:1536], w_ring[:, r, HI, 0:1536].bitcast(F32),
                                ALU.subtract).then_inc(d_w1, 1)

            def low_w2(g, c):
                dve.wait_ge(h_w2, g * 4 + (c + 1))
                r = (KC + c) % NRING
                V.tensor_tensor(w_ring[:, r, LO, 0:1536], w2_slots[:, c, 0:1536], w_ring[:, r, HI, 0:1536].bitcast(F32),
                                ALU.subtract).then_inc(d_w2, 1)

            def low_x(g):
                dve.wait_ge(b_xH, g + 1)
                V.tensor_tensor(xT[:, LO, :, :].rearrange("p c q -> p (c q)"), ps[:, 6:8, :].rearrange("p b n -> p (b n)"),
                                xT[:, HI, :, :].bitcast(F32).rearrange("p c q -> p (c q)"), ALU.subtract).then_inc(b_xL, 1)

            def low_a(n):
                dve.wait_ge(b_aH, n)
                V.tensor_tensor(aT[:, LO, :, :].rearrange("p c q -> p (c q)"), ps[:, 6:8, :].rearrange("p b n -> p (b n)"),
                                aT[:, HI, :, :].bitcast(F32).rearrange("p c q -> p (c q)"), ALU.subtract).then_inc(b_aL, 1)

            def clamp_glu(g):
                dve.wait_ge(q_w1, g * KC + KC)
                for j in range(2):
                    V.tensor_scalar(a_g[:, 512 * j:512 * j + 512], ps[:, j, :], LIM, None, ALU.min).then_inc(b_min, 1)

            def clamp_lin(g, first=False):
                if not first:
                    dve.wait_ge(b_aps, g)
                V.tensor_scalar(a_l.rearrange("p (b n) -> p b n", b=2), ps[:, 2:4, :], LIM, -LIM, ALU.min, ALU.max).then_inc(b_hread, 1)

            def swiglu(n):
                dve.wait_ge(b_hread, n)
                dve.wait_ge(b_min, n * 2)
                V.scalar_tensor_tensor(a_l, a_l, 1.0, a_g, ALU.add, ALU.mult).then_inc(b_lin, 1)
                dve.wait_ge(b_sig, n * 2)
                dve.wait_ge(b_lin, n)
                V.tensor_tensor(a_l, a_l, a_s, ALU.mult).then_inc(b_act, 1)

            def step(g, tail=True, off=0):
                for k in range(KC):
                    low_w1(g, k, off)
                    if k == 0:
                        one_hot(g + 1)
                    if k == 2 and tail:
                        swiglu(g)
                        if not (isinstance(g, int) and g < 2):
                            dve.wait_ge(q_w2, g * 4 - 4)
                        select(selB, g - 1, b_selB)
                    if k == 4:
                        table(g + 1)
                    if k == 7 and tail:
                        low_a(g)
                if tail:
                    for c in range(3):
                        low_w2(g - 1, c)
                clamp_glu(g)
                if tail:
                    low_w2(g - 1, 3)
                clamp_lin(g, first=not tail)
                low_x(g + 1)
                select(selA, g + 1, b_selA)

            one_hot(0)
            table(0)
            select(selA, 0, b_selA)
            low_x(0)
            dve.wait_ge(st_x1, 16 * NT)
            step(0, tail=False, off=1)
            step(1)
            with dve.Fori(2, last_b + 1) as g:
                step(g)
            swiglu(last_b + 1)
            dve.wait_ge(q_w2, last_b * 4)
            select(selB, last_b, b_selB)
            low_a(last_b + 1)
            for c in range(4):
                low_w2(last_b, c)
            for t in range(NT):
                dve.wait_ge(l_fin[t], 16)
                if t == 0:
                    dve.wait_ge(f_ld, 48)
                y4 = w1_slots[:, 2 * t:2 * t + 2, :].rearrange("p a (b n) -> p a b n", b=2)
                link(V.tensor_tensor(y4[:, 0, :, :], y4[:, 0, :, :], y4[:, 1, :, :], ALU.add))
                link(V.tensor_tensor(y4[:, 0, 0, :], y4[:, 0, 0, :], y4[:, 0, 1, :], ALU.add))
                link(V.tensor_tensor(y4[:, 0, 0, :], y4[:, 0, 0, :], fin_gate2, ALU.mult))
                V.tensor_tensor(fin_x1[:, t, :], fin_x1[:, t, :], y4[:, 0, 0, :], ALU.add).then_inc(f_sum, 1)
            for t in range(NT):
                dve.wait_ge(f_sd, t + 1)
                link(V.reciprocal(st[:, 8 + t:9 + t], st[:, 4 + t:5 + t]))
                V.scalar_tensor_tensor(fin_x1[:, t, :], fin_x1[:, t, :], st[:, 8 + t:9 + t], fin_g, ALU.mult, ALU.mult).then_inc(f_o, 1)

        @block.tensor
        def _(pe):
            T = nc.tensor

            def turn(bank, k, src, ev, done):
                for t in range(NT):
                    last = T.transpose(ps[:, bank, part(t)], src[:, t, P * k:P * k + P], ident)
                last.then_inc(done, 1)

            pe.wait_ge(l_cst, 16)
            pe.wait_ge(l_par, 16 * N_PAR)
            T.transpose(ps[:, 0, 0:R_N], parms[0:R_N, :], ident[0:R_N, 0:R_N]).then_inc(s["t_par"], 1)
            T.transpose(ps[:, 0, R_N:R_N + 2 * TAPS], taps_r, ident[0:2 * TAPS, 0:2 * TAPS]).then_inc(s["t_par"], 1)
            T.transpose(ps[:, 0, 256:256 + NH], sgub_r, ident[0:NH, 0:NH]).then_inc(s["t_par"], 1)
            T.matmul(ps[0:NH, 6, :], relb[:], buckets[:, 0:512], start=True, stop=True)
            T.matmul(ps[0:NH, 7, 0:NDIST - 512], relb[:], buckets[:, 512:NDIST], start=True, stop=True).then_inc(s["t_bias"], 1)
            for h in range(NH):
                last = T.transpose(ps[:, 1, part(h)], sguw_r[:, h, :], ident)
            last.then_inc(s["t_wmix"], 1)

            def column_sums(bank, acc, done):
                for j in range(16):
                    last = T.matmul(ps[:, bank, j:j + 1], acc[:, P * j:P * j + P], ones[:, 0:1], start=True, stop=True)
                last.then_inc(done, 1)

            pe.wait_ge(s["v_mod0"], KC)
            column_sums(2, acc0, s["m_mod0"])
            pe.wait_ge(s["v_xn"], NT)
            for k in range(KC):
                if k == 0:
                    pe.wait_ge(s["c_par"], 1)
                if k == 1:
                    pe.wait_ge(s["c_wmix"], 1)
                if k >= 2:
                    pe.wait_ge(s["a_hT"], k - 1)
                turn(k % 2, k, rows, None, s["t_hT"])
            for i, (kind, n, wc) in enumerate(PROJ):
                if i == 0:
                    pe.wait_ge(s["c_mod"], 1)
                j = i - 4
                if j in (1, 3):
                    pe.wait_ge(s["e_glu"], j // 2 + 1)
                elif j in (0, 2):
                    pe.wait_ge(s["e_act"], j // 2 + 1)
                elif j >= 4:
                    pe.wait_ge(s["e_act"], j - 1)
                bank = ps[:, 2 + i % 4, :]
                for k in range(KC):
                    if i == 0:
                        pe.wait_ge(s["a_hT"], k + 1)
                        pe.wait_ge(l_w1[k], 32)
                    if kind == "v":
                        last = T.matmul(bank[:, 0:GW], colsT[:, k, part(n)], w1_slots[:, k, 1024:1280],
                                        start=(k == 0), stop=(k == KC - 1))
                    elif kind == "s":
                        last = T.matmul(bank, colsT[:, k, part(n)], w1_slots[:, k, 1536:2048],
                                        start=(k == 0), stop=(k == KC - 1))
                    else:
                        last = T.matmul(bank, w1_slots[:, k, P * wc:P * wc + P], colsT[:, k, :],
                                        start=(k == 0), stop=(k == KC - 1))
                last.then_inc(s["p_proj"], 1)
                if i == 12:
                    pe.wait_ge(s["g_added"], KC)
                    column_sums(0, acc12, s["m_modA"])
            pe.wait_ge(s["v_conv"], 2 * TAPS)
            pe.wait_ge(s["c_bias"], 1)
            for t in range(NT):
                for c in range(2):
                    last = T.transpose(ps[:, 6 + t // 2, GW * (t % 2) + P * c:GW * (t % 2) + P * c + P],
                                       pT[:, c, part(t)], ident)
            last.then_inc(s["t_conv"], 1)
            pe.wait_ge(s["v_poolT"], 1)
            pe.wait_ge(l_pw, 64)
            pe.wait_ge(s["e_act"], 14)
            for t in range(NT):
                for c in range(2):
                    last = T.matmul(ps[:, 4 + t // 2, GW * (t % 2) + P * c:GW * (t % 2) + P * c + P],
                                    pT[:, 8 + c, part(t)], poolw[:, c, :], start=True, stop=True)
            last.then_inc(s["m_pool"], 1)

            def att_scores(i):
                h, q = ATT[i]
                hp = slice(HD * (h % 2), HD * (h % 2) + HD)
                if i == 0:
                    pe.wait_ge(s["v_sgu"], 1)
                if i >= 2:
                    pe.wait_ge(s["v_att"], i - 1)
                T.matmul(ps[:, 6 + h % 2, 0:P * (q + 1)], pT[hp, 4 + h // 2, part(q)], pT[hp, 6 + h // 2, 0:P * (q + 1)],
                         start=True, stop=True).then_inc(s["s_att"], 1)

            def att_turn(i):
                h, q = ATT[i]
                pe.wait_ge(s["a_att"], i + 1)
                if i == 0:
                    pe.wait_ge(s["c_mod12"], 1)
                if i >= 2:
                    pe.wait_ge(s["a_attT"], i - 1)
                for j in range(q + 1):
                    last = T.transpose(ps[:, i % 2, part(j)], prob[:, i % 2, part(j)], ident)
                last.then_inc(s["t_att"], 1)

            def att_out(i):
                h, q = ATT[i]
                pe.wait_ge(s["a_attT"], i + 1)
                if i >= 2:
                    pe.wait_ge(s["v_attO"], i - 1)
                for j in range(q + 1):
                    last = T.matmul(ps[:, 2 + i % 2, 0:HD], probT[:, i % 2, part(j)], pR[:, j, HD * h:HD * h + HD],
                                    start=(j == 0), stop=(j == q))
                last.then_inc(s["o_att"], 1)

            for i in range(NA + 2):
                if i < NA:
                    att_scores(i)
                if i == 1:
                    pe.wait_ge(s["v_convE"], 1)
                    for t in range(NT):
                        for h in range(NH):
                            last = T.matmul(ps[:, 4 + t // 2, GW * (t % 2) + HD * h:GW * (t % 2) + HD * h + HD], wmixT[:, h, :],
                                            pR[:, t, 2 * GW + HD * h:2 * GW + HD * h + HD], start=True, stop=True)
                    last.then_inc(s["m_sgu"], 1)
                if 1 <= i <= NA:
                    att_turn(i - 1)
                if i >= 2:
                    att_out(i - 2)
            pe.wait_ge(s["g_added"], 2 * KC)
            pe.wait_ge(s["v_sguE"], 8)
            pe.wait_ge(s["v_att"], NA)
            for j in range(4):
                last = T.matmul(ps[:, 4 + j, :], ones, acc12[:, 512 * j:512 * j + 512], start=True, stop=True)
            last.then_inc(s["m_mod"], 1)
            pe.wait_ge(s["v_mixed"], NT)
            for k in range(KC):
                if k >= 2:
                    pe.wait_ge(s["a_mixT"], k - 1)
                turn(k % 2, k, rows, None, s["t_mixT"])
            pe.wait_ge(s["a_mixT"], KC)
            for k in range(KC):
                for b, c in ((6, gs2[:, k:k + 1]), (0, mod[:, 24 + k:25 + k])):
                    last = T.matmul(ps[:, b + k // 4, part(k % 4)], c.to_broadcast([P, P]), ident, start=True, stop=True)
            last.then_inc(s["t_rows2"], 1)
            pe.wait_ge(s["c_mod12"], 3)
            pe.wait_ge(s["v_attO"], NA)
            for c in range(4):
                pe.wait_ge(l_w2[c], 112)
            for t in range(NT):
                if t >= 2:
                    pe.wait_ge(s["v_x1"], t - 1)
                for n in range(2):
                    for k in range(KC):
                        last = T.matmul(ps[:, 2 + 2 * (t % 2) + n, :], colsT[:, k, part(t)],
                                        w2_slots[:, k // 2, 1024 * (k % 2) + 512 * n:1024 * (k % 2) + 512 * n + 512],
                                        start=(k == 0), stop=(k == KC - 1))
                    last.then_inc(s["m_out"], 1)
            pe.wait_ge(s["v_h2"], NT)
            for k in range(KC):
                if k >= 2:
                    pe.wait_ge(s["a_h2T"], k - 1)
                turn(k % 2, k, rows, None, s["t_h2T"])
            pe.wait_ge(s["a_h2T"], KC)
            pe.wait_ge(l_row, 16 * 7)
            pe.wait_ge(s["v_x1"], NT)
            for t in range(NT):
                for k in range(KC):
                    last = T.matmul(ps[:, 2, NE * t:NE * t + NE], colsT[:, k, part(t)], rw_sb[:, k, :],
                                    start=(k == 0), stop=(k == KC - 1))
            last.then_inc(s["m_lg"], 1)
            pe.wait_ge(s["v_memb"], 1)
            strict = cst[:, C_STRICT:C_STRICT + P]
            for t in range(NT):
                for j in range(t + 1):
                    T.matmul(ps[:, 3, NE * t:NE * t + NE], strict if j == t else ones, memb[:, j, :],
                             start=(j == 0), stop=(j == t))
            for t in range(NT):
                last = T.matmul(ps[:, 3, 128:128 + NE], ones, memb[:, t, :], start=(t == 0), stop=(t == NT - 1))
            last.then_inc(s["m_rank"], 1)

            for used in (d_w1, p_w1):
                pe.nop().then_inc(used, KC)
            for used in (d_w2, p_w2):
                pe.nop().then_inc(used, 4)
            pe.nop().then_inc(b_yev, 1)
            pe.wait_ge(s["v_tables"], 1)
            last_b = pe.value_load(bendi[0:1, NE:NE + 1], min_val=0, max_val=MAXBLK - 2)

            def expert(g):
                return pe.value_load(egi[0:1, bass.ds(g, 1)], min_val=0, max_val=NE - 1)

            def table(g, first=False):
                e = expert(g)
                pe.wait_ge(b_hot, g + 1)
                if not first:
                    pe.wait_ge(b_xL, g)
                for t in range(NT):
                    last = T.matmul(ps[:, 6, 0:4], hot[:, t, :], vtab[:, t, bass.ds(e, 1), :].rearrange("p e c -> p (e c)"),
                                    start=(t == 0), stop=(t == NT - 1))
                last.then_inc(b_tab, 1)

            def turn_rows(g, turned=True):
                pe.wait_ge(b_gat, g * 16 + 16)
                pe.wait_ge(b_idx, g + 1)
                if turned:
                    pe.wait_ge(b_aL, g - 1)
                for k in range(KC):
                    last = T.transpose(ps[:, 6 + k // 4, part(k % 4)], xg[:, P * k:P * k + P], ident)
                last.then_inc(b_xps, 1)

            def turn_act(n):
                pe.wait_ge(b_act, n)
                for i in range(KC):
                    last = T.transpose(ps[:, 6 + i // 4, part(i % 4)],
                                       a_l.rearrange("p (c q j) -> p c j q", c=4, j=2)[:, i // 2, i % 2, :], ident)
                last.then_inc(b_aps, 1)

            def up(g, tail=True, off=0):
                pe.wait_ge(b_selA, g + 1)
                pe.wait_ge(b_xL, g + 1)
                if tail:
                    pe.wait_ge(b_hread, g)
                for n in range(4):
                    T.matmul(ps[:, n, :], selA[0:96, :], b_bf[:, 512 * n:512 * n + 512], start=True, stop=False)
                for k in range(KC):
                    r = (k + off) % NRING
                    pe.wait_ge(h_w1, g * KC + (k + 1))
                    for x in (HI, LO):
                        for n in range(4):
                            T.matmul(ps[:, n, :], xT[:, x, k, :], w_ring[:, r, HI, 512 * n:512 * n + 512], start=False, stop=False)
                    pe.wait_ge(d_w1, g * KC + (KC + k + 1))
                    for n in range(4):
                        if n == 3:
                            pe.wait_ge(p_w1, g * KC + (KC + k + 1))
                        last = T.matmul(ps[:, n, :], xT[:, HI, k, :], w_ring[:, r, LO, 512 * n:512 * n + 512],
                                        start=False, stop=(k == KC - 1))
                    last.then_inc(q_w1, 1)
                    if k == 0:
                        table(g + 1)
                    if k == 4 and tail:
                        pe.wait_ge(b_idx, g + 2)
                        turn_act(g)

            def down(n, first=False):
                pe.wait_ge(b_selB, n)
                pe.wait_ge(b_aL, n)
                if not first:
                    pe.wait_ge(b_yev, n)
                for j in range(2):
                    T.matmul(ps[:, 4 + j, :], selB[0:96, :], b_bf[:, 2048 + 512 * j:2560 + 512 * j], start=True, stop=False)
                for c in range(4):
                    r = (KC + c) % NRING
                    pe.wait_ge(h_w2, n * 4 + (c - 3))
                    for x, w in ((HI, HI), (LO, HI), (HI, LO)):
                        if w == LO:
                            pe.wait_ge(d_w2, n * 4 + (c + 1))
                        for j in range(2):
                            for h in range(2):
                                if w == LO and j == 1 and h == 1:
                                    pe.wait_ge(p_w2, n * 4 + (c + 1))
                                at = 1024 * j + 512 * h
                                last = T.matmul(ps[:, 4 + h, :], aT[:, x, 2 * c + j, :], w_ring[:, r, w, at:at + 512],
                                                start=False, stop=(c == 3 and w == LO and j == 1))
                    last.then_inc(q_w2, 1)

            pe.wait_ge(s["g_bf"], 6)
            table(0, first=True)
            turn_rows(0, turned=False)
            up(0, tail=False, off=1)
            turn_rows(1, turned=False)
            up(1)
            turn_rows(2)
            down(1, first=True)
            with pe.Fori(2, last_b + 1) as g:
                up(g)
                turn_rows(g + 1)
                down(g)
            pe.wait_ge(b_xL, last_b + 2)
            turn_act(last_b + 1)
            down(last_b + 1)


_OUTS = [((1, S, D), "float32")]
_INS = ["x", "c", "w_mod", "b_mod", "norm1_g", "w_in", "conv_w", "conv_b", "conv_norm_g", "conv_norm_b", "rel_bias", "pool_w",
        "pool_scale", "sgu_norm_g", "sgu_norm_b", "sgu_w", "sgu_b", "mix_out_g", "w_out", "norm2_g", "router_w", "router_b",
        "exp_w1", "exp_b1", "exp_w2", "exp_b2", "final_norm_g"]


def kernel(**inputs):
    import concourse.bacc as bacc
    from concourse.bass_utils import run_bass_kernel_spmd

    nc = bacc.Bacc("TRN2", target_bir_lowering=False, num_devices=1)
    arrays, args = {}, {}
    for name in _INS:
        v = np.ascontiguousarray(inputs[name])
        arrays[f"in_{name}"] = v
        args[name] = nc.dram_tensor(f"in_{name}", v.shape, mybir.dt.from_np(v.dtype), kind="ExternalInput").ap()
    extra = []
    for name, v in (("consts", constants()), ("buckets", distance_buckets())):
        arrays[f"in_{name}"] = v
        extra.append(nc.dram_tensor(f"in_{name}", v.shape, F32, kind="ExternalInput").ap())
    out = nc.dram_tensor("out_0", _OUTS[0][0], F32, kind="ExternalOutput").ap()
    build(nc, args, extra[0], extra[1], out)
    r = run_bass_kernel_spmd(nc, [arrays], core_ids=[0])
    return r.results[0]["out_0"]
```

```python
import math
from contextlib import ExitStack

import numpy as np
import concourse.bass as bass
from concourse import mybir

ALU = mybir.AluOpType
ACT = mybir.ActivationFunctionType
AX = mybir.AxisListType
F32 = mybir.dt.float32
F32R = mybir.dt.float32r
BF16 = mybir.dt.bfloat16
U32 = mybir.dt.uint32

P = 128
D, S = 1024, 512
NT = S // P
KC = D // P
GW, NH, HD = 256, 4, 64
TAPS = 31
PADT = TAPS - 1
NE, TOPK, DFF = 32, 4, 1024
LIM, ALPHA, EPS = 7.0, 1.702, 1e-6
MAXBLK = NE + S * TOPK // P
EMPTY = 4096
NBUCK, MAXDIST = 32, 128
NDIST = S + P
NEG = -1.0e30

C_ID, C_TRI, C_STRICT, C_ONES, C_SLOT = 0, 128, 256, 384, 512
C_PM = 640
C_IOB = 641
C_IOE = C_IOB + MAXBLK
C_TOK = C_IOE + NE
C_ASG = C_TOK + NT
C_RW = C_ASG + NT * TOPK
C_RC = C_RW + 2
C_EPS = C_RC + 32
C_N = C_EPS + 1

R_C, R_N1, R_N2, R_MIX, R_BMOD, R_CB, R_N = 0, 8, 16, 24, 32, 80, 82


def constants():
    c = np.zeros((P, C_N), np.float32)
    p = np.arange(P)
    c[:, C_ID:C_ID + P] = np.eye(P)
    c[:, C_TRI:C_TRI + P] = p[:, None] <= p[None, :]
    c[:, C_STRICT:C_STRICT + P] = p[:, None] < p[None, :]
    c[:, C_ONES:C_ONES + P] = 1.0
    c[:, C_SLOT:C_SLOT + P] = p[None, :] + 1
    c[:, C_PM] = p % NE
    c[:, C_IOB:C_IOB + MAXBLK] = np.arange(MAXBLK)
    c[:, C_IOE:C_IOE + NE] = np.arange(NE)
    tok = p[:, None] + P * np.arange(NT)[None, :]
    c[:, C_TOK:C_TOK + NT] = tok - EMPTY
    c[:, C_ASG:C_ASG + NT * TOPK] = (tok[:, :, None] * TOPK + np.arange(TOPK)).reshape(P, -1)
    for ch in range(2):
        w = 2 ** (1 + 2 * ch + p // 64)
        c[:, C_RW + ch] = 1.0 / w
        c[:, C_RC + 16 * ch:C_RC + 16 * ch + 16] = 1.0 / np.minimum(np.arange(1, 17)[None, :], w[:, None])
    c[:, C_EPS] = EPS
    return c


def distance_buckets():
    dist = (S - 1) - np.arange(NDIST)
    n = np.maximum(dist, 0)
    exact = NBUCK // 2
    large = exact + (np.log(np.maximum(n, 1).astype(np.float32) / np.float32(exact)) / np.float32(math.log(MAXDIST / exact))
                     * (NBUCK - exact)).astype(np.int32)
    b = np.where(n < exact, n, np.minimum(large, NBUCK - 1))
    out = np.zeros((NBUCK + 1, NDIST), np.float32)
    out[:NBUCK] = (b[None, :] == np.arange(NBUCK)[:, None]) & (dist >= 0)[None, :]
    out[NBUCK:] = np.where(dist < 0, NEG, 0.0)
    return out


def build(nc, a, consts_d, buckets_d, out_d):
    with ExitStack() as ctx:
        def sb(name, shape, dt=F32):
            return ctx.enter_context(nc.sbuf_tensor(name, shape, dt))

        def sem(name):
            return ctx.enter_context(nc.semaphore(name))

        hl_at = (nc.sbuf_base + 31) // 32 * 32
        rows = sb("rows", [P, NT, D])
        colsT = sb("colsT", [P, KC, S])
        arena = sb("arena", [P, 16384])
        arena_at = hl_at + 32 * 1024
        w1_slots = sb("w1_slots", [P, KC, 2 * DFF])
        w2_slots = sb("w2_slots", [P, 4, 2048])
        cst = sb("cst", [P, C_N])
        parms, taps_r, sgub_r = colsT[:, 0, 0:P], colsT[0:2 * TAPS, 1, 0:P], colsT[0:NH, 2, 0:P]
        buckets = colsT[0:NBUCK + 1, 3:5, :].rearrange("p a s -> p (a s)")[:, 0:NDIST]
        sguw_r = colsT[:, 5, :].rearrange("p (h j) -> p h j", h=NH)
        pc = sb("pc", [P, R_N + 2 * TAPS])
        taps = pc[:, R_N:R_N + 2 * TAPS]
        cond = sb("cond", [P, KC])
        mod = sb("mod", [P, 48])
        gs1 = sb("gs1", [P, KC])
        gs2 = sb("gs2", [P, KC])
        st = sb("st", [P, 160])
        lrows = sb("lrows", [P, 5, GW])
        sgub = sb("sgub", [P, NH])
        relb = sb("relb", [NBUCK + 1, NH])
        rw_sb = sb("rw_sb", [P, KC, NE])
        rb_sb = sb("rb_sb", [P, NE])

        def view(kb, n):
            return arena[:, kb * 256:kb * 256 + n]

        x_sb = view(0, NT * D).rearrange("p (t c) -> p t c", t=NT)
        bias_t = view(0, NH * S).rearrange("p (h m) -> p h m", h=NH)
        prob = view(8, 2 * S).rearrange("p (b m) -> p b m", b=2)
        pool_a, pool_b = view(48, S), view(50, S)
        probT = view(12, 2 * S).rearrange("p (b m) -> p b m", b=2)
        pT = view(16, 10 * S).rearrange("p (j s) -> p j s", j=10)
        pR = view(36, NT * 768).rearrange("p (t c) -> p t c", t=NT)
        acc0 = view(48, 2048)
        ypad = view(48, 2 * (PADT + S)).rearrange("p (c s) -> p c s", c=2)
        acc1, acc2 = view(8, 2048), view(56, 2048)
        wmixT = view(53, NH * P).rearrange("p (h i) -> p h i", h=NH)
        poolw = view(55, 2 * P).rearrange("p (c d) -> p c d", c=2)
        gate2 = view(56, D)
        bias_row = view(40, NDIST)[0:NH, :]
        dense = pT[:, 2:4, :].rearrange("p c s -> p (c s)")
        sqv = pT[:, 0:2, :].rearrange("p c s -> p (c s)")
        b_f32 = view(0, 3072)
        gate2 = view(12, D)
        x1 = view(18, NT * D).rearrange("p (t c) -> p t c", t=NT)
        g2row = view(34, D)
        gs2_row, sh2_row = view(38, D), view(42, D)
        gated = view(46, D)
        gate1 = view(50, D)
        sq_dump = view(52, GW)
        b_bf = view(57, 1536).bitcast(BF16)[0:96, :]
        HI, LO = 0, 1
        NRING = 3
        w1_at, w2_at = arena_at + 64 * 1024, arena_at + 128 * 1024
        wo_hi = nc.alloc_sbuf_tensor_at("wo_hi", [P, 4, 2048], F32R, offset=w1_at)
        wo_lo = nc.alloc_sbuf_tensor_at("wo_lo", [P, 4, 2048], F32R, offset=w2_at)
        mixT_hi = nc.alloc_sbuf_tensor_at("mixT_hi", [P, KC, S], F32R, offset=hl_at + 16 * 1024)
        mixT_f = w1_slots[:, 4, :].rearrange("p (b k q) -> p b k q", b=2, k=KC)
        mixT_lo = nc.alloc_sbuf_tensor_at("mixT_lo", [P, 2, KC, P], F32R, offset=w1_at + 32 * 1024)
        w_ring = nc.alloc_sbuf_tensor_at("w_ring", [P, NRING, 2, 2048], F32R, offset=hl_at)
        a_g, a_s, a_l = (view(16 + 4 * i, DFF) for i in range(3))
        aT = nc.alloc_sbuf_tensor_at("aT", [P, 2, KC, P], F32R, offset=arena_at + 28 * 1024)
        xT = nc.alloc_sbuf_tensor_at("xT", [P, 2, KC, P], F32R, offset=arena_at + 36 * 1024)
        xg = view(44, D)
        y_sb = view(48, D)
        hot = view(52, NT * P).rearrange("p (t s) -> p t s", t=NT)
        selA = view(54, P // 2).bitcast(BF16)
        selB = arena[:, 54 * 256 + P // 2:54 * 256 + P].bitcast(BF16)
        fin_x1 = w1_slots[:, 0:2, :].rearrange("p a (b n) -> p (a b) n", b=2)
        fin_gate2, fin_g = w1_slots[:, 2, 0:D], w1_slots[:, 2, D:2 * D]
        fin_sq = w1_slots[:, 3, 0:D]
        hotT = view(36, S).rearrange("p (t q) -> p t q", t=NT)
        fin_y = [(w1_slots[:, 4:6, :], w1_slots[:, 6:8, :], w2_slots[:, 0:2, :], w2_slots[:, 2:4, :])[t] for t in range(NT)]
        routing = view(50, 1024)

        lg = routing[:, 0:NT * NE].rearrange("p (t e) -> p t e", t=NT)
        memb = routing[:, 128:256].rearrange("p (t e) -> p t e", t=NT)
        pos = view(63, 128).rearrange("p (t e) -> p t e", t=NT)
        eq4, tmp4 = (view(46 + 2 * i, NT * NE * TOPK).rearrange("p (t e k) -> p t e k", t=NT, e=NE) for i in range(2))
        v8 = routing[:, 640:672].rearrange("p (t k) -> p t k", t=NT)
        i8 = routing[:, 672:704].bitcast(U32).rearrange("p (t k) -> p t k", t=NT)
        i8f = routing[:, 704:736].rearrange("p (t k) -> p t k", t=NT)
        gk = routing[:, 736:752].rearrange("p (t k) -> p t k", t=NT)
        gsum = routing[:, 752:756]
        cnt = routing[:, 768:800]
        nblk = routing[:, 800:832]
        bend = routing[:, 832:864]
        bstart = routing[:, 864:896]
        slot_no = arena[:, 63 * 256 + 128:64 * 256]
        vtab = view(55, NT * NE * 4).rearrange("p (t e c) -> p t e c", t=NT, c=4)
        egf = sb("egf", [P, MAXBLK])
        egi = sb("egi", [P, MAXBLK], U32)
        bendi = sb("bendi", [P, NE + 2], U32)
        idx_out = sb("idx_out", [P, MAXBLK], U32)
        idx_tok = sb("idx_tok", [P, MAXBLK], U32)
        gcol = sb("gcol", [P, MAXBLK])
        cur_out = sb("cur_out", [P, 1], U32)
        cur_tok = sb("cur_tok", [P, 1], U32)
        cmp_be = view(0, MAXBLK * NE).rearrange("p (b e) -> p b e", b=MAXBLK)

        ps = ctx.enter_context(nc.psum_tensor("ps", [P, 8, 512], F32))

        bias_d = nc.dram_tensor("bias_scratch", [NH, NDIST], F32).ap()
        skew_d = nc.dram_tensor("skew_scratch", [NH, P, NDIST], F32).ap()
        h2_d = nc.dram_tensor("h2_scratch", [S, D], F32).ap()
        x1_d = nc.dram_tensor("x1_scratch", [S, D], F32).ap()
        g2_d = nc.dram_tensor("gate2_scratch", [1, D], F32).ap()
        ys_d = nc.dram_tensor("ys_scratch", [S * TOPK, D], F32).ap()

        ident = cst[:, C_ID:C_ID + P]
        ones = cst[:, C_ONES:C_ONES + P]
        eps = cst[:, C_EPS:C_EPS + 1]

        def col(r):
            return pc[:, r:r + 1]

        l_cst, l_par, l_x, l_row = (sem("l_" + n) for n in ("cst", "par", "x", "row"))
        l_w1 = [sem(f"l_w1_{k}") for k in range(KC)]
        l_w2 = [sem(f"l_w2_{c}") for c in range(4)]
        l_bt, l_gate, l_x1, l_be, l_pw = (sem("l_" + n) for n in ("bt", "gate", "x1", "be", "pw"))
        l_fin = [sem(f"l_fin_{t}") for t in range(NT)]
        st_bias, st_h2, st_out = (sem("st_" + n) for n in ("bias", "h2", "out"))
        names = """e_act e_glu m_modA t_par c_par c_cond a_ss v_var a_sd v_xn t_bias c_bias v_mod0 m_mod0 c_mod t_hT a_hT
                   p_proj a_scaled g_added m_mod c_mod12 t_wmix c_wmix g_pw v_conv t_conv
                   v_convE g_poolT g_chain m_pool v_cen v_sgu m_sgu v_sguE s_att v_att a_att t_att a_attT o_att v_attO
                   v_cx a_silu v_mixed t_mixT v_mixT m_out v_x1 v_h2 t_h2T a_h2T m_lg v_gexp a_gexp v_memb m_cnt m_rank
                   v_tables g_bf v_chain t_rows2 a_rows2 a_woH g_woL""".split()
        s = {n: sem(n) for n in names}
        h_w1, h_w2, d_w1, d_w2, p_w1, p_w2 = (sem(n) for n in ("h_w1", "h_w2", "d_w1", "d_w2", "p_w1", "p_w2"))
        q_w1, q_w2, g_xg, b_yfree = (sem(n) for n in ("q_w1", "q_w2", "g_xg", "b_yfree"))
        st_x1, st_g2 = sem("st_x1"), sem("st_g2")
        (b_hot, b_tab, b_idx, b_gat, b_xps, b_xH, b_xL, b_min, b_sig, b_hread, b_act, b_aps, b_aH, b_aL, b_yev, b_sca,
         b_selA, b_selB, b_chain, b_cur, b_curs, b_lin, b_issued) = (sem("b_" + n) for n in (
             "hot", "tab", "idx", "gat", "xps", "xH", "xL", "min", "sig", "hread", "act", "aps", "aH", "aL", "yev",
             "sca", "selA", "selB", "chain", "cur", "curs", "lin", "issued"))
        f_ld, f_pair, f_sum, f_sq, f_sd, f_o, f_zero, f_hot, f_turn, f_hotT, f_y, f_last, f_clear, f_base = (sem("f_" + n) for n in (
            "ld", "pair", "sum", "sq", "sd", "o", "zero", "hot", "turn", "hotT", "y", "last", "clear", "base"))

        x_rows = a["x"].rearrange("b (t p) d -> p (b t) d", p=P)
        wmod_r = a["w_mod"].rearrange("l (k p) (g n) -> (l k) p g n", p=P, g=6)
        win_r = a["w_in"].rearrange("l (k p) n -> (l k) p n", p=P)
        wout_r = a["w_out"].rearrange("l (c j p) n -> (l c) p j n", p=P, j=2)
        w1_r = a["exp_w1"].rearrange("l e (k p) n -> (l e) k p n", p=P)
        w2_r = a["exp_w2"].rearrange("l e (c p j) n -> (l e) c p (j n)", p=P, j=2)
        ys_r = ys_d.rearrange("(t p k) d -> t p (k d)", p=P, k=TOPK)
        out_r = out_d.rearrange("b (t p) d -> (b t) p d", p=P)
        N_PAR = 12

        def part(t):
            return slice(P * t, P * (t + 1))

        PROJ = [("g", 0, 2), ("a", 0, 0), ("g", 1, 3), ("a", 1, 1), ("f", 4, 4), ("f", 5, 5), ("f", 6, 6), ("f", 7, 7)]
        PROJ += [("v", t, None) for t in range(NT)]
        PROJ += [("f", 8, 10), ("f", 9, 11)]
        PROJ += [("s", t, None) for t in range(NT)]
        NPROJ = len(PROJ)
        BASE = 12

        TURN = (0, 1, 6, 7)

        def proj_bank(i):
            return ps[:, 2 + i % 4 if i < BASE else 4 + i % 2, :]

        ATT = [(h, q) for q in range(NT) for h in range(NH)]
        NA = len(ATT)

        def settle(eng):
            eng.wait_ge(s["v_tables"], 1)

        block = ctx.enter_context(nc.Block())

        @block.sync
        def _(sp):
            sp.dma_start(cst[:], consts_d).then_inc(l_cst, 16)
            for r, name in ((R_C, "c"), (R_N1, "norm1_g"), (R_N2, "norm2_g"), (R_MIX, "mix_out_g"), (R_CB, "conv_b")):
                n = a[name].shape[1] // P
                sp.dma_start(parms[r:r + n, :], a[name].rearrange("l (r q) -> (l r) q", q=P)).then_inc(l_par, 16)
            sp.dma_start(parms[R_BMOD:R_BMOD + 48, :], a["b_mod"].rearrange("l (r q) -> (l r) q", q=P)).then_inc(l_par, 16)
            sp.dma_start(taps_r[:], a["conv_w"].rearrange("l t (h q) -> (l t h) q", q=P)).then_inc(l_par, 16)
            sp.dma_start(sgub_r[:], a["sgu_b"].rearrange("l h q -> (l h) q")).then_inc(l_par, 16)
            sp.dma_start(relb[0:NBUCK, :], a["rel_bias"]).then_inc(l_par, 16)
            sp.dma_start(relb[NBUCK:NBUCK + 1, :], consts_d[0:1, C_ONES:C_ONES + NH]).then_inc(l_par, 16)
            sp.dma_start(buckets, buckets_d).then_inc(l_par, 16)
            sp.dma_start(sguw_r, a["sgu_w"].rearrange("l h i j -> i (l h) j")).then_inc(l_par, 16)
            for k in range(KC):
                sp.dma_start(w1_slots[:, k, :].rearrange("p (g n) -> p g n", g=2), wmod_r[k][:, 0:2, :]).then_inc(l_w1[k], 16)
                if k == 1:
                    sp.dma_start(x_sb, x_rows).then_inc(l_x, 16)
            for k in range(KC):
                sp.wait_ge(s["v_mod0"], k + 1)
                sp.dma_start(w1_slots[:, k, :], win_r[k]).then_inc(l_w1[k], 16)
            for i in range(2 * KC):
                if i >= 4:
                    sp.wait_ge(s["g_added"], i - 3)
                dst = w2_slots[:, i % 4, :].rearrange("p (g n) -> p g n", g=2)
                if i < KC:
                    sp.dma_start(dst, wmod_r[i][:, 3:5, :]).then_inc(l_w2[i % 4], 16)
                else:
                    sp.dma_start(dst[:, 0, :], wmod_r[i - KC][:, 2, :]).then_inc(l_w2[i % 4], 16)
                    sp.dma_start(dst[:, 1, :], wmod_r[i - KC][:, 5, :]).then_inc(l_w2[i % 4], 16)
            for c in range(4):
                sp.wait_ge(s["g_added"], 2 * KC - 3 + c)
                sp.dma_start(w2_slots[:, c, :].rearrange("p (j n) -> p j n", j=2), wout_r[c]).then_inc(l_w2[c], 16)
            for k in range(5, KC):
                sp.wait_ge(s["p_proj"], NPROJ)
                sp.dma_start(w1_slots[:, k, :], w1_r[0, k]).then_inc(l_w1[k], 16)
            for t in range(NT):
                if t == NT - 1:
                    for k in range(5):
                        sp.wait_ge(s["m_out"], 2 * NT)
                        sp.dma_start(w1_slots[:, k, :], w1_r[0, k]).then_inc(l_w1[k], 16)
                sp.wait_ge(s["v_h2"], t + 1)
                sp.dma_start(h2_d[part(t), :], rows[:, t, :]).then_inc(st_h2, 16)
            for t in range(NT):
                sp.dma_start(x1_d[part(t), :], x1[:, t, :]).then_inc(st_x1, 16)
            sp.dma_start(g2_d, gate2[0:1, :]).then_inc(st_g2, 16)
            sp.wait_ge(s["v_tables"], 1)
            e_first = sp.value_load(egi[0:1, 0:1], min_val=0, max_val=NE - 1)
            for c in range(4):
                sp.dma_start(w2_slots[:, c, :], w2_r[e_first, c]).then_inc(l_w2[c], 16)

            def load_w1(e, ge):
                for k in range(KC):
                    sp.wait_ge(d_w1, ge * KC + (k + 1))
                    settle(sp)
                    sp.wait_ge(p_w1, ge * KC + (k + 1))
                    settle(sp)
                    sp.wait_ge(l_w1[k], 16 * (e + 2))
                    settle(sp)
                    sp.dma_start(w1_slots[:, k, :], w1_r[e, k]).then_inc(l_w1[k], 16)

            ge0 = sp.value_load(bendi[0:1, 0:1], min_val=0, max_val=MAXBLK - 1)
            load_w1(1, ge0)
            with sp.Fori(2, NE) as e:
                ge_w1 = sp.value_load(bendi[0:1, bass.ds(e - 1, 1)], min_val=0, max_val=MAXBLK - 1)
                load_w1(e, ge_w1)
            last = sp.value_load(bendi[0:1, NE:NE + 1], min_val=0, max_val=MAXBLK - 2)
            sp.wait_ge(d_w1, last * KC + 2 * KC)
            sp.wait_ge(p_w1, last * KC + 2 * KC)
            for k in range(KC):
                sp.wait_ge(l_w1[k], 16 * (NE + 2))
            sp.wait_ge(st_x1, 16 * NT)
            sp.wait_ge(st_g2, 16)
            sp.dma_start(fin_x1, x1_d.rearrange("(t p) d -> p t d", p=P)).then_inc(f_ld, 16)
            sp.dma_start(fin_gate2, g2_d.to_broadcast([P, D])).then_inc(f_ld, 16)
            sp.dma_start(fin_g, a["final_norm_g"].rearrange("(l d) -> l d", l=1).to_broadcast([P, D])).then_inc(f_ld, 16)
            sp.wait_ge(f_zero, 16)
            sp.wait_ge(b_sca, last * 16)
            settle(sp)
            for t in range(NT):
                if t == 2:
                    sp.wait_ge(d_w2, last * 4 + 8)
                    settle(sp)
                    sp.wait_ge(p_w2, last * 4 + 8)
                    settle(sp)
                sp.dma_start(fin_y[t], ys_r[t].rearrange("p (a b) -> p a b", a=2)).then_inc(l_fin[t], 16)
            for t in range(NT):
                sp.wait_ge(f_o, t + 1)
                sp.dma_start(out_r[t], fin_x1[:, t, :]).then_inc(st_out, 16)
            sp.wait_ge(st_out, 16 * NT)

        @block.gpsimd
        def _(pool):
            for i, name in enumerate(("conv_norm_g", "conv_norm_b", "pool_scale", "sgu_norm_g", "sgu_norm_b")):
                pool.dma_start(lrows[:, i, :], a[name].to_broadcast([P, GW])).then_inc(l_row, 16)
            pool.dma_start(rb_sb[:], a["router_b"].to_broadcast([P, NE])).then_inc(l_row, 16)
            pool.dma_start(rw_sb[:], a["router_w"].rearrange("l (k p) e -> p (l k) e", p=P)).then_inc(l_row, 16)
            pool.wait_ge(s["c_bias"], 1)
            pool.dma_start(bias_d, bias_row).then_inc(st_bias, 16)
            pool.wait_ge(s["v_xn"], NT)
            pool.wait_ge(st_bias, 16)
            for h in range(NH):
                pool.dma_start(skew_d[h], bias_d[h:h + 1, :].to_broadcast([P, NDIST])).then_inc(st_bias, 16)
            pool.wait_ge(st_bias, 80)
            pool.dma_start(bias_t, bass.AP(tensor=skew_d.tensor, offset=P - 1,
                                           ap=[[NDIST - 1, P], [P * NDIST, NH], [1, S]])).then_inc(l_bt, 16)
            pool.wait_ge(s["m_mod0"], 1)
            nc.gpsimd.memset(poolw, 0.0).then_inc(s["g_pw"], 1)
            pool.wait_ge(s["g_pw"], 1)
            for g in range(4):
                q = slice(64 * (g % 2), 64 * (g % 2) + 64)
                pool.dma_start(poolw[q, g // 2, q], a["pool_w"][0, g]).then_inc(l_pw, 16)
            for i in range(2 * KC):
                pool.wait_ge(s["a_scaled"], i + 1)
                acc = acc1 if i < KC else acc2
                if i % KC == 0:
                    continue
                if i % KC == 1:
                    nc.gpsimd.tensor_tensor(acc, w2_slots[:, (i - 1) % 4, :], w2_slots[:, i % 4, :], ALU.add).then_inc(s["g_added"], 2)
                else:
                    pool.wait_ge(s["g_added"], i)
                    nc.gpsimd.tensor_tensor(acc, acc, w2_slots[:, i % 4, :], ALU.add).then_inc(s["g_added"], 1)
            G = nc.gpsimd
            chain = [0]

            def link(ins):
                chain[0] += 1
                ins.then_inc(s["g_chain"], 1)
                pool.wait_ge(s["g_chain"], chain[0])

            def double(dst, src, lag, half):
                q = slice(64, P) if half else slice(0, P)
                link(G.tensor_copy(dst[q, 0:lag], src[q, 0:lag]))
                link(G.tensor_tensor(dst[q, lag:S], src[q, lag:S], src[q, 0:S - lag], ALU.add))

            def pooled(c, lo, hi):
                for q, src in ((slice(0, 64), lo), (slice(64, P), hi)):
                    z = pT[q, 8 + c, :]
                    link(G.tensor_tensor(src[q, 0:16], src[q, 0:16], cst[q, C_RC + 16 * c:C_RC + 16 * c + 16], ALU.mult))
                    link(G.tensor_tensor(src[q, 16:S], src[q, 16:S], cst[q, C_RW + c:C_RW + c + 1].to_broadcast([64, S - 16]),
                                         ALU.mult))
                    link(G.tensor_tensor(z, src[q, :], z, ALU.subtract))

            pool.wait_ge(s["e_act"], BASE)
            pool.wait_ge(s["v_conv"], 2 * TAPS)
            double(pool_a, pT[:, 8, :], 1, False)
            double(pool_b, pool_a, 2, True)
            pooled(0, pool_a, pool_b)
            double(pool_a, pT[:, 9, :], 1, False)
            double(pool_b, pool_a, 2, False)
            double(pool_a, pool_b, 4, False)
            double(pool_b, pool_a, 8, True)
            pooled(1, pool_a, pool_b)
            pool.sem_inc(s["g_poolT"], 1)
            for c in range(4):
                pool.wait_ge(s["a_woH"], c + 1)
                G.tensor_tensor(wo_lo[:, c, :], w2_slots[:, c, :], wo_hi[:, c, :].bitcast(F32), ALU.subtract).then_inc(s["g_woL"], 1)
            pool.wait_ge(s["v_attO"], NA)
            pool.wait_ge(s["v_sguE"], 8)
            pool.wait_ge(s["v_convE"], 1)
            pool.wait_ge(s["a_ss"], NT + 16)
            pool.dma_start(gate1, a["b_mod"][:, 2 * D:3 * D].to_broadcast([P, D])).then_inc(l_gate, 16)
            pool.dma_start(g2row, a["b_mod"][:, 5 * D:6 * D].to_broadcast([P, D])).then_inc(l_gate, 16)
            pool.dma_start(x1, x_rows).then_inc(l_x1, 16)
            pool.wait_ge(s["m_mod"], 2)
            for j in range(3):
                pool.dma_start(b_f32[32 * j:32 * j + 32, 0:2048], a["exp_b1"][0]).then_inc(l_be, 16)
                pool.dma_start(b_f32[32 * j:32 * j + 32, 2048:3072], a["exp_b2"][0]).then_inc(l_be, 16)
            pool.wait_ge(s["g_bf"], 1)
            nc.gpsimd.tensor_tensor(b_f32[0:96, :], b_f32[0:96, :], b_bf, ALU.subtract).then_inc(s["g_bf"], 1)
            pool.wait_ge(s["g_bf"], 4)
            nc.gpsimd.tensor_tensor(b_f32[64:96, :], b_f32[64:96, :], b_bf[64:96, :], ALU.subtract).then_inc(s["g_bf"], 1)

            def gather(g):
                pool.wait_ge(b_idx, g + 1)
                nc.gpsimd.tensor_copy(cur_tok[:], idx_tok[:, bass.ds(g, 1)]).then_inc(b_cur, 1)
                pool.wait_ge(b_cur, g + 1)
                pool.sem_inc(b_issued, 1)
                pool.indirect_dma_start(xg, None, h2_d, bass.IndirectOffsetOnAxis(ap=cur_tok[:], axis=0),
                                        bounds_check=S - 1, oob_is_err=False).then_inc(b_gat, 16)

            def scatter(g):
                pool.wait_ge(b_yev, g + 2)
                nc.gpsimd.tensor_copy(cur_out[:], idx_out[:, bass.ds(g, 1)]).then_inc(b_curs, 1)
                pool.wait_ge(b_curs, g + 1)
                pool.sem_inc(b_issued, 1)
                pool.indirect_dma_start(ys_d, bass.IndirectOffsetOnAxis(ap=cur_out[:], axis=0), y_sb, None,
                                        bounds_check=S * TOPK - 1, oob_is_err=False).then_inc(b_sca, 16)

            pool.wait_ge(st_h2, 16 * NT)
            pool.wait_ge(s["v_tables"], 1)
            last_b = pool.value_load(bendi[0:1, NE:NE + 1], min_val=0, max_val=MAXBLK - 2)
            prev_b = pool.value_load(bendi[0:1, NE + 1:NE + 2], min_val=0, max_val=MAXBLK - 3)
            Q = slice(1536, 2048)

            def low_w1(g, k, off=0):
                pool.wait_ge(h_w1, g * KC + (k + 1))
                r = (k + off) % NRING
                nc.gpsimd.tensor_tensor(w_ring[:, r, LO, Q], w1_slots[:, k, Q], w_ring[:, r, HI, Q].bitcast(F32),
                                        ALU.subtract).then_inc(p_w1, 1)

            def low_w2(g, c):
                pool.wait_ge(h_w2, g * 4 + (c + 1))
                r = (KC + c) % NRING
                nc.gpsimd.tensor_tensor(w_ring[:, r, LO, Q], w2_slots[:, c, Q], w_ring[:, r, HI, Q].bitcast(F32),
                                        ALU.subtract).then_inc(p_w2, 1)

            def step(g, sca=True, w2=True, off=0):
                for k in range(KC):
                    low_w1(g, k, off)
                    if k == 3 and sca:
                        scatter(g - 2)
                    if k == 5:
                        if isinstance(g, int) and g == 0:
                            pool.wait_ge(b_xps, 1)
                        gather(g + 1)
                if w2:
                    for c in range(4):
                        low_w2(g - 1, c)
                if sca:
                    pool.wait_ge(b_sca, g * 16 - 16)
                    pool.sem_inc(b_yfree, 1)
                pool.wait_ge(b_gat, g * 16 + 32)

            nc.gpsimd.memset(xg, 0.0).then_inc(g_xg, 1)
            pool.wait_ge(g_xg, 1)
            gather(0)
            pool.wait_ge(b_gat, 16)
            step(0, sca=False, w2=False, off=1)
            step(1, sca=False)
            with pool.Fori(2, last_b + 1) as g:
                step(g)
            pool.wait_ge(b_xps, last_b + 2)
            pool.sem_inc(b_issued, 1)
            nc.gpsimd.memset(xg, 0.0).then_inc(f_clear, 1)
            nc.gpsimd.tensor_copy(cur_tok[:], idx_out[:, bass.ds(last_b, 1)]).then_inc(b_cur, 1)
            pool.wait_ge(b_cur, last_b + 3)
            pool.sem_inc(b_issued, 1)
            pool.wait_ge(f_clear, 1)
            pool.indirect_dma_start(ys_d, bass.IndirectOffsetOnAxis(ap=cur_tok[:], axis=0), xg, None,
                                    bounds_check=S * TOPK - 1, oob_is_err=False).then_inc(f_zero, 16)
            pool.wait_ge(f_zero, 16)
            scatter(prev_b)
            for c in range(4):
                low_w2(last_b, c)
            for t in range(NT):
                pool.wait_ge(l_fin[t], 16)
                y4 = fin_y[t].rearrange("p a (b n) -> p (a b) n", b=2)
                if t < NT - 1:
                    nc.gpsimd.tensor_tensor(y4[:, 0:2, :], y4[:, 0:2, :], y4[:, 2:4, :], ALU.add).then_inc(f_pair, 1)
                else:
                    nc.gpsimd.tensor_tensor(y4[:, 2, :], y4[:, 2, :], y4[:, 3, :], ALU.add).then_inc(f_pair, 1)

        @block.scalar
        def _(act):
            act.wait_ge(l_cst, 16)
            act.wait_ge(s["c_par"], 1)
            nc.scalar.activation(cond[:], pc[:, R_C:R_C + KC], ACT.Silu).then_inc(s["c_cond"], 1)
            act.wait_ge(l_x, 16)
            for t in range(NT):
                nc.scalar.activation(rows[:, t, :], x_sb[:, t, :], ACT.Square, accum_out=st[:, t:t + 1]).then_inc(s["a_ss"], 1)

            sq = [0]

            def root(dst, src, n):
                sq[0] += 1
                act.wait_ge(s["v_var"], sq[0])
                nc.scalar.activation(dst, src, ACT.Sqrt, bias=eps, scale=1.0 / n).then_inc(s["a_sd"], 1)


            def own_root(dst, src, n, sums):
                act.wait_ge(s["a_ss"], sums)
                nc.scalar.activation(dst, src, ACT.Sqrt, bias=eps, scale=1.0 / n).then_inc(s["a_sd"], 1)

            own_root(st[:, 4:8], st[:, 0:4], D, NT)
            act.wait_ge(s["c_mod"], 1)
            for k in range(KC):
                act.wait_ge(s["t_hT"], k + 1)
                nc.scalar.activation(colsT[:, k, :], ps[:, TURN[k % 4], :], ACT.Identity, bias=mod[:, k:k + 1],
                                     scale=gs1[:, k:k + 1]).then_inc(s["a_hT"], 1)

            def evac(i):
                kind, n, _ = PROJ[i]
                bank = proj_bank(i)
                if kind != "a":
                    act.wait_ge(s["p_proj"], i + 1)
                if kind == "g":
                    nc.scalar.activation(pT[:, 2 + n, :], bank, ACT.Sigmoid).then_inc(s["e_act"], 1)
                elif kind == "f":
                    nc.scalar.activation(pT[:, n, :], bank, ACT.Copy).then_inc(s["e_act"], 1)
                elif kind == "v":
                    act.wait_ge(st_bias, 16)
                    nc.scalar.activation(pR[:, n, 0:GW], bank[:, 0:GW], ACT.Copy).then_inc(s["e_act"], 1)
                elif kind == "s":
                    nc.scalar.activation(pR[:, n, GW:3 * GW], bank, ACT.Gelu).then_inc(s["e_act"], 1)

            def scale_chunk(c):
                act.wait_ge(l_w2[c % 4], 16 * (c // 4 + 1) if c < KC else 32 * (c // 4))
                nc.scalar.activation(w2_slots[:, c % 4, :], w2_slots[:, c % 4, :], ACT.Copy,
                                     scale=cond[:, c % KC:c % KC + 1]).then_inc(s["a_scaled"], 1)

            for c in range(4):
                scale_chunk(c)
            scaled = 4
            for i, until in enumerate((4, 4, 4, 5, 7, 8, 10, 12, 12, 13, 14, 16)):
                evac(i)
                for c in range(scaled, until):
                    scale_chunk(c)
                scaled = until

            def att_exp(i):
                h, q = ATT[i]
                n = P * (q + 1)
                act.wait_ge(s["v_att"], i + 1)
                nc.scalar.activation(prob[:, i % 2, 0:n], prob[:, i % 2, 0:n], ACT.Exp, bias=st[:, 64 + i:65 + i],
                                     accum_out=st[:, 80 + i:81 + i]).then_inc(s["a_att"], 1)

            def att_evac(i):
                n = P * (ATT[i][1] + 1)
                act.wait_ge(s["t_att"], i + 1)
                if i >= 2:
                    act.wait_ge(s["o_att"], i - 1)
                nc.scalar.activation(probT[:, i % 2, 0:n], ps[:, i % 2, 0:n], ACT.Copy).then_inc(s["a_attT"], 1)

            squares = [NT]

            def square(t, m):
                act.wait_ge(s["a_ss"], squares[0])
                nc.scalar.activation(sq_dump, rows[:, t, GW * m:GW * m + GW], ACT.Square,
                                     accum_out=st[:, 96 + 4 * t + m:97 + 4 * t + m]).then_inc(s["a_ss"], 1)
                squares[0] += 1

            for i in range(NA + 1):
                if i < NA:
                    att_exp(i)
                if i == 1:
                    root(st[:, 32:48], st[:, 16:32], HD)
                if i == 3:
                    act.wait_ge(s["v_cx"], 1)
                    nc.scalar.activation(rows[:, :, 0:GW], rows[:, :, 0:GW], ACT.Silu).then_inc(s["a_silu"], 1)
                if i == 9:
                    root(st[:, 52:54], st[:, 48:50], GW)
                if i == 13:
                    root(st[:, 54:56], st[:, 50:52], GW)
                if i >= 1:
                    att_evac(i - 1)
                for j in range(NPROJ - BASE):
                    if (KC * j + KC - 1) // 4 == i:
                        evac(BASE + j)
                if 4 <= i < 8:
                    act.wait_ge(s["a_silu"], 1)
                    square(i - 4, 0)
                if i in (6, 10, 14):
                    act.wait_ge(s["v_attO"], i - 2)
                    square((i - 6) // 4, 1)
                if 12 <= i < 16:
                    c = i - 12
                    act.wait_ge(s["p_proj"], NPROJ)
                    act.wait_ge(l_w2[c], 112)
                    nc.scalar.activation(wo_hi[:, c, :], w2_slots[:, c, :], ACT.Copy).then_inc(s["a_woH"], 1)
                if i in (14, 15):
                    act.wait_ge(s["v_convE"], 1)
                    square(2 * (i - 14), 2)
                    square(2 * (i - 14) + 1, 2)
            for t in range(NT):
                act.wait_ge(s["v_sguE"], 4 if t < 2 else 8)
                if t == NT - 1:
                    act.wait_ge(s["v_attO"], NA)
                    square(t, 1)
                square(t, 3)
                own_root(st[:, 112 + 4 * t:116 + 4 * t], st[:, 96 + 4 * t:100 + 4 * t], GW, squares[0])
            act.wait_ge(s["t_rows2"], 1)
            nc.scalar.activation(gs2_row.rearrange("p (b n) -> p b n", b=2), ps[:, 6:8, :], ACT.Copy).then_inc(s["a_rows2"], 1)
            def h2T_evac(t):
                act.wait_ge(s["t_h2T"], t + 1)
                nc.scalar.activation(colsT[:, :, part(t)], ps[:, 6:8, :].rearrange("p b (c q) -> p (b c) q", c=4),
                                     ACT.Copy).then_inc(s["a_h2T"], 1)

            act.wait_ge(l_be, 96)
            act.wait_ge(s["m_mod"], 2)
            nc.scalar.activation(b_bf, b_f32[0:96, :], ACT.Copy).then_inc(s["g_bf"], 1)
            for t in range(NT):
                if t == 1:
                    act.wait_ge(s["g_bf"], 2)
                    nc.scalar.activation(b_bf[32:64, :], b_f32[32:64, :], ACT.Copy).then_inc(s["g_bf"], 1)
                    nc.scalar.activation(b_bf[64:96, :], b_f32[64:96, :], ACT.Copy).then_inc(s["g_bf"], 1)
                if t == 2:
                    act.wait_ge(s["g_bf"], 5)
                    nc.scalar.activation(b_bf[64:96, :], b_f32[64:96, :], ACT.Copy).then_inc(s["g_bf"], 1)
                if t == NT - 1:
                    h2T_evac(t - 1)
                act.wait_ge(s["v_x1"], t + 1)
                nc.scalar.activation(rows[:, t, :], x1[:, t, :], ACT.Square, accum_out=st[:, 128 + t:129 + t]).then_inc(s["a_ss"], 1)
                own_root(st[:, 132 + t:133 + t], st[:, 128 + t:129 + t], D, NT + 16 + t + 1)
                if t == 0:
                    act.wait_ge(s["t_rows2"], 2)
                    nc.scalar.activation(sh2_row.rearrange("p (b n) -> p b n", b=2), ps[:, 6:8, :], ACT.Copy).then_inc(s["a_rows2"], 1)
                if 1 <= t < NT - 1:
                    h2T_evac(t - 1)
            h2T_evac(NT - 1)
            act.wait_ge(s["v_gexp"], 1)
            nc.scalar.activation(gk[:], gk[:], ACT.Exp).then_inc(s["a_gexp"], 1)

            act.wait_ge(s["v_tables"], 1)
            last_b = act.value_load(bendi[0:1, NE:NE + 1], min_val=0, max_val=MAXBLK - 2)
            prev_b = act.value_load(bendi[0:1, NE + 1:NE + 2], min_val=0, max_val=MAXBLK - 3)

            def high_x(g):
                act.wait_ge(b_xps, g + 1)
                for j in range(2):
                    last = nc.scalar.activation(xT[:, HI, 4 * j:4 * j + 4, :],
                                                ps[:, 6 + j, :].rearrange("p (c q) -> p c q", c=4), ACT.Copy)
                last.then_inc(b_xH, 1)

            def high_a(n):
                act.wait_ge(b_aps, n)
                for j in range(2):
                    last = nc.scalar.activation(aT[:, HI, 4 * j:4 * j + 4, :],
                                                ps[:, 6 + j, :].rearrange("p (c q) -> p c q", c=4), ACT.Copy)
                last.then_inc(b_aH, 1)

            def sigmoid(g):
                for j in range(2):
                    act.wait_ge(b_min, g * 2 + (j + 1))
                    sl = slice(512 * j, 512 * j + 512)
                    nc.scalar.activation(a_s[:, sl], a_g[:, sl], ACT.Sigmoid, scale=ALPHA).then_inc(b_sig, 1)

            def evac_y(n, idx, wait_scatter=True):
                act.wait_ge(q_w2, n * 4)
                if wait_scatter:
                    act.wait_ge(b_yfree, idx + 1)
                nc.scalar.activation(y_sb.rearrange("p (j n) -> p j n", j=2), ps[:, 4:6, :], ACT.Copy,
                                     scale=gcol[:, bass.ds(idx, 1)]).then_inc(b_yev, 1)

            def high_w1(g, k, e, off=0):
                act.wait_ge(l_w1[k], e * 16 + 48)
                nc.scalar.activation(w_ring[:, (k + off) % NRING, HI, :], w1_slots[:, k, :], ACT.Copy).then_inc(h_w1, 1)

            def high_w2(g, c):
                act.wait_ge(l_w2[c], g * 16 + 128)
                nc.scalar.activation(w_ring[:, (KC + c) % NRING, HI, :], w2_slots[:, c, :], ACT.Copy).then_inc(h_w2, 1)

            def expert(g):
                return act.value_load(egi[0:1, bass.ds(g, 1)], min_val=0, max_val=NE - 1)

            def step(g, last_y=True, tail=True, off=0, begin=0):
                e = expert(g)
                for k in range(begin, KC):
                    if k >= 3:
                        act.wait_ge(q_w1, g * KC + (k - 2))
                    elif last_y:
                        act.wait_ge(q_w2, g * 4 + (k - 6))
                    elif tail:
                        act.wait_ge(q_w1, 6 + k)
                    high_w1(g, k, e, off)
                    if k == 2 and last_y:
                        evac_y(g - 1, g - 2, wait_scatter=not (isinstance(g, int) and g <= 2))
                    if k == 7 and tail:
                        high_a(g)
                if tail:
                    for c in range(4):
                        if c < 3:
                            act.wait_ge(q_w1, g * KC + (6 + c))
                        else:
                            act.wait_ge(q_w2, g * 4 - 3)
                        high_w2(g - 1, c)
                high_x(g + 1)
                sigmoid(g)
                if tail:
                    for c in range(4):
                        act.wait_ge(d_w2, g * 4 + (c + 1))
                        settle(act)
                        act.wait_ge(p_w2, g * 4 + (c + 1))
                        settle(act)
                        act.dma_start(w2_slots[:, c, :], w2_r[e, c]).then_inc(l_w2[c], 16)

            act.wait_ge(st_h2, 16 * NT)
            act.wait_ge(st_g2, 16)
            e_first = expert(0)
            for k in range(NRING):
                high_w1(0, k, e_first, off=1)
            high_x(0)
            step(0, last_y=False, tail=False, off=1, begin=NRING)
            step(1, last_y=False)
            with act.Fori(2, last_b + 1) as g:
                step(g)
            evac_y(last_b, prev_b)
            high_a(last_b + 1)
            for c in range(4):
                if c == 3:
                    act.wait_ge(q_w2, last_b * 4 + 1)
                else:
                    act.wait_ge(q_w1, last_b * KC + (6 + c))
                high_w2(last_b, c)
                if c == 2:
                    act.wait_ge(f_turn, 1)
                    nc.scalar.activation(hotT, ps[:, 6, :].rearrange("p (t q) -> p t q", t=NT), ACT.Copy).then_inc(f_hotT, 1)
            for t in range(NT):
                act.wait_ge(f_sum, t + 1)
                nc.scalar.activation(fin_sq, fin_x1[:, t, :], ACT.Square, accum_out=st[:, t:t + 1]).then_inc(f_sq, 1)
                act.wait_ge(f_sq, t + 1)
                nc.scalar.activation(st[:, 4 + t:5 + t], st[:, t:t + 1], ACT.Sqrt, bias=eps, scale=1.0 / D).then_inc(f_sd, 1)

        @block.vector
        def _(dve):
            V = nc.vector
            chain = [0]

            def link(ins):
                chain[0] += 1
                ins.then_inc(s["v_chain"], 1)
                dve.wait_ge(s["v_chain"], chain[0])


            dve.wait_ge(s["t_par"], 3)
            link(V.tensor_copy(pc[:], ps[:, 0, 0:R_N + 2 * TAPS]))
            V.tensor_copy(sgub[:], ps[:, 0, 256:256 + NH]).then_inc(s["c_par"], 1)
            dve.wait_ge(s["c_cond"], 1)
            dve.wait_ge(s["t_bias"], 1)
            V.tensor_copy(bias_row, ps[0:NH, 6:8, :].rearrange("p b m -> p (b m)")[:, 0:NDIST]).then_inc(s["c_bias"], 1)
            for k in range(KC):
                dve.wait_ge(l_w1[k], 16)
                if k == 0:
                    V.tensor_scalar(acc0, w1_slots[:, 0, :], cond[:, 0:1], None, ALU.mult).then_inc(s["v_mod0"], 1)
                else:
                    dve.wait_ge(s["v_mod0"], k)
                    V.scalar_tensor_tensor(acc0, w1_slots[:, k, :], cond[:, k:k + 1], acc0, ALU.mult, ALU.add).then_inc(s["v_mod0"], 1)
                if k == 3:
                    dve.wait_ge(s["a_sd"], 1)
                    link(V.reciprocal(st[:, 8:12], st[:, 4:8]))
                    for t in range(NT):
                        V.tensor_scalar(rows[:, t, :], x_sb[:, t, :], st[:, 8 + t:9 + t], None, ALU.mult).then_inc(s["v_xn"], 1)
            dve.wait_ge(s["m_mod0"], 1)
            link(V.tensor_tensor(mod[:, 0:16], ps[:, 2, 0:16], pc[:, R_BMOD:R_BMOD + 16], ALU.add))
            V.scalar_tensor_tensor(gs1[:], mod[:, 8:16], 1.0, pc[:, R_N1:R_N1 + KC], ALU.add, ALU.mult).then_inc(s["c_mod"], 1)
            dve.wait_ge(s["t_wmix"], 1)
            V.tensor_tensor(wmixT, ps[:, 5, :].rearrange("p (h i) -> p h i", h=NH),
                            cst[:, None, C_TRI:C_TRI + P].to_broadcast([P, NH, P]), ALU.mult).then_inc(s["c_wmix"], 1)
            dve.wait_ge(s["m_mod0"], 1)
            link(V.memset(ypad[:, :, 0:PADT], 0.0))
            for c in range(2):
                dve.wait_ge(s["p_proj"], 2 * c + 2)
                dve.wait_ge(s["e_act"], c + 1)
                V.tensor_tensor(ypad[:, c, PADT:PADT + S], ps[:, 3 + 2 * c, :], pT[:, 2 + c, :], ALU.mult).then_inc(s["e_glu"], 1)
            dve.wait_ge(s["e_glu"], 2)
            for tap in range(TAPS):
                for c in range(2):
                    w = taps[:, 2 * tap + c:2 * tap + c + 1]
                    src = ypad[:, c, tap:tap + S]
                    if tap:
                        dve.wait_ge(s["v_conv"], 2 * tap + c - 1)
                        V.scalar_tensor_tensor(pT[:, c, :], src, w, pT[:, c, :], ALU.mult, ALU.add).then_inc(s["v_conv"], 1)
                    else:
                        V.tensor_scalar(pT[:, c, :], src, w, col(R_CB + c), ALU.mult, ALU.add).then_inc(s["v_conv"], 1)
            dve.wait_ge(s["m_modA"], 1)
            link(V.tensor_tensor(mod[:, 24:40], ps[:, 0, 0:16], pc[:, R_BMOD + 24:R_BMOD + 40], ALU.add))
            V.scalar_tensor_tensor(gs2[:], mod[:, 32:40], 1.0, pc[:, R_N2:R_N2 + KC], ALU.add, ALU.mult).then_inc(s["c_mod12"], 1)

            def centre(dst, src, n, base, g):
                m = st[:, base:base + g]
                link(V.tensor_reduce(m, src, AX.X, ALU.add))
                link(V.tensor_scalar(m, m, -1.0 / n, None, ALU.mult))
                link(V.tensor_tensor(dst, src, m[:, :, None].to_broadcast([P, g, n]), ALU.add))

            dve.wait_ge(s["t_conv"], 1)
            cps = ps[:, 6:8, :].rearrange("p b (t c) -> p (b t) c", t=2).rearrange("p t (h d) -> p (t h) d", h=NH)
            cx = rows[:, :, 0:GW]
            dv = dense.rearrange("p (g n) -> p g n", n=HD)
            d4 = dense.rearrange("p (t c) -> p t c", t=NT)
            centre(dv, cps, HD, 16, 16)
            dve.sem_inc(s["v_cen"], 1)

            def conv_var():
                link(V.tensor_tensor(sqv, dense, dense, ALU.mult))
                V.tensor_reduce(st[:, 16:32], sqv.rearrange("p (g n) -> p g n", n=HD), AX.X, ALU.add).then_inc(s["v_var"], 1)

            def conv_norm():
                dve.wait_ge(s["a_sd"], 2)
                link(V.reciprocal(st[:, 16:32], st[:, 32:48]))
                link(V.tensor_tensor(dv, dv, st[:, 16:32, None].to_broadcast([P, 16, HD]), ALU.mult))
                link(V.tensor_tensor(d4, d4, lrows[:, None, 0, :].to_broadcast([P, NT, GW]), ALU.mult))
                V.tensor_tensor(cx, d4, lrows[:, None, 1, :].to_broadcast([P, NT, GW]), ALU.add).then_inc(s["v_cx"], 1)

            def sgu_var(b):
                t2 = slice(2 * b, 2 * b + 2)
                dve.wait_ge(s["e_act"], BASE + 2 * b + 2)
                dve.wait_ge(s["v_cx"], 1)
                centre(d4[:, t2, :], pR[:, t2, 2 * GW:3 * GW], GW, 48 + 2 * b, 2)
                sq = sqv[:, 512 * b:512 * b + 512]
                link(V.tensor_tensor(sq, dense[:, 512 * b:512 * b + 512], dense[:, 512 * b:512 * b + 512], ALU.mult))
                V.tensor_reduce(st[:, 48 + 2 * b:50 + 2 * b], sq.rearrange("p (g n) -> p g n", n=GW), AX.X, ALU.add).then_inc(s["v_var"], 1)

            def sgu_norm(b):
                t2 = slice(2 * b, 2 * b + 2)
                d = d4[:, t2, :]
                m = st[:, 48 + 2 * b:50 + 2 * b]
                dve.wait_ge(s["a_sd"], 3 + b)
                link(V.reciprocal(m, st[:, 52 + 2 * b:54 + 2 * b]))
                link(V.tensor_tensor(d, d, m[:, :, None].to_broadcast([P, 2, GW]), ALU.mult))
                link(V.tensor_tensor(d, d, lrows[:, None, 3, :].to_broadcast([P, 2, GW]), ALU.mult))
                V.tensor_tensor(pR[:, t2, 2 * GW:3 * GW], d, lrows[:, None, 4, :].to_broadcast([P, 2, GW]), ALU.add).then_inc(s["v_sgu"], 1)

            def att_scores(i):
                h, q = ATT[i]
                n = P * (q + 1)
                dve.wait_ge(s["s_att"], i + 1)
                if i >= 2:
                    dve.wait_ge(s["t_att"], i - 1)
                link(V.scalar_tensor_tensor(prob[:, i % 2, 0:n], ps[:, 6 + h % 2, 0:n], HD ** -0.5,
                                            bias_t[:, h, S - P - P * q:S], ALU.mult, ALU.add))
                V.tensor_reduce(st[:, 64 + i:65 + i], prob[:, i % 2, 0:n], AX.X, ALU.max, negate=True).then_inc(s["v_att"], 1)

            def att_norm(i):
                h, q = ATT[i]
                dve.wait_ge(s["o_att"], i + 1)
                link(V.reciprocal(st[:, 80 + i:81 + i], st[:, 80 + i:81 + i]))
                V.tensor_scalar(rows[:, q, GW + HD * h:GW + HD * h + HD], ps[:, 2 + i % 2, 0:HD], st[:, 80 + i:81 + i],
                                None, ALU.mult).then_inc(s["v_attO"], 1)

            dve.wait_ge(l_bt, 16)
            def normalise(t):
                dve.wait_ge(s["a_sd"], 5 + t)
                root_t = st[:, 112 + 4 * t:116 + 4 * t]
                link(V.reciprocal(root_t, root_t))
                r = rows[:, t, :].rearrange("p (m c) -> p m c", m=4)
                V.tensor_tensor(r, r, root_t[:, :, None].to_broadcast([P, 4, GW]), ALU.mult).then_inc(s["v_mixed"], 1)

            for i in range(NA + 2):
                if i < NA:
                    att_scores(i)
                if i == 1:
                    conv_var()
                if i == 2:
                    conv_norm()
                if i == 8:
                    sgu_var(0)
                if i == 10:
                    sgu_norm(0)
                if i == 12:
                    sgu_var(1)
                if i == 14:
                    sgu_norm(1)
                if i == 13:
                    dve.wait_ge(s["m_pool"], 1)
                    V.tensor_tensor(rows[:, :, 2 * GW:3 * GW], ps[:, 4:6, :].rearrange("p b (t c) -> p (b t) c", t=2),
                                    lrows[:, None, 2, :].to_broadcast([P, NT, GW]), ALU.mult).then_inc(s["v_convE"], 1)
                if i >= 2:
                    att_norm(i - 2)
                if i == NA + 1:
                    normalise(0)
                    normalise(1)
                if i in (15, NA + 1):
                    b = 0 if i == 15 else 1
                    dve.wait_ge(s["m_sgu"], b + 1)
                    t2 = slice(2 * b, 2 * b + 2)
                    for h in range(NH):
                        o = slice(HD * h, HD * h + HD)
                        V.scalar_tensor_tensor(rows[:, t2, 3 * GW + HD * h:3 * GW + HD * h + HD],
                                               ps[:, 4 + b, :].rearrange("p (t c) -> p t c", t=2)[:, :, o], sgub[:, h:h + 1],
                                               pR[:, t2, GW + HD * h:GW + HD * h + HD], ALU.add, ALU.mult).then_inc(s["v_sguE"], 1)

            def mixT_evac(t):
                dve.wait_ge(s["t_mixT"], t + 1)
                if t >= 2:
                    dve.wait_ge(s["m_out"], 2 * t - 2)
                f, lo, hi = mixT_f[:, t % 2, :, :], mixT_lo[:, t % 2, :, :], mixT_hi[:, :, part(t)]
                link(V.tensor_tensor(f, ps[:, 0:2, :].rearrange("p b (c q) -> p (b c) q", c=4),
                                     pc[:, R_MIX:R_MIX + KC, None].to_broadcast([P, KC, P]), ALU.mult))
                link(V.tensor_copy(hi, f))
                V.tensor_tensor(lo, f, hi.bitcast(F32), ALU.subtract).then_inc(s["v_mixT"], 1)

            mixT_evac(0)
            normalise(2)
            normalise(3)
            dve.wait_ge(s["m_mod"], 1)
            dve.wait_ge(l_gate, 32)
            V.tensor_tensor(gate1, gate1, ps[:, 6:8, :].rearrange("p b n -> p (b n)"), ALU.add).then_inc(s["c_mod12"], 1)
            dve.wait_ge(s["m_mod"], 2)
            V.tensor_tensor(gate2, g2row, ps[:, 2:4, :].rearrange("p b n -> p (b n)"), ALU.add).then_inc(s["c_mod12"], 1)
            dve.wait_ge(l_x1, 16)
            for t in range(NT):
                if t + 1 < NT:
                    mixT_evac(t + 1)
                dve.wait_ge(s["m_out"], 2 * t + 2)
                po = ps[:, 4 - 2 * (t % 2):6 - 2 * (t % 2), :].rearrange("p b n -> p (b n)")
                if t == 0:
                    dve.wait_ge(s["c_mod12"], 3)
                link(V.tensor_tensor(gated, po, gate1, ALU.mult))
                V.tensor_tensor(x1[:, t, :], x1[:, t, :], gated, ALU.add).then_inc(s["v_x1"], 1)
                dve.wait_ge(s["v_x1"], t + 1)
                dve.wait_ge(s["a_sd"], 9 + t)
                link(V.reciprocal(st[:, 132 + t:133 + t], st[:, 132 + t:133 + t]))
                if t == 0:
                    dve.wait_ge(s["a_rows2"], 2)
                h2 = rows[:, t, :]
                link(V.scalar_tensor_tensor(h2, x1[:, t, :], st[:, 132 + t:133 + t], gs2_row, ALU.mult, ALU.mult))
                V.tensor_tensor(h2, h2, sh2_row, ALU.add).then_inc(s["v_h2"], 1)
            dve.wait_ge(s["m_lg"], 1)
            link(V.tensor_tensor(lg, ps[:, 0, 0:NT * NE].rearrange("p (t e) -> p t e", t=NT),
                                 rb_sb[:, None, :].to_broadcast([P, NT, NE]), ALU.add))
            for t in range(NT):
                link(V.max(v8[:, t, :], lg[:, t, :]))
                link(V.max_index(i8[:, t, :], v8[:, t, :], lg[:, t, :]))
            link(V.tensor_copy(i8f, i8))
            every = [P, NT, NE, TOPK]
            link(V.tensor_tensor(eq4, cst[:, None, C_IOE:C_IOE + NE, None].to_broadcast(every),
                                 i8f[:, :, None, 0:TOPK].to_broadcast(every), ALU.is_equal))
            V.tensor_reduce(memb, eq4, AX.X, ALU.add).then_inc(s["v_memb"], 1)
            V.tensor_tensor(gk, v8[:, :, 0:TOPK], v8[:, :, 0:1].to_broadcast([P, NT, TOPK]), ALU.subtract).then_inc(s["v_gexp"], 1)
            asg = cst[:, C_ASG:C_ASG + NT * TOPK].rearrange("p (t k) -> p t k", t=NT)
            tab_r, tab_g = vtab[:, :, :, 0], vtab[:, :, :, 2]
            link(V.tensor_tensor(tmp4, eq4, asg[:, :, None, :].to_broadcast(every), ALU.mult))
            link(V.tensor_reduce(tab_r, tmp4, AX.X, ALU.add))
            dve.wait_ge(s["v_memb"], 1)
            link(V.scalar_tensor_tensor(tab_r, memb, -float(EMPTY), tab_r, ALU.mult, ALU.add))
            link(V.tensor_tensor(vtab[:, :, :, 1], memb, cst[:, C_TOK:C_TOK + NT, None].to_broadcast([P, NT, NE]), ALU.mult))
            V.memset(vtab[:, :, :, 3], 0.0)
            dve.wait_ge(s["a_gexp"], 1)
            link(V.tensor_reduce(gsum, gk, AX.X, ALU.add))
            link(V.reciprocal(gsum, gsum))
            link(V.tensor_tensor(gk, gk, gsum[:, :, None].to_broadcast([P, NT, TOPK]), ALU.mult))
            link(V.tensor_tensor(eq4, eq4, gk[:, :, None, :].to_broadcast(every), ALU.mult))
            link(V.tensor_reduce(tab_g, eq4, AX.X, ALU.add))
            dve.wait_ge(s["m_cnt"], 1)
            link(V.tensor_copy(cnt, ps[:, 2, 0:NE]))
            link(V.tensor_scalar(nblk, cnt, 0.0, None, ALU.is_gt))
            for b in range(1, S // P):
                link(V.scalar_tensor_tensor(nblk, cnt, float(P * b), nblk, ALU.is_gt, ALU.add))
            link(V.tensor_tensor_scan(bend, cst[:, C_ONES:C_ONES + NE], nblk, 0.0, ALU.mult, ALU.add))
            link(V.tensor_copy(bendi[:, 0:NE], bend))
            link(V.tensor_scalar(bendi[:, NE:NE + 1], bend[:, NE - 1:NE], 1.0, None, ALU.subtract))
            link(V.tensor_scalar(bendi[:, NE + 1:NE + 2], bend[:, NE - 1:NE], 2.0, None, ALU.subtract))
            link(V.tensor_tensor(bstart, bend, nblk, ALU.subtract))
            link(V.tensor_scalar(bstart, bstart, float(P), 1.0, ALU.mult, ALU.add))
            dve.wait_ge(s["m_rank"], 1)
            link(V.tensor_tensor(pos, ps[:, 3, 0:NT * NE].rearrange("p (t e) -> p t e", t=NT),
                                 bstart[:, None, :].to_broadcast([P, NT, NE]), ALU.add))
            link(V.tensor_tensor(pos, pos, memb, ALU.mult))
            dve.wait_ge(s["g_bf"], 6)
            link(V.tensor_tensor(cmp_be, bend[:, None, :].to_broadcast([P, MAXBLK, NE]),
                                 cst[:, C_IOB:C_IOB + MAXBLK, None].to_broadcast([P, MAXBLK, NE]), ALU.is_le))
            link(V.tensor_reduce(egf[:], cmp_be, AX.X, ALU.add))
            link(V.tensor_scalar(egf[:], egf[:], float(NE - 1), None, ALU.min))
            link(V.tensor_copy(egi[:], egf[:]))
            link(V.tensor_copy(slot_no, cst[:, C_SLOT:C_SLOT + P]))
            V.memset(st[:, 158:159], 0.0).then_inc(s["v_tables"], 1)

            last_b = dve.value_load(bendi[0:1, NE:NE + 1], min_val=0, max_val=MAXBLK - 2)

            def one_hot(g):
                e = dve.value_load(egi[0:1, bass.ds(g, 1)], min_val=0, max_val=NE - 1)
                dve.wait_ge(b_tab, g)
                for t in range(NT):
                    last = V.tensor_scalar(hot[:, t, :], slot_no, pos[:, t, bass.ds(e, 1)], None, ALU.is_equal)
                last.then_inc(b_hot, 1)
                dve.wait_ge(b_hot, g + 1)
                V.tensor_scalar(slot_no, slot_no, float(P), None, ALU.add).then_inc(b_chain, 1)
                dve.wait_ge(b_chain, g + 1)

            def table(g):
                dve.wait_ge(b_tab, g + 1)
                V.tensor_scalar(idx_out[:, bass.ds(g, 1)], ps[:, 6, 0:1], float(EMPTY), None, ALU.add)
                V.tensor_scalar(idx_tok[:, bass.ds(g, 1)], ps[:, 6, 1:2], float(EMPTY), None, ALU.add)
                V.tensor_copy(gcol[:, bass.ds(g, 1)], ps[:, 6, 2:3]).then_inc(b_idx, 1)

            def select(dst, g, signal):
                V.tensor_tensor(dst[0:96, :], cst[0:96, C_PM:C_PM + 1].to_broadcast([96, P]),
                                egf[0:96, bass.ds(g, 1)].to_broadcast([96, P]), ALU.is_equal).then_inc(signal, 1)

            def low_w1(g, k, off=0):
                dve.wait_ge(h_w1, g * KC + (k + 1))
                r = (k + off) % NRING
                V.tensor_tensor(w_ring[:, r, LO, 0:1536], w1_slots[:, k, 0:1536], w_ring[:, r, HI, 0:1536].bitcast(F32),
                                ALU.subtract).then_inc(d_w1, 1)

            def low_w2(g, c):
                dve.wait_ge(h_w2, g * 4 + (c + 1))
                r = (KC + c) % NRING
                V.tensor_tensor(w_ring[:, r, LO, 0:1536], w2_slots[:, c, 0:1536], w_ring[:, r, HI, 0:1536].bitcast(F32),
                                ALU.subtract).then_inc(d_w2, 1)

            def low_x(g):
                dve.wait_ge(b_xH, g + 1)
                V.tensor_tensor(xT[:, LO, :, :].rearrange("p c q -> p (c q)"), ps[:, 6:8, :].rearrange("p b n -> p (b n)"),
                                xT[:, HI, :, :].bitcast(F32).rearrange("p c q -> p (c q)"), ALU.subtract).then_inc(b_xL, 1)

            def low_a(n):
                dve.wait_ge(b_aH, n)
                V.tensor_tensor(aT[:, LO, :, :].rearrange("p c q -> p (c q)"), ps[:, 6:8, :].rearrange("p b n -> p (b n)"),
                                aT[:, HI, :, :].bitcast(F32).rearrange("p c q -> p (c q)"), ALU.subtract).then_inc(b_aL, 1)

            def clamp_glu(g):
                dve.wait_ge(q_w1, g * KC + KC)
                for j in range(2):
                    V.tensor_scalar(a_g[:, 512 * j:512 * j + 512], ps[:, j, :], LIM, None, ALU.min).then_inc(b_min, 1)

            def clamp_lin(g, first=False):
                if not first:
                    dve.wait_ge(b_aps, g)
                V.tensor_scalar(a_l.rearrange("p (b n) -> p b n", b=2), ps[:, 2:4, :], LIM, -LIM, ALU.min, ALU.max).then_inc(b_hread, 1)

            def swiglu(n):
                dve.wait_ge(b_hread, n)
                dve.wait_ge(b_min, n * 2)
                V.scalar_tensor_tensor(a_l, a_l, 1.0, a_g, ALU.add, ALU.mult).then_inc(b_lin, 1)
                dve.wait_ge(b_sig, n * 2)
                dve.wait_ge(b_lin, n)
                V.tensor_tensor(a_l, a_l, a_s, ALU.mult).then_inc(b_act, 1)

            def step(g, tail=True, off=0, begin=0):
                for k in range(KC):
                    if k >= begin:
                        low_w1(g, k, off)
                    if k == 0:
                        one_hot(g + 1)
                    if k == 2 and tail:
                        swiglu(g)
                        if not (isinstance(g, int) and g < 2):
                            dve.wait_ge(q_w2, g * 4 - 4)
                        select(selB, g - 1, b_selB)
                    if k == 4:
                        table(g + 1)
                    if k == 7 and tail:
                        low_a(g)
                if tail:
                    for c in range(3):
                        low_w2(g - 1, c)
                clamp_glu(g)
                if tail:
                    low_w2(g - 1, 3)
                clamp_lin(g, first=not tail)
                low_x(g + 1)
                select(selA, g + 1, b_selA)

            one_hot(0)
            table(0)
            select(selA, 0, b_selA)
            for k in range(NRING):
                low_w1(0, k, off=1)
            low_x(0)
            dve.wait_ge(st_x1, 16 * NT)
            step(0, tail=False, off=1, begin=NRING)
            step(1)
            with dve.Fori(2, last_b + 1) as g:
                step(g)
            swiglu(last_b + 1)
            dve.wait_ge(q_w2, last_b * 4)
            select(selB, last_b, b_selB)
            e_last = dve.value_load(egi[0:1, bass.ds(last_b, 1)], min_val=0, max_val=NE - 1)
            dve.wait_ge(b_tab, last_b + 2)
            V.tensor_scalar(slot_no, slot_no, float(2 * P), None, ALU.subtract).then_inc(b_chain, 1)
            dve.wait_ge(b_chain, last_b + 3)
            for t in range(NT):
                last = V.tensor_scalar(hot[:, t, :], slot_no, pos[:, t, bass.ds(e_last, 1)], None, ALU.is_equal)
            last.then_inc(f_hot, 1)
            low_a(last_b + 1)
            for c in range(4):
                low_w2(last_b, c)
            dve.wait_ge(f_ld, 48)
            dve.wait_ge(q_w2, last_b * 4 + 4)
            dve.wait_ge(b_sca, last_b * 16)
            V.scalar_tensor_tensor(y_sb, ps[:, 4:6, :].rearrange("p b n -> p (b n)"), gcol[:, bass.ds(last_b, 1)], fin_gate2,
                                   ALU.mult, ALU.mult).then_inc(f_y, 1)
            def finish(t):
                dve.wait_ge(f_sd, t + 1)
                link(V.reciprocal(st[:, 8 + t:9 + t], st[:, 4 + t:5 + t]))
                V.scalar_tensor_tensor(fin_x1[:, t, :], fin_x1[:, t, :], st[:, 8 + t:9 + t], fin_g, ALU.mult, ALU.mult).then_inc(f_o, 1)

            for t in range(NT):
                dve.wait_ge(f_last, t + 1)
                V.tensor_tensor(fin_x1[:, t, :], fin_x1[:, t, :], ps[:, 2 * t:2 * t + 2, :].rearrange("p b n -> p (b n)"),
                                ALU.add).then_inc(f_base, 1)
            for t in range(NT):
                if t < NT - 1:
                    dve.wait_ge(f_pair, t + 1)
                else:
                    dve.wait_ge(l_fin[t], 16)
                y4 = fin_y[t].rearrange("p a (b n) -> p (a b) n", b=2)
                link(V.tensor_tensor(y4[:, 0, :], y4[:, 0, :], y4[:, 1, :], ALU.add))
                if t == NT - 1:
                    dve.wait_ge(f_pair, t + 1)
                    link(V.tensor_tensor(y4[:, 0, :], y4[:, 0, :], y4[:, 2, :], ALU.add))
                link(V.tensor_tensor(y4[:, 0, :], y4[:, 0, :], fin_gate2, ALU.mult))
                if t == 0:
                    dve.wait_ge(f_base, NT)
                V.tensor_tensor(fin_x1[:, t, :], fin_x1[:, t, :], y4[:, 0, :], ALU.add).then_inc(f_sum, 1)
                if t >= 1:
                    finish(t - 1)
            finish(NT - 1)

        @block.tensor
        def _(pe):
            T = nc.tensor

            def turn(bank, k, src, ev, done):
                for t in range(NT):
                    last = T.transpose(ps[:, bank, part(t)], src[:, t, P * k:P * k + P], ident)
                last.then_inc(done, 1)

            pe.wait_ge(l_cst, 16)
            pe.wait_ge(l_par, 16 * N_PAR)
            T.transpose(ps[:, 0, 0:R_N], parms[0:R_N, :], ident[0:R_N, 0:R_N]).then_inc(s["t_par"], 1)
            T.transpose(ps[:, 0, R_N:R_N + 2 * TAPS], taps_r, ident[0:2 * TAPS, 0:2 * TAPS]).then_inc(s["t_par"], 1)
            T.transpose(ps[:, 0, 256:256 + NH], sgub_r, ident[0:NH, 0:NH]).then_inc(s["t_par"], 1)
            T.matmul(ps[0:NH, 6, :], relb[:], buckets[:, 0:512], start=True, stop=True)
            T.matmul(ps[0:NH, 7, 0:NDIST - 512], relb[:], buckets[:, 512:NDIST], start=True, stop=True).then_inc(s["t_bias"], 1)
            for h in range(NH):
                last = T.transpose(ps[:, 5, part(h)], sguw_r[:, h, :], ident)
            last.then_inc(s["t_wmix"], 1)

            def column_sums(bank, acc, done):
                for j in range(16):
                    last = T.matmul(ps[:, bank, j:j + 1], acc[:, P * j:P * j + P], ones[:, 0:1], start=True, stop=True)
                last.then_inc(done, 1)

            def turn_x(k):
                if k == 0:
                    pe.wait_ge(s["v_xn"], NT)
                    pe.wait_ge(s["c_par"], 1)
                    pe.wait_ge(s["c_bias"], 1)
                if k >= 4:
                    pe.wait_ge(s["a_hT"], k - 3)
                turn(TURN[k % 4], k, rows, None, s["t_hT"])

            for k in range(4):
                turn_x(k)
            pe.wait_ge(s["v_mod0"], KC)
            column_sums(2, acc0, s["m_mod0"])
            def product(i, k):
                kind, n, wc = PROJ[i]
                if k == 0:
                    j = i - 4 if i < BASE else i - 2
                    if i == 0:
                        pe.wait_ge(s["c_mod"], 1)
                    if i == 3:
                        pe.wait_ge(s["c_wmix"], 1)
                    if j in (1, 3):
                        pe.wait_ge(s["e_glu"], j // 2 + 1)
                    elif j in (0, 2):
                        pe.wait_ge(s["e_act"], j // 2 + 1)
                    elif j >= 4:
                        pe.wait_ge(s["e_act"], j - 1)
                if i == 0:
                    pe.wait_ge(s["a_hT"], k + 1)
                    pe.wait_ge(l_w1[k], 32)
                bank = proj_bank(i)
                if kind == "v":
                    last = T.matmul(bank[:, 0:GW], colsT[:, k, part(n)], w1_slots[:, k, 1024:1280],
                                    start=(k == 0), stop=(k == KC - 1))
                elif kind == "s":
                    last = T.matmul(bank, colsT[:, k, part(n)], w1_slots[:, k, 1536:2048],
                                    start=(k == 0), stop=(k == KC - 1))
                else:
                    last = T.matmul(bank, w1_slots[:, k, P * wc:P * wc + P], colsT[:, k, :],
                                    start=(k == 0), stop=(k == KC - 1))
                if k == KC - 1:
                    last.then_inc(s["p_proj"], 1)

            for k in range(KC):
                for i in range(4):
                    product(i, k)
                if k < 4:
                    turn_x(k + 4)
            for i in range(4, BASE):
                for k in range(KC):
                    product(i, k)
            pe.wait_ge(s["g_added"], KC)
            column_sums(0, acc1, s["m_modA"])
            pe.wait_ge(s["v_conv"], 2 * TAPS)
            pe.wait_ge(s["c_bias"], 1)
            for t in range(NT):
                for c in range(2):
                    last = T.transpose(ps[:, 6 + t // 2, GW * (t % 2) + P * c:GW * (t % 2) + P * c + P],
                                       pT[:, c, part(t)], ident)
            last.then_inc(s["t_conv"], 1)

            def att_scores(i):
                h, q = ATT[i]
                hp = slice(HD * (h % 2), HD * (h % 2) + HD)
                if i == 0:
                    pe.wait_ge(s["e_act"], BASE - 2)
                    pe.wait_ge(s["v_cen"], 1)
                if i >= 2:
                    pe.wait_ge(s["v_att"], i - 1)
                T.matmul(ps[:, 6 + h % 2, 0:P * (q + 1)], pT[hp, 4 + h // 2, part(q)], pT[hp, 6 + h // 2, 0:P * (q + 1)],
                         start=True, stop=True).then_inc(s["s_att"], 1)

            def att_turn(i):
                h, q = ATT[i]
                pe.wait_ge(s["a_att"], i + 1)
                if i == 0:
                    pe.wait_ge(s["c_mod12"], 1)
                if i >= 2:
                    pe.wait_ge(s["a_attT"], i - 1)
                for j in range(q + 1):
                    last = T.transpose(ps[:, i % 2, part(j)], prob[:, i % 2, part(j)], ident)
                last.then_inc(s["t_att"], 1)

            def att_out(i):
                h, q = ATT[i]
                pe.wait_ge(s["a_attT"], i + 1)
                if i >= 2:
                    pe.wait_ge(s["v_attO"], i - 1)
                for j in range(q + 1):
                    last = T.matmul(ps[:, 2 + i % 2, 0:HD], probT[:, i % 2, part(j)], pR[:, j, HD * h:HD * h + HD],
                                    start=(j == 0), stop=(j == q))
                last.then_inc(s["o_att"], 1)

            for i in range(NA + 2):
                if i < NA:
                    att_scores(i)
                for m in range(4 * i, min(4 * i + 4, KC * (NPROJ - BASE))):
                    product(BASE + m // KC, m % KC)
                if 1 <= i <= NA:
                    att_turn(i - 1)
                if i >= 2:
                    att_out(i - 2)
                if i == 12:
                    pe.wait_ge(s["g_poolT"], 1)
                    pe.wait_ge(l_pw, 64)
                    pe.wait_ge(s["e_act"], NPROJ - 2)
                    for t in range(NT):
                        for c in range(2):
                            last = T.matmul(ps[:, 4 + t // 2, GW * (t % 2) + P * c:GW * (t % 2) + P * c + P],
                                            pT[:, 8 + c, part(t)], poolw[:, c, :], start=True, stop=True)
                    last.then_inc(s["m_pool"], 1)
                if i in (14, NA):
                    b = 0 if i == 14 else 1
                    pe.wait_ge(s["v_convE"], 1)
                    pe.wait_ge(s["v_sgu"], b + 1)
                    for t in (2 * b, 2 * b + 1):
                        for h in range(NH):
                            last = T.matmul(ps[:, 4 + b, GW * (t % 2) + HD * h:GW * (t % 2) + HD * h + HD], wmixT[:, h, :],
                                            pR[:, t, 2 * GW + HD * h:2 * GW + HD * h + HD], start=True, stop=True)
                    last.then_inc(s["m_sgu"], 1)

            def mixed_turn(t):
                pe.wait_ge(s["v_mixed"], t + 1)
                if t:
                    pe.wait_ge(s["v_mixT"], t)
                for k in range(KC):
                    last = T.transpose(ps[:, k // 4, part(k % 4)], rows[:, t, P * k:P * k + P], ident)
                last.then_inc(s["t_mixT"], 1)

            def row_of(bank, first):
                for k in range(KC):
                    last = T.matmul(ps[:, bank + k // 4, part(k % 4)], first[:, k:k + 1].to_broadcast([P, P]), ident,
                                    start=True, stop=True)
                last.then_inc(s["t_rows2"], 1)

            def project_out(t, n):
                if n == 0:
                    pe.wait_ge(s["v_mixT"], t + 1)
                if t == 0 and n == 0:
                    pe.wait_ge(s["v_sguE"], 8)
                    pe.wait_ge(s["g_woL"], 4)
                if t == 1:
                    pe.wait_ge(s["c_mod12"], 3)
                if t >= 2:
                    pe.wait_ge(s["v_x1"], t - 1)
                hi, lo = mixT_hi[:, :, part(t)], mixT_lo[:, t % 2, :, :]
                for x, w in ((hi, wo_hi), (lo, wo_hi), (hi, wo_lo)):
                    for k in range(KC):
                        at = 1024 * (k % 2) + 512 * n
                        last = T.matmul(ps[:, 4 - 2 * (t % 2) + n, :], x[:, k, :], w[:, k // 2, at:at + 512],
                                        start=(w is wo_hi and x is hi and k == 0), stop=(w is wo_lo and k == KC - 1))
                last.then_inc(s["m_out"], 1)

            def h2_turn(t):
                pe.wait_ge(s["v_h2"], t + 1)
                if t == 0:
                    pe.wait_ge(s["a_rows2"], 2)
                else:
                    pe.wait_ge(s["a_h2T"], t)
                for k in range(KC):
                    last = T.transpose(ps[:, 6 + k // 4, part(k % 4)], rows[:, t, P * k:P * k + P], ident)
                last.then_inc(s["t_h2T"], 1)

            def router(t):
                pe.wait_ge(s["a_h2T"], t + 1)
                for k in range(KC):
                    last = T.matmul(ps[:, 0, NE * t:NE * t + NE], colsT[:, k, part(t)], rw_sb[:, k, :],
                                    start=(k == 0), stop=(k == KC - 1))
                if t == NT - 1:
                    last.then_inc(s["m_lg"], 1)

            pe.wait_ge(l_row, 16 * 7)
            pe.wait_ge(s["a_attT"], NA)
            mixed_turn(0)
            pe.wait_ge(s["g_added"], 2 * KC)
            pe.wait_ge(s["v_att"], NA)
            pe.wait_ge(s["v_attO"], NA)
            for g in range(2):
                for j in range(2):
                    last = T.matmul(ps[:, (6, 2)[g] + j, :], ones, acc2[:, D * g + 512 * j:D * g + 512 * j + 512],
                                    start=True, stop=True)
                last.then_inc(s["m_mod"], 1)
            project_out(0, 0)
            mixed_turn(1)
            project_out(0, 1)
            pe.wait_ge(s["c_mod12"], 2)
            row_of(6, gs2)
            project_out(1, 0)
            mixed_turn(2)
            pe.wait_ge(s["a_rows2"], 1)
            row_of(6, mod[:, 24:32])
            project_out(1, 1)
            project_out(2, 0)
            mixed_turn(3)
            h2_turn(0)
            project_out(2, 1)
            project_out(3, 0)
            pe.wait_ge(s["v_mixT"], NT)
            h2_turn(1)
            router(0)
            project_out(3, 1)
            h2_turn(2)
            router(1)
            router(2)
            h2_turn(3)
            router(3)
            pe.wait_ge(s["v_memb"], 1)
            for t in range(NT):
                last = T.matmul(ps[:, 2, 0:NE], ones, memb[:, t, :], start=(t == 0), stop=(t == NT - 1))
            last.then_inc(s["m_cnt"], 1)
            strict = cst[:, C_STRICT:C_STRICT + P]
            for t in range(NT):
                for j in range(t + 1):
                    last = T.matmul(ps[:, 3, NE * t:NE * t + NE], strict if j == t else ones, memb[:, j, :],
                                    start=(j == 0), stop=(j == t))
            last.then_inc(s["m_rank"], 1)

            for used in (d_w1, p_w1):
                pe.nop().then_inc(used, KC)
            for used in (d_w2, p_w2):
                pe.nop().then_inc(used, 4)
            pe.nop().then_inc(b_yev, 1)
            pe.nop().then_inc(b_yfree, 1)
            pe.wait_ge(s["v_tables"], 1)
            last_b = pe.value_load(bendi[0:1, NE:NE + 1], min_val=0, max_val=MAXBLK - 2)

            def expert(g):
                return pe.value_load(egi[0:1, bass.ds(g, 1)], min_val=0, max_val=NE - 1)

            def table(g, first=False):
                e = expert(g)
                pe.wait_ge(b_hot, g + 1)
                if not first:
                    pe.wait_ge(b_xL, g)
                for t in range(NT):
                    last = T.matmul(ps[:, 6, 0:4], hot[:, t, :], vtab[:, t, bass.ds(e, 1), :].rearrange("p e c -> p (e c)"),
                                    start=(t == 0), stop=(t == NT - 1))
                last.then_inc(b_tab, 1)

            def turn_rows(g, turned=True):
                pe.wait_ge(b_gat, g * 16 + 16)
                pe.wait_ge(b_idx, g + 1)
                if turned:
                    pe.wait_ge(b_aL, g - 1)
                for k in range(KC):
                    last = T.transpose(ps[:, 6 + k // 4, part(k % 4)], xg[:, P * k:P * k + P], ident)
                last.then_inc(b_xps, 1)

            def turn_act(n):
                pe.wait_ge(b_act, n)
                for i in range(KC):
                    last = T.transpose(ps[:, 6 + i // 4, part(i % 4)],
                                       a_l.rearrange("p (c q j) -> p c j q", c=4, j=2)[:, i // 2, i % 2, :], ident)
                last.then_inc(b_aps, 1)

            def up(g, tail=True, off=0):
                pe.wait_ge(b_selA, g + 1)
                pe.wait_ge(b_xL, g + 1)
                if tail:
                    pe.wait_ge(b_hread, g)
                for n in range(4):
                    T.matmul(ps[:, n, :], selA[0:96, :], b_bf[:, 512 * n:512 * n + 512], start=True, stop=False)
                for k in range(KC):
                    r = (k + off) % NRING
                    pe.wait_ge(h_w1, g * KC + (k + 1))
                    for x in (HI, LO):
                        for n in range(4):
                            T.matmul(ps[:, n, :], xT[:, x, k, :], w_ring[:, r, HI, 512 * n:512 * n + 512], start=False, stop=False)
                    pe.wait_ge(d_w1, g * KC + (KC + k + 1))
                    for n in range(4):
                        if n == 3:
                            pe.wait_ge(p_w1, g * KC + (KC + k + 1))
                        last = T.matmul(ps[:, n, :], xT[:, HI, k, :], w_ring[:, r, LO, 512 * n:512 * n + 512],
                                        start=False, stop=(k == KC - 1))
                    last.then_inc(q_w1, 1)
                    if k == 0:
                        table(g + 1)
                    if k == 4 and tail:
                        pe.wait_ge(b_idx, g + 2)
                        turn_act(g)

            def down(n, first=False):
                pe.wait_ge(b_selB, n)
                pe.wait_ge(b_aL, n)
                if not first:
                    pe.wait_ge(b_yev, n)
                for j in range(2):
                    T.matmul(ps[:, 4 + j, :], selB[0:96, :], b_bf[:, 2048 + 512 * j:2560 + 512 * j], start=True, stop=False)
                for c in range(4):
                    r = (KC + c) % NRING
                    pe.wait_ge(h_w2, n * 4 + (c - 3))
                    for x, w in ((HI, HI), (LO, HI), (HI, LO)):
                        if w == LO:
                            pe.wait_ge(d_w2, n * 4 + (c + 1))
                        for j in range(2):
                            for h in range(2):
                                if w == LO and j == 1 and h == 1:
                                    pe.wait_ge(p_w2, n * 4 + (c + 1))
                                at = 1024 * j + 512 * h
                                last = T.matmul(ps[:, 4 + h, :], aT[:, x, 2 * c + j, :], w_ring[:, r, w, at:at + 512],
                                                start=False, stop=(c == 3 and w == LO and j == 1))
                    last.then_inc(q_w2, 1)

            pe.wait_ge(s["g_bf"], 6)
            table(0, first=True)
            turn_rows(0, turned=False)
            up(0, tail=False, off=1)
            turn_rows(1, turned=False)
            up(1)
            turn_rows(2)
            down(1, first=True)
            with pe.Fori(2, last_b + 1) as g:
                up(g)
                turn_rows(g + 1)
                down(g)
            pe.wait_ge(b_xL, last_b + 2)
            turn_act(last_b + 1)
            pe.wait_ge(b_aL, last_b + 1)
            pe.wait_ge(f_hot, 1)
            for t in range(NT):
                last = T.transpose(ps[:, 6, part(t)], hot[:, t, :], ident)
            last.then_inc(f_turn, 1)
            down(last_b + 1)
            pe.wait_ge(b_hread, last_b + 1)
            pe.wait_ge(f_hotT, 1)
            pe.wait_ge(f_y, 1)
            for t in range(NT):
                for h in range(2):
                    last = T.matmul(ps[:, 2 * t + h, :], hotT[:, t, :], y_sb[:, 512 * h:512 * h + 512], start=True, stop=True)
                last.then_inc(f_last, 1)


_OUTS = [((1, S, D), "float32")]
_INS = ["x", "c", "w_mod", "b_mod", "norm1_g", "w_in", "conv_w", "conv_b", "conv_norm_g", "conv_norm_b", "rel_bias", "pool_w",
        "pool_scale", "sgu_norm_g", "sgu_norm_b", "sgu_w", "sgu_b", "mix_out_g", "w_out", "norm2_g", "router_w", "router_b",
        "exp_w1", "exp_b1", "exp_w2", "exp_b2", "final_norm_g"]


def kernel(**inputs):
    import concourse.bacc as bacc
    from concourse.bass_utils import run_bass_kernel_spmd

    nc = bacc.Bacc("TRN2", target_bir_lowering=False, num_devices=1)
    arrays, args = {}, {}
    for name in _INS:
        v = np.ascontiguousarray(inputs[name])
        arrays[f"in_{name}"] = v
        args[name] = nc.dram_tensor(f"in_{name}", v.shape, mybir.dt.from_np(v.dtype), kind="ExternalInput").ap()
    extra = []
    for name, v in (("consts", constants()), ("buckets", distance_buckets())):
        arrays[f"in_{name}"] = v
        extra.append(nc.dram_tensor(f"in_{name}", v.shape, F32, kind="ExternalInput").ap())
    out = nc.dram_tensor("out_0", _OUTS[0][0], F32, kind="ExternalOutput").ap()
    build(nc, args, extra[0], extra[1], out)
    r = run_bass_kernel_spmd(nc, [arrays], core_ids=[0])
    return r.results[0]["out_0"]
```
